# Optimizing a Trainium2 kernel written in Bass

```python
import math
import jax
import jax.numpy as jnp
from jax import lax
import numpy as np

'''One inference step (2 layers) of a hybrid decoder trunk, run for a prompt group and a sample group
with the same weights. Layer i uses token mixer (i mod 2): even layers a Griffin RG-LRU recurrent block,
odd layers FoX forgetting attention. Every layer is followed by a PEER product-key expert channel mixer.
Normalisation is DeepNorm post-LayerNorm: x <- LN(ALPHA*x + f(x)). 16 learned meta tokens are prepended to
every prompt sequence and dropped from y_prompt.

Inputs:
  x_prompt   (BATCH, SEQ, D_MODEL)
  x_sample   (DEC_BATCH, DEC_SEQ, D_MODEL)
  cache_k, cache_v (N_ATTN_LAYERS, N_POOL, PAGE_SIZE, N_HEADS, HEAD_DIM)  paged K/V pool
  cache_logf (N_ATTN_LAYERS, N_POOL, PAGE_SIZE, N_HEADS)                 paged per-row log forget values
  state_h    (N_RG_LAYERS, DEC_BATCH, D_RNN)                             RG-LRU hidden state
  state_conv (N_RG_LAYERS, DEC_BATCH, CONV_W-1, D_RNN)                   last conv input rows
  page_table (DEC_BATCH, N_PAGES) int32, N_PAGES = PAST_LEN // PAGE_SIZE
  followed by the weights.
Returns the tuple:
  y_prompt (BATCH, SEQ, D_MODEL), y_sample (DEC_BATCH, DEC_SEQ, D_MODEL),
  state_h_prompt (N_RG_LAYERS, BATCH, D_RNN), state_conv_prompt (N_RG_LAYERS, BATCH, CONV_W-1, D_RNN),
  k_prompt, v_prompt (N_ATTN_LAYERS, BATCH, N_META+SEQ, N_HEADS, HEAD_DIM),
  logf_prompt (N_ATTN_LAYERS, BATCH, N_META+SEQ, N_HEADS),
  state_h_sample (N_RG_LAYERS, DEC_BATCH, D_RNN), state_conv_sample (N_RG_LAYERS, DEC_BATCH, CONV_W-1, D_RNN),
  k_sample, v_sample (N_ATTN_LAYERS, DEC_BATCH, DEC_SEQ, N_HEADS, HEAD_DIM),
  logf_sample (N_ATTN_LAYERS, DEC_BATCH, DEC_SEQ, N_HEADS)
'''

D_MODEL = 1024
BATCH = 1
SEQ = 256
DEPTH = 2
DEC_BATCH = 8
DEC_SEQ = 8
PAST_LEN = 256
PAGE_SIZE = 128

N_MIXERS = 2
N_RG_LAYERS = (DEPTH + 1) // 2
N_ATTN_LAYERS = DEPTH // 2
N_META = 16
D_RNN = D_MODEL
RG_BLOCKS = 8
RG_BLOCK = D_RNN // RG_BLOCKS
CONV_W = 4
RG_C = 8.0
N_HEADS = 8
HEAD_DIM = D_MODEL // N_HEADS
Q_BLOCK = 128
ATTN_SCALE = HEAD_DIM ** -0.5
PEER_HEADS = 8
PEER_TOPK = 16
N_KEYS = 128
N_EXPERTS = N_KEYS * N_KEYS
D_KEY = 256
D_HALF = D_KEY // 2
PEER_CHUNK = 128
ALPHA = (2.0 * DEPTH) ** 0.25
BETA = (8.0 * DEPTH) ** -0.25
LN_EPS = 1e-5

kernel_name = 'hybrid_rglru_fox_peer_step'

def layer_norm(x, g, b):
    xf = x.astype(jnp.float32)
    mu = jnp.mean(xf, axis=-1, keepdims=True)
    var = jnp.mean(jnp.square(xf - mu), axis=-1, keepdims=True)
    return ((xf - mu) * lax.rsqrt(var + LN_EPS) * g + b).astype(x.dtype)

def rglru_mixer(x, conv_buf, h0, w_in, conv_w, conv_b, w_a, b_a, w_x, b_x, lam, w_out):
    B, T, _ = x.shape
    xin = x @ w_in
    gate = jax.nn.gelu(xin[..., :D_RNN])
    rec = xin[..., D_RNN:]
    xp = jnp.concatenate([conv_buf.astype(rec.dtype), rec], axis=1)
    rec = conv_b + sum(xp[:, k:k + T] * conv_w[k] for k in range(CONV_W))
    new_buf = xp[:, T:]
    rb = rec.reshape(B, T, RG_BLOCKS, RG_BLOCK)
    r = jax.nn.sigmoid((jnp.einsum('btnc,ncd->btnd', rb, w_a).reshape(B, T, D_RNN) + b_a).astype(jnp.float32))
    i = jax.nn.sigmoid((jnp.einsum('btnc,ncd->btnd', rb, w_x).reshape(B, T, D_RNN) + b_x).astype(jnp.float32))
    log_a = -RG_C * r * jax.nn.softplus(-lam.astype(jnp.float32))
    a = jnp.exp(log_a)
    bx = jnp.sqrt(-jnp.expm1(2.0 * log_a)) * (i * rec.astype(jnp.float32))

    def step(h, ab):
        at, bt = ab
        h = at * h + bt
        return h, h

    hT, hs = lax.scan(step, h0.astype(jnp.float32), (a.swapaxes(0, 1), bx.swapaxes(0, 1)))
    y = hs.swapaxes(0, 1).astype(x.dtype) * gate
    return y @ w_out, new_buf, hT.astype(x.dtype)

def fox_project(x, w_in, b_f):
    B, T, _ = x.shape
    z = x @ w_in
    q = z[..., :D_MODEL].reshape(B, T, N_HEADS, HEAD_DIM)
    k = z[..., D_MODEL:2 * D_MODEL].reshape(B, T, N_HEADS, HEAD_DIM)
    v = z[..., 2 * D_MODEL:3 * D_MODEL].reshape(B, T, N_HEADS, HEAD_DIM)
    logf = jax.nn.log_sigmoid((z[..., 3 * D_MODEL:] + b_f).astype(jnp.float32))
    return q, k, v, logf

def fox_attend(qb, cq, qpos, kk, vv, ck, kpos):
    s = jnp.einsum('bqhd,bkhd->bhqk', qb, kk).astype(jnp.float32) * ATTN_SCALE
    s = s + jnp.transpose(cq, (0, 2, 1))[..., :, None] - jnp.transpose(ck, (0, 2, 1))[..., None, :]
    s = jnp.where(kpos[None, :] <= qpos[:, None], s, -jnp.inf)
    p = jax.nn.softmax(s, axis=-1).astype(vv.dtype)
    return jnp.einsum('bhqk,bkhd->bqhd', p, vv)

def fox_prompt_attn(q, k, v, logf):
    B, T = q.shape[:2]
    n_real = T - N_META
    nb = n_real // Q_BLOCK
    c = jnp.cumsum(logf, axis=1)
    kpos = jnp.arange(T)
    meta_pos = jnp.arange(N_META)
    out_m = fox_attend(q[:, :N_META], c[:, :N_META], meta_pos, k[:, :N_META], v[:, :N_META], c[:, :N_META], meta_pos)
    qr = q[:, N_META:].reshape(B, nb, Q_BLOCK, N_HEADS, HEAD_DIM).swapaxes(0, 1)
    cr = c[:, N_META:].reshape(B, nb, Q_BLOCK, N_HEADS).swapaxes(0, 1)
    qpos = (N_META + jnp.arange(n_real)).reshape(nb, Q_BLOCK)
    outs = lax.map(lambda a: fox_attend(a[0], a[1], a[2], k, v, c, kpos), (qr, cr, qpos))
    out_r = outs.swapaxes(0, 1).reshape(B, n_real, N_HEADS, HEAD_DIM)
    return jnp.concatenate([out_m, out_r], axis=1)

def fox_sample_attn(q, k, v, logf, ck_pool, cv_pool, cl_pool, page_table):
    DB, S = q.shape[:2]
    kp = ck_pool[page_table].reshape(DB, -1, N_HEADS, HEAD_DIM)
    vp = cv_pool[page_table].reshape(DB, -1, N_HEADS, HEAD_DIM)
    lp = cl_pool[page_table].reshape(DB, -1, N_HEADS)
    P = kp.shape[1]
    c = jnp.cumsum(jnp.concatenate([lp.astype(jnp.float32), logf], axis=1), axis=1)
    c_past = jnp.transpose(c[:, :P], (0, 2, 1))
    c_new = jnp.transpose(c[:, P:], (0, 2, 1))
    s_past = jnp.einsum('bqhd,bkhd->bhqk', q, kp).astype(jnp.float32) * ATTN_SCALE
    s_past = s_past + c_new[..., :, None] - c_past[..., None, :]
    s_new = jnp.einsum('bqhd,bkhd->bhqk', q, k).astype(jnp.float32) * ATTN_SCALE
    s_new = s_new + c_new[..., :, None] - c_new[..., None, :]
    causal = jnp.arange(S)[None, :] <= jnp.arange(S)[:, None]
    s_new = jnp.where(causal, s_new, -jnp.inf)
    p = jax.nn.softmax(jnp.concatenate([s_past, s_new], axis=-1), axis=-1).astype(v.dtype)
    return jnp.einsum('bhqk,bkhd->bqhd', p[..., :P], vp) + jnp.einsum('bhqk,bkhd->bqhd', p[..., P:], v)

def peer_ffn(x, w_q, keys1, keys2, u, v):
    shape = x.shape
    xf = x.reshape(-1, D_MODEL)
    n = xf.shape[0]
    pad = (-n) % PEER_CHUNK
    xc = jnp.pad(xf, ((0, pad), (0, 0))).reshape(-1, PEER_CHUNK, D_MODEL)

    def chunk(xb):
        q = (xb @ w_q).reshape(PEER_CHUNK, PEER_HEADS, D_KEY)
        s1 = jnp.einsum('thc,hkc->thk', q[..., :D_HALF], keys1).astype(jnp.float32)
        s2 = jnp.einsum('thc,hkc->thk', q[..., D_HALF:], keys2).astype(jnp.float32)
        v1, i1 = lax.top_k(s1, PEER_TOPK)
        v2, i2 = lax.top_k(s2, PEER_TOPK)
        cand = (v1[..., :, None] + v2[..., None, :]).reshape(PEER_CHUNK, PEER_HEADS, PEER_TOPK * PEER_TOPK)
        cand_idx = (i1[..., :, None] * N_KEYS + i2[..., None, :]).reshape(PEER_CHUNK, PEER_HEADS, PEER_TOPK * PEER_TOPK)
        sc, j = lax.top_k(cand, PEER_TOPK)
        idx = jnp.take_along_axis(cand_idx, j, axis=-1)
        g = jax.nn.softmax(sc, axis=-1)
        act = jax.nn.gelu(jnp.einsum('thkd,td->thk', u[idx], xb).astype(jnp.float32))
        w = (g * act).astype(xb.dtype)
        return jnp.einsum('thk,thkd->td', w, v[idx])

    out = lax.map(chunk, xc).reshape(-1, D_MODEL)[:n]
    return out.reshape(shape)

def setup_inputs(seed: int = 0) -> dict:
    key = jax.random.key(seed)
    ks = jax.random.split(key, 32)
    f32 = jnp.float32

    def nrm(k, shape, s):
        return jax.random.normal(k, shape, f32) * s

    n_pages = PAST_LEN // PAGE_SIZE
    n_used = DEC_BATCH * n_pages
    n_pool = n_used + n_used // 4
    x_prompt = nrm(ks[0], (BATCH, SEQ, D_MODEL), 1.0)
    x_sample = nrm(ks[1], (DEC_BATCH, DEC_SEQ, D_MODEL), 1.0)
    cache_k = nrm(ks[2], (N_ATTN_LAYERS, n_pool, PAGE_SIZE, N_HEADS, HEAD_DIM), 1.0)
    cache_v = nrm(ks[3], (N_ATTN_LAYERS, n_pool, PAGE_SIZE, N_HEADS, HEAD_DIM), 1.0)
    cache_logf = jax.nn.log_sigmoid(4.0 + jax.random.normal(ks[4], (N_ATTN_LAYERS, n_pool, PAGE_SIZE, N_HEADS), f32))
    state_h = nrm(ks[5], (N_RG_LAYERS, DEC_BATCH, D_RNN), 0.5)
    state_conv = nrm(ks[6], (N_RG_LAYERS, DEC_BATCH, CONV_W - 1, D_RNN), 1.0)
    page_table = jax.random.permutation(ks[7], n_pool)[:n_used].reshape(DEC_BATCH, n_pages).astype(jnp.int32)
    meta_tokens = nrm(ks[8], (N_META, D_MODEL), 1.0)
    rg_w_in = nrm(ks[9], (N_RG_LAYERS, D_MODEL, 2 * D_RNN), D_MODEL ** -0.5)
    rg_conv_w = nrm(ks[10], (N_RG_LAYERS, CONV_W, D_RNN), CONV_W ** -0.5)
    rg_conv_b = nrm(ks[11], (N_RG_LAYERS, D_RNN), 0.01)
    rg_w_a = nrm(ks[12], (N_RG_LAYERS, RG_BLOCKS, RG_BLOCK, RG_BLOCK), RG_BLOCK ** -0.5)
    rg_b_a = nrm(ks[13], (N_RG_LAYERS, D_RNN), 0.01)
    rg_w_x = nrm(ks[14], (N_RG_LAYERS, RG_BLOCKS, RG_BLOCK, RG_BLOCK), RG_BLOCK ** -0.5)
    rg_b_x = nrm(ks[15], (N_RG_LAYERS, D_RNN), 0.01)
    a_c = jax.random.uniform(ks[16], (N_RG_LAYERS, D_RNN), f32, 0.9, 0.999)
    a0 = a_c ** (1.0 / RG_C)
    rg_lambda = jnp.log(a0) - jnp.log1p(-a0)
    rg_w_out = nrm(ks[17], (N_RG_LAYERS, D_RNN, D_MODEL), D_RNN ** -0.5 * BETA)
    col_scale = jnp.concatenate([jnp.ones((2 * D_MODEL,), f32), jnp.full((D_MODEL,), BETA, f32), jnp.ones((N_HEADS,), f32)])
    fox_w_in = nrm(ks[18], (N_ATTN_LAYERS, D_MODEL, 3 * D_MODEL + N_HEADS), D_MODEL ** -0.5) * col_scale
    fox_b_f = 2.0 + 4.0 * jax.random.uniform(ks[19], (N_ATTN_LAYERS, N_HEADS), f32)
    fox_w_o = nrm(ks[20], (N_ATTN_LAYERS, D_MODEL, D_MODEL), D_MODEL ** -0.5 * BETA)
    peer_w_q = nrm(ks[21], (DEPTH, D_MODEL, PEER_HEADS * D_KEY), D_MODEL ** -0.5)
    peer_keys1 = nrm(ks[22], (DEPTH, PEER_HEADS, N_KEYS, D_HALF), D_HALF ** -0.5)
    peer_keys2 = nrm(ks[23], (DEPTH, PEER_HEADS, N_KEYS, D_HALF), D_HALF ** -0.5)
    peer_u = nrm(ks[24], (DEPTH, N_EXPERTS, D_MODEL), D_MODEL ** -0.5)
    peer_v = nrm(ks[25], (DEPTH, N_EXPERTS, D_MODEL), BETA)
    ln_mix_g = 1.0 + nrm(ks[26], (DEPTH, D_MODEL), 0.05)
    ln_mix_b = nrm(ks[27], (DEPTH, D_MODEL), 0.02)
    ln_ffn_g = 1.0 + nrm(ks[28], (DEPTH, D_MODEL), 0.05)
    ln_ffn_b = nrm(ks[29], (DEPTH, D_MODEL), 0.02)
    return {'x_prompt': x_prompt, 'x_sample': x_sample, 'cache_k': cache_k, 'cache_v': cache_v,
            'cache_logf': cache_logf, 'state_h': state_h, 'state_conv': state_conv, 'page_table': page_table,
            'meta_tokens': meta_tokens, 'rg_w_in': rg_w_in, 'rg_conv_w': rg_conv_w, 'rg_conv_b': rg_conv_b,
            'rg_w_a': rg_w_a, 'rg_b_a': rg_b_a, 'rg_w_x': rg_w_x, 'rg_b_x': rg_b_x, 'rg_lambda': rg_lambda,
            'rg_w_out': rg_w_out, 'fox_w_in': fox_w_in, 'fox_b_f': fox_b_f, 'fox_w_o': fox_w_o,
            'peer_w_q': peer_w_q, 'peer_keys1': peer_keys1, 'peer_keys2': peer_keys2, 'peer_u': peer_u,
            'peer_v': peer_v, 'ln_mix_g': ln_mix_g, 'ln_mix_b': ln_mix_b, 'ln_ffn_g': ln_ffn_g, 'ln_ffn_b': ln_ffn_b}

def reference(x_prompt, x_sample, cache_k, cache_v, cache_logf, state_h, state_conv, page_table,
              meta_tokens, rg_w_in, rg_conv_w, rg_conv_b, rg_w_a, rg_b_a, rg_w_x, rg_b_x, rg_lambda,
              rg_w_out, fox_w_in, fox_b_f, fox_w_o, peer_w_q, peer_keys1, peer_keys2, peer_u, peer_v,
              ln_mix_g, ln_mix_b, ln_ffn_g, ln_ffn_b):
    B = x_prompt.shape[0]
    DB, S = x_sample.shape[:2]
    meta = jnp.broadcast_to(meta_tokens.astype(x_prompt.dtype), (B, N_META, D_MODEL))
    hp = jnp.concatenate([meta, x_prompt], axis=1)
    T = hp.shape[1]
    hs = x_sample
    sh_p, sc_p, k_p, v_p, lf_p = [], [], [], [], []
    sh_s, sc_s, k_s, v_s, lf_s = [], [], [], [], []
    for i in range(DEPTH):
        l = i // N_MIXERS
        if i % N_MIXERS == 0:
            rg = (rg_w_in[l], rg_conv_w[l], rg_conv_b[l], rg_w_a[l], rg_b_a[l], rg_w_x[l], rg_b_x[l], rg_lambda[l], rg_w_out[l])
            zero_buf = jnp.zeros((B, CONV_W - 1, D_RNN), hp.dtype)
            zero_h = jnp.zeros((B, D_RNN), hp.dtype)
            mp, buf_p, h_p = rglru_mixer(hp, zero_buf, zero_h, *rg)
            ms, buf_s, h_s = rglru_mixer(hs, state_conv[l], state_h[l], *rg)
            sh_p.append(h_p)
            sc_p.append(buf_p)
            sh_s.append(h_s)
            sc_s.append(buf_s)
        else:
            qp, kp, vp, lp = fox_project(hp, fox_w_in[l], fox_b_f[l])
            mp = fox_prompt_attn(qp, kp, vp, lp).reshape(B, T, D_MODEL) @ fox_w_o[l]
            qs, ks_, vs, ls = fox_project(hs, fox_w_in[l], fox_b_f[l])
            ms = fox_sample_attn(qs, ks_, vs, ls, cache_k[l], cache_v[l], cache_logf[l], page_table).reshape(DB, S, D_MODEL) @ fox_w_o[l]
            k_p.append(kp)
            v_p.append(vp)
            lf_p.append(lp.astype(hp.dtype))
            k_s.append(ks_)
            v_s.append(vs)
            lf_s.append(ls.astype(hs.dtype))
        hp = layer_norm(ALPHA * hp + mp, ln_mix_g[i], ln_mix_b[i])
        hs = layer_norm(ALPHA * hs + ms, ln_mix_g[i], ln_mix_b[i])
        hp = layer_norm(ALPHA * hp + peer_ffn(hp, peer_w_q[i], peer_keys1[i], peer_keys2[i], peer_u[i], peer_v[i]), ln_ffn_g[i], ln_ffn_b[i])
        hs = layer_norm(ALPHA * hs + peer_ffn(hs, peer_w_q[i], peer_keys1[i], peer_keys2[i], peer_u[i], peer_v[i]), ln_ffn_g[i], ln_ffn_b[i])
    y_prompt = hp[:, N_META:]
    y_sample = hs
    return (y_prompt, y_sample,
            jnp.stack(sh_p), jnp.stack(sc_p), jnp.stack(k_p), jnp.stack(v_p), jnp.stack(lf_p),
            jnp.stack(sh_s), jnp.stack(sc_s), jnp.stack(k_s), jnp.stack(v_s), jnp.stack(lf_s))


_drawn_inputs = setup_inputs


def setup_inputs(seed=0):
    import zlib

    import numpy as np

    out = dict(_drawn_inputs(seed))
    spreads = {}
    factors = {'cache_logf': 3.602, 'rg_b_a': 25.081, 'rg_b_x': 6.022}
    for name, (base, spread) in spreads.items():
        noise = np.random.default_rng([zlib.crc32(name.encode()), seed]).standard_normal(out[name].shape)
        drawn = base * np.exp(spread * noise) if base else spread * noise
        out[name] = jnp.asarray(drawn.astype(out[name].dtype))
    for name, factor in factors.items():
        out[name] = (out[name] * factor).astype(out[name].dtype)
    return out
```

```python
from contextlib import ExitStack

import numpy as np

import concourse.bass as bass
from concourse import mybir
from concourse.alu_op_type import AluOpType as ALU

F32, I32, U32 = mybir.dt.float32, mybir.dt.int32, mybir.dt.uint32
ACT = mybir.ActivationFunctionType
AXX = mybir.AxisListType.X

D = 1024
C = D // 128
DB, DS = 8, 8
NS = DB * DS
META, SEQ = 16, 256
TP = META + SEQ
T = NS + TP
TT, NT = 112, 3
P0 = TT - NS
CW = 4
RG_C = 8.0
H, HD = 8, 128
PAGE, PAGES = 128, 2
PAST = PAGE * PAGES
PH, TK, NK = 8, 16, 128
NE = NK * NK
SLOTS = PH * TK
DEPTH = 2
ALPHA = (2.0 * DEPTH) ** 0.25
SCALE = HD ** -0.5
EPS = 1e-5
LOW = -1e30
GONE = -3e38

SEQW = CW - 1 + DS
RECW = CW - 1 + TP + DB * SEQW
PADW = RECW - (CW - 1)
S0 = TP + CW - 1
SMALL = DB + DB * (CW - 1) + CW + 4
R_H, R_CS, R_CW = 0, DB, DB + DB * (CW - 1)
R_CB = R_CW + CW
R_BA, R_BX, R_LAM = R_CB + 1, R_CB + 2, R_CB + 3
NST = 1 + DB + (CW - 1) + DB * (CW - 1)

HALF = 8
RING = 2 * HALF
U_BODIES = SLOTS // RING
V_BODIES = TT // RING
USES_PER_LAYER = U_BODIES + 2 * (1 + 2 * V_BODIES) + V_BODIES

QCOL = [NS, TT, 2 * TT]
QROWS = [P0, TT, TT]
KEYS = [P0, P0 + TT, P0 + 2 * TT]
NKEYS = PAST + NS
ITEMS = [("p", h, t) for h in range(H) for t in range(NT)] + [("s", b, 0) for b in range(DB)]


class Banks:

    def __init__(self):
        self.at, self.count, self.turn = {}, [0] * 8, 0

    def add(self, name, width):
        b = self.turn % width
        self.turn += 1
        self.at[name] = (b, self.count[b])
        self.count[b] += 1


def psum_plan():
    k = Banks()

    def xt(n, width):
        for i in range(NT):
            for hf in range(2):
                k.add(("xt", n, i, hf), width)

    def out(layer):
        for i in range(NT):
            for hf in range(2):
                k.add(("out", layer, i, hf), 8)

    def peer(layer):
        for j in range(4):
            k.add(("kt", layer, j), 4)
        for m in range(2 * PH):
            k.add(("q", layer, m), 4)
        for i in range(NT):
            for j in range(4):
                k.add(("s", layer, i, j), 4)
        for name in (("ixT", 0), ("ixT", 1), ("wT", 0), ("ixT", 2), ("wT", 1), ("wT", 2)):
            k.add((name[0], layer, name[1]), 4)

    k.add(("small",), 8)
    xt(0, 8)
    for kind in ("rec", "gate"):
        for m in range(C):
            k.add((kind, m), 8)
    for m in range(C):
        k.add(("ra", m), 8)
        k.add(("ix", m), 8)
    for j in range(2):
        k.add(("st", j), 8)
    out(0)
    xt(1, 4)
    peer(0)
    xt(2, 4)
    k.add(("f",), 8)
    for m in range(C):
        k.add(("qf", m), 8)
    for kind in ("kn", "vn"):
        for hf in range(2):
            for i in range(NT):
                k.add((kind, i, hf), 8)
    for i in range(NT):
        for hf in range(2):
            k.add(("kf", i, hf), 8)
    k.add(("lfT",), 8)
    for j in range(4):
        k.add(("lpT", j), 8)
    for n in range(len(ITEMS) + 2):
        if n >= 2:
            k.add(("O", n - 2), 8)
        if n < len(ITEMS):
            if ITEMS[n][0] == "s":
                for j in range(4):
                    k.add(("kc", ITEMS[n][1], j), 8)
            k.add(("S", n), 8)
        if 0 <= n - 1 < len(ITEMS):
            k.add(("T", n - 1), 8)
    out(1)
    xt(3, 4)
    peer(1)
    return k.at


class Chain:

    def __init__(self, eng, sem):
        self.eng, self.sem, self.n = eng, sem, 0

    def add(self, ins):
        ins.then_inc(self.sem, 1)
        self.n += 1
        return self.n

    def wait(self, n=None):
        self.eng.wait_ge(self.sem, self.n if n is None else n)


def trunk(nc, a, o):
    at = psum_plan()
    ctx = ExitStack()
    base = [(nc.sbuf_base + 31) // 32 * 32]

    def place(name, shape, dt=F32, cell=base):
        size = 4 * int(np.prod(shape[1:]))
        t = nc.alloc_sbuf_tensor_at(name, shape, dt, offset=cell[0])
        cell[0] += (size + 31) // 32 * 32
        return t

    X = place("x_nat", [TT, NT, D])
    XT = place("x_transposed", [128, C, T])
    IDENT = place("ident", [128, 128])
    LNG = place("ln_gain", [TT, D])
    LNB = place("ln_bias", [TT, D])
    IOTA16 = place("iota16", [TT, TK])
    PIDX = place("page_rows", [128, DB * PAGES], I32)
    PTI = place("page_table_all", [128, DB * PAGES], I32)
    PTF = place("page_table_f", [128, DB * PAGES])
    IOP = place("iota_partition", [128, 1])
    LPN = place("page_logf", [128, DB * PAGES, H])
    STATS = place("ln_stats", [TT, NT, 2, 6])
    MV = place("ln_mean_var", [TT, NT, 2])
    STD = place("ln_std", [TT, NT, 1])
    RSTD = place("ln_rstd", [TT, NT, 1])

    RA0 = base[0]
    RB0 = RA0 + 4 * 16 * D
    RC0 = RB0 + 4 * 16 * D

    WIN = place("rg_w_in", [128, C, 2 * D], cell=[RA0])
    WO = place("w_out", [128, C, D], cell=[RA0])
    b = [RB0]
    REC = place("rec", [128, C, RECW], cell=b)
    CONV = place("conv", [128, C * PADW], cell=b)
    RA = place("rg_a", [128, C * PADW], cell=b)
    IB = place("rg_i", [128, C * PADW], cell=b)
    TH = place("rg_th", [128, C * PADW], cell=b)
    SMN = place("small_nat", [SMALL, D], cell=b)
    SMT = place("small_t", [128, C, SMALL], cell=b)
    ST = place("state_t", [128, C, NST], cell=b)
    assert b[0] <= RC0
    c = [RC0]
    GATE = place("gate", [128, C, T], cell=c)
    Y = place("mixer_t", [128, C, T], cell=c)
    WG = place("rg_gate_w", [128, 2, C, 128], cell=c)
    STN = place("state_nat", [NST, D], cell=c)
    LSG = [place(f"lam_{n}", [128, C], cell=c) for n in range(7)]
    NEGS = place("a_scale", [128, C], cell=c)
    POSS = place("a_scale_neg", [128, C], cell=c)
    cmax = c[0]

    RINGB = place("expert_rows", [128, RING, D], cell=[RA0])
    WQ = place("peer_w_q", [128, C, 2 * D], cell=[RB0])
    b = [RB0]
    S = place("scores", [TT, NT, 2 * PH, NK], cell=b)
    CAND = place("cand", [TT, PH, TK * TK], cell=b)
    EQ = place("hit", [TT, PH * TK, TK], cell=b)
    V16 = place("top_val", [TT, 2 * PH, TK], cell=b)
    I16 = place("top_idx", [TT, 2 * PH, TK], U32, cell=b)
    I16F = place("top_idx_f", [TT, 2 * PH, TK], cell=b)
    SC = place("pair_val", [TT, PH, TK], cell=b)
    J = place("pair_idx", [TT, PH * TK], U32, cell=b)
    JA = place("pair_a", [TT, PH * TK], U32, cell=b)
    JB = place("pair_b", [TT, PH * TK], U32, cell=b)
    JAF = place("pair_a_f", [TT, PH * TK], cell=b)
    JBF = place("pair_b_f", [TT, PH * TK], cell=b)
    E1 = place("expert_hi", [TT, PH * TK], cell=b)
    E2 = place("expert_lo", [TT, PH * TK], cell=b)
    SUBM = place("pair_shift", [TT, PH, TK], cell=b)
    GS = place("g_sum", [TT, PH], cell=b)
    ACTV = place("u_dot_x", [TT, SLOTS], cell=b)
    GELU = place("act", [TT, SLOTS], cell=b)
    WN = place("w_nat", [TT, SLOTS], cell=b)
    YO = place("y_rows", [HALF, 2, D], cell=b)
    YT = place("y_tile", [TT, D], cell=b)
    assert b[0] <= RC0
    c = [RC0]
    QT = place("peer_q", [128, 2 * PH, T], cell=c)
    KN = place("keys_nat", [128, 2, PH, 128], cell=c)
    KT = place("keys_t", [128, 2, PH, 128], cell=c)
    IDXF = place("idx_f", [TT, NT, SLOTS], cell=c)
    IDX = place("idx", [TT, NT, SLOTS], I32, cell=c)
    IDXT = place("idx_t", [128, NT, TT], I32, cell=c)
    G = place("g", [TT, NT, PH, TK], cell=c)
    WT = place("w_t", [128, NT, TT], cell=c)
    DG = place("w_diag", [128, 2, HALF * HALF], cell=c)
    ACC = place("dots", [TT, 2, HALF], cell=c)
    STG = place("idx_stage", [128, 2, HALF], I32, cell=c)
    cmax = max(cmax, c[0])

    WF = place("fox_w_in", [128, 4, C, 512], cell=[RA0])
    CACHE = place("cache_rows", [128, 2, 2, PAGES, D], cell=[RA0 + 4 * 8 * D])
    b = [RB0]
    QF = place("q_t", [128, H, T], cell=b)
    KF = place("k_t", [128, H, T], cell=b)
    KNF = place("k_nat", [TT, NT, D], cell=b)
    VN = place("v_nat", [TT, NT, D], cell=b)
    OT = place("attn_t", [128, H, T], cell=b)
    PT = place("probs_t", [TT, 2, NT, TT], cell=b)
    PTS = place("probs_t_s", [128, 2, 3, NS], cell=b)
    LFN = place("logf_nat", [TT, NT, H], cell=b)
    assert b[0] <= RC0
    c = [RC0]
    KC = place("cache_k_t", [128, 2, H, NKEYS], cell=c)
    PS = place("probs_s", [NS, 2, NKEYS], cell=c)
    PP = place("probs", [TT, 2, T], cell=c)
    QM = place("q_masked", [128, 2, H * (NS + 1)], cell=c)
    CS = place("c_sample", [H, DB, PAST + DS], cell=c)
    WFF = place("fox_w_f", [128, C, H], cell=c)
    ONES = place("ones", [H, NKEYS], cell=c)
    CP = place("c_prompt", [H, TP], cell=c)
    NCP = place("c_prompt_neg", [H, TP], cell=c)
    MASKC = place("causal", [TT, TT], cell=c)
    MASKS = place("causal_s", [NS, DB, NS], cell=c)
    CSN = place("c_new", [H, NS], cell=c)
    SEL = place("head_sel", [H, NS], cell=c)
    NSEL = place("head_sel_neg", [H, NS], cell=c)
    CQ = place("c_query", [H, 2, NS], cell=c)
    BF = place("b_f", [H, 1], cell=c)
    NMX = place("neg_max", [TT, 2], cell=c)
    SUMS = place("sums", [TT, 2], cell=c)
    RSUM = place("inv_sums", [TT, 2], cell=c)
    cmax = max(cmax, c[0])
    c = [RC0]
    LF = [place(f"logf_{n}", [H, T], cell=c) for n in range(7)]
    LPX = place("logf_sample", [H, DB, PAST + DS], cell=c)
    assert c[0] <= RC0 + 4 * 2 * H * NKEYS
    assert cmax <= nc.sbuf_usable_end, (cmax, nc.sbuf_usable_end)
    BANK = [ctx.enter_context(nc.psum_tensor(f"bank{n}", [128, 512], F32)) for n in range(4)]
    VB = [ctx.enter_context(nc.psum_tensor(f"banks_v{n}", [128, 2, 512], F32)) for n in range(2)]

    def sem(name):
        return ctx.enter_context(nc.semaphore(name))

    mm_done = [sem(f"mm_done{n}") for n in range(8)]
    bank_free = [sem(f"bank_free{n}") for n in range(8)]
    x_loaded, small_loaded, table_loaded = sem("x_loaded"), sem("small_loaded"), sem("table_loaded")
    win_loaded = [sem(f"win_loaded{n}") for n in range(4)]
    wg_loaded, wo_loaded, ln_loaded = sem("wg_loaded"), sem("wo_loaded"), sem("ln_loaded")
    wq_loaded = [sem(f"wq_loaded{n}") for n in range(4)]
    keys_loaded, wff_loaded = sem("keys_loaded"), sem("wff_loaded")
    wf_loaded = [sem(f"wf_loaded{n}") for n in range(6)]
    logf_loaded = sem("logf_loaded")
    cache_loaded = [[sem(f"cache_{kv}_loaded{n}") for n in range(2)] for kv in "kv"]
    y_loaded = sem("y_loaded")
    ident_ready, iota_ready, consts_ready = sem("ident_ready"), sem("iota_ready"), sem("consts_ready")
    pool_steps, page_rows_ready = sem("pool_steps"), sem("page_rows_ready")
    dve_steps, act_steps = sem("dve_steps"), sem("act_steps")
    lam_in, lam_exp, lam_u, lam_ln, lam_scaled = (sem(x) for x in ("lam_in", "lam_exp", "lam_u", "lam_ln", "lam_scaled"))
    conv_done, gates_ready, sq_in, sq_ready, y_ready, state_cols = (
        sem(x) for x in ("conv_done", "gates_ready", "sq_in", "sq_ready", "y_ready", "state_cols"))
    var_ready, std_ready, ln_done = sem("var_ready"), sem("std_ready"), sem("ln_done")
    idxf_ready, idx_ready, sc_ready, exp_ready = (sem(x) for x in ("idxf_ready", "idx_ready", "sc_ready", "exp_ready"))
    staged, issue = sem("staged"), sem("issue")
    row_in = [sem(f"row_in{n}") for n in range(RING)]
    half_used = [sem("half_a_used"), sem("half_b_used")]
    dots_kept, act_ready, w_ready = sem("dots_kept"), sem("act_ready"), sem("w_ready")
    diag_zero, diag_ready, y_rows_ready = sem("diag_zero"), sem("diag_ready"), sem("y_rows_ready")
    y_written = [sem("y_written0"), sem("y_written1")]
    f_in, f_exp, f_u, f_ln, f_ready, c_ready, kc_new = (
        sem(x) for x in ("f_in", "f_exp", "f_u", "f_ln", "f_ready", "c_ready", "kc_new"))
    q_masked, nmax_ready, probs_exp, probs_ready = (
        sem(x) for x in ("q_masked", "nmax_ready", "probs_exp", "probs_ready"))
    stored = sem("stored")
    STORES = [0]

    y_dram = nc.dram_tensor("y_scratch", (T, D), F32, kind="Internal").ap()
    u_dram = a["peer_u"].rearrange("l e d -> (l e) d")
    v_dram = a["peer_v"].rearrange("l e d -> (l e) d")
    k_dram = a["cache_k"].rearrange("l n p h d -> (l n p) (h d)")
    cv_dram = a["cache_v"].rearrange("l n p h d -> (l n p) (h d)")
    cl_dram = a["cache_logf"].rearrange("l n p h -> (l n p) h")

    def bank(name):
        n = at[name][0]
        return BANK[n] if n < 4 else VB[(n - 4) // 2][:, (n - 4) % 2, :]

    def ps(name, rows, lo, hi):
        n = at[name][0]
        return BANK[n][0:rows, lo:hi] if n < 4 else VB[(n - 4) // 2][0:rows, (n - 4) % 2, lo:hi]

    def begin(pe, name):
        n, uses = at[name]
        if uses:
            pe.wait_ge(bank_free[n], uses)

    def computed(eng, name):
        n, uses = at[name]
        eng.wait_ge(mm_done[n], uses + 1)

    def moved(eng, name):
        n, uses = at[name]
        eng.wait_ge(bank_free[n], uses + 1)

    def padded(t):
        return t[:, :].rearrange("p (m t) -> p m t", m=C)

    block = ctx.enter_context(nc.Block())

    @block.sync
    def _(sp):
        def store(dst, src):
            sp.dma_start(dst, src).then_inc(stored, 16)
            STORES[0] += 16

        xs = a["x_sample"].rearrange("b s d -> (b s) d")
        xp = a["x_prompt"].rearrange("b s d -> (b s) d")
        n0 = P0 - META
        sp.dma_start(X[0:NS, 0, :], xs).then_inc(x_loaded, 16)
        sp.dma_start(X[NS:NS + META, 0, :], a["meta_tokens"]).then_inc(x_loaded, 16)
        sp.dma_start(X[NS + META:TT, 0, :], xp[0:n0, :]).then_inc(x_loaded, 16)
        for i in (1, 2):
            sp.dma_start(X[:, i, :], xp[n0 + (i - 1) * TT:n0 + i * TT, :]).then_inc(x_loaded, 16)
        for row, src in ((R_H, a["state_h"][0]), (R_CS, a["state_conv"][0].rearrange("b j d -> (b j) d")),
                         (R_CW, a["rg_conv_w"][0]), (R_CB, a["rg_conv_b"]), (R_BA, a["rg_b_a"]),
                         (R_BX, a["rg_b_x"]), (R_LAM, a["rg_lambda"])):
            sp.dma_start(SMN[row:row + src.shape[0], :], src).then_inc(small_loaded, 16)
        pt = a["page_table"].rearrange("b j -> (b j)")
        sp.dma_start(PTI[:, :], pt.partition_broadcast(128)).then_inc(table_loaded, 16)
        win = a["rg_w_in"][0].rearrange("(c p) n -> p c n", p=128)
        for blk in (2, 3, 0, 1):
            sp.dma_start(WIN[:, :, blk * 512:blk * 512 + 512], win[:, :, blk * 512:blk * 512 + 512]).then_inc(win_loaded[blk], 16)
        sp.dma_start(WG[:, 0, :, :], a["rg_w_a"][0].rearrange("n c d -> c n d")).then_inc(wg_loaded, 16)
        sp.dma_start(WG[:, 1, :, :], a["rg_w_x"][0].rearrange("n c d -> c n d")).then_inc(wg_loaded, 16)

        def load_ln(n, g, bb):
            if n:
                sp.wait_ge(ln_done, NT * n)
            sp.dma_start(LNG[:, :], g.partition_broadcast(TT)).then_inc(ln_loaded, 16)
            sp.dma_start(LNB[:, :], bb.partition_broadcast(TT)).then_inc(ln_loaded, 16)

        load_ln(0, a["ln_mix_g"][0], a["ln_mix_b"][0])
        computed(sp, ("gate", C - 1))
        sp.dma_start(WO[:, :, :], a["rg_w_out"][0].rearrange("(c p) n -> p c n", p=128)).then_inc(wo_loaded, 16)
        def load_peer(layer):
            wq = a["peer_w_q"][layer].rearrange("(c p) n -> p c n", p=128)
            for blk in range(4):
                sp.dma_start(WQ[:, :, blk * 512:blk * 512 + 512], wq[:, :, blk * 512:blk * 512 + 512]).then_inc(wq_loaded[blk], 16)
            for half, keys in enumerate((a["peer_keys1"], a["peer_keys2"])):
                sp.dma_start(KN[:, half, :, :], keys[layer].rearrange("h k c -> k h c")).then_inc(keys_loaded, 16)

        sp.wait_ge(y_ready, 1)
        computed(sp, ("st", 1))
        for j in range(2):
            moved(sp, ("st", j))
        store(o["state_h_prompt"][0], STN[0:1, :])
        store(o["state_h_sample"][0], STN[1:1 + DB, :])
        store(o["state_conv_prompt"][0, 0], STN[1 + DB:DB + CW, :])
        store(o["state_conv_sample"][0].rearrange("b j d -> (b j) d"), STN[DB + CW:NST, :])
        computed(sp, ("out", 0, NT - 1, 1))
        sp.wait_ge(stored, STORES[0])
        load_peer(0)
        load_ln(1, a["ln_ffn_g"][0], a["ln_ffn_b"][0])

        def y_rows(layer):
            for i in range(NT):
                first = (layer * NT + i) * V_BODIES
                with sp.Fori(0, V_BODIES) as j:
                    for s in range(2):
                        sp.wait_ge(y_rows_ready, 2 * j + (2 * first + s + 1))
                        sp.dma_start(y_dram[bass.ds(j * RING + (i * TT + s * HALF), HALF), :], YO[:, s, :]).then_inc(y_written[s], 16)
                for s in range(2):
                    sp.wait_ge(y_written[s], 16 * (first + V_BODIES))
                done = NT * (2 * layer + 1) + i
                sp.wait_ge(ln_done, done)
                sp.dma_start(YT[:, :], y_dram[i * TT:(i + 1) * TT, :]).then_inc(y_loaded, 16)

        y_rows(0)

        wf = a["fox_w_in"][0].rearrange("(c p) n -> p c n", p=128)
        sp.wait_ge(y_loaded, 16 * NT)
        sp.dma_start(WFF[:, :, :], wf[:, :, 3 * D:3 * D + H]).then_inc(wff_loaded, 16)
        sp.dma_start(BF[:, :], a["fox_b_f"].rearrange("l h -> h l")).then_inc(wff_loaded, 16)
        for blk in range(6):
            if blk >= 4:
                computed(sp, ("qf", 4 * (blk - 4) + 3))
            sp.dma_start(WF[:, blk % 4, :, :], wf[:, :, blk * 512:blk * 512 + 512]).then_inc(wf_loaded[blk], 16)
        load_ln(2, a["ln_mix_g"][1], a["ln_mix_b"][1])
        for i in range(NT):
            computed(sp, ("vn", i, 1))
        sp.dma_start(WO[:, :, :], a["fox_w_o"][0].rearrange("(c p) n -> p c n", p=128)).then_inc(wo_loaded, 16)
        rows = [(0, TT), (TT - NS, TT), (2 * TT - NS, TT)]
        for kind, buf, prompt, sample in (("kn", KNF, o["k_prompt"], o["k_sample"]), ("vn", VN, o["v_prompt"], o["v_sample"])):
            for i in range(NT):
                for hf in range(2):
                    moved(sp, (kind, i, hf))
            prompt = prompt.rearrange("l b t h d -> (l b t) (h d)")
            sample = sample.rearrange("l b t h d -> (l b t) (h d)")
            store(sample, buf[0:NS, 0, :])
            store(prompt[0:P0, :], buf[NS:TT, 0, :])
            for i in (1, 2):
                store(prompt[rows[i][0]:rows[i][0] + TT, :], buf[:, i, :])
        moved(sp, ("lfT",))
        lp = o["logf_prompt"].rearrange("l b t h -> (l b t) h")
        store(o["logf_sample"].rearrange("l b t h -> (l b t) h"), LFN[0:NS, 0, :])
        store(lp[0:P0, :], LFN[NS:TT, 0, :])
        for i in (1, 2):
            store(lp[rows[i][0]:rows[i][0] + TT, :], LFN[:, i, :])
        computed(sp, ("out", 1, NT - 1, 1))
        sp.wait_ge(stored, STORES[0])
        load_peer(1)
        load_ln(3, a["ln_ffn_g"][1], a["ln_ffn_b"][1])
        y_rows(1)
        sp.wait_ge(ln_done, NT * 3 + 1)
        store(o["y_sample"].rearrange("b s d -> (b s) d"), X[0:NS, 0, :])
        yp = o["y_prompt"].rearrange("b s d -> (b s) d")
        store(yp[0:n0, :], X[NS + META:TT, 0, :])
        for i in (1, 2):
            sp.wait_ge(ln_done, NT * 3 + i + 1)
            store(yp[n0 + (i - 1) * TT:n0 + i * TT, :], X[:, i, :])
        sp.wait_ge(stored, STORES[0])

    @block.gpsimd
    def _(g):
        steps = Chain(g, pool_steps)
        steps.add(g.memset(IDENT[:, :], 0.0))
        steps.wait()
        g.affine_select(out=IDENT[:, :], in_=IDENT[:, :], compare_op=ALU.not_equal, fill=1.0,
                        base=0, pattern=[[-1, 128]], channel_multiplier=1).then_inc(ident_ready, 1)
        g.iota(IOP[:, :], pattern=[[0, 1]], base=0, channel_multiplier=1,
               allow_small_or_imprecise_dtypes=True).then_inc(iota_ready, 1)
        g.iota(IOTA16[:, :], pattern=[[1, TK]], base=0, channel_multiplier=0,
               allow_small_or_imprecise_dtypes=True).then_inc(iota_ready, 1)
        g.wait_ge(page_rows_ready, 1)
        for n in range(DB * PAGES):
            g.indirect_dma_start(out=LPN[:, n, :], out_offset=None, in_=cl_dram,
                                 in_offset=bass.IndirectOffsetOnAxis(ap=PIDX[:, n:n + 1], axis=0)).then_inc(logf_loaded, 16)

        def gather(half, k, table, rows, stage):
            slot = half * HALF + k
            g.indirect_dma_start(out=RINGB[0:rows, slot, :], out_offset=None, in_=table,
                                 in_offset=bass.IndirectOffsetOnAxis(ap=STG[0:rows, stage, k:k + 1], axis=0)).then_inc(row_in[slot], 16)

        staged_n = [0]

        def half_ring(half, use, idx_cols, rows, table, stage_count):
            g.wait_ge(half_used[half], HALF * use)
            g.tensor_copy(STG[0:rows, half, :], idx_cols).then_inc(staged, 1)
            g.wait_ge(staged, stage_count)
            g.sem_inc(issue, 1)
            for k in range(HALF):
                gather(half, k, table, rows, half)

        def experts(layer):
            use = layer * USES_PER_LAYER

            def u_bodies(i, col, n, use):
                base_n = staged_n[0]
                with g.Fori(0, n) as j:
                    for half in range(2):
                        half_ring(half, j + use, IDX[:, i, bass.ds(j * RING + (col + half * HALF), HALF)], TT, u_dram,
                                  2 * j + (base_n + half + 1))
                staged_n[0] += 2 * n

            def uv_bodies(i, use):
                base_n = staged_n[0]
                with g.Fori(0, V_BODIES) as j:
                    for s in range(2):
                        half_ring(0, 2 * j + (use + s), IDX[:, i + 1, bass.ds(j * RING + (RING + s * HALF), HALF)], TT, u_dram,
                                  4 * j + (base_n + 2 * s + 1))
                        half_ring(1, 2 * j + (use + s), IDXT[:, i, bass.ds(j * RING + s * HALF, HALF)], 128, v_dram,
                                  4 * j + (base_n + 2 * s + 2))
                staged_n[0] += 4 * V_BODIES

            g.wait_ge(idx_ready, layer * NT + 1)
            u_bodies(0, 0, U_BODIES, use)
            use += U_BODIES
            for i in range(NT - 1):
                g.wait_ge(idx_ready, layer * NT + i + 2)
                moved(g, ("ixT", layer, i))
                u_bodies(i + 1, 0, 1, use)
                use += 1
                uv_bodies(i, use)
                use += 2 * V_BODIES
            moved(g, ("ixT", layer, NT - 1))
            base_n = staged_n[0]
            with g.Fori(0, V_BODIES) as j:
                for s in range(2):
                    half_ring(s, j + use, IDXT[:, NT - 1, bass.ds(j * RING + s * HALF, HALF)], 128, v_dram,
                              2 * j + (base_n + s + 1))
            staged_n[0] += 2 * V_BODIES

        computed(g, ("out", 0, NT - 1, 1))
        experts(0)

        g.wait_ge(ln_done, 2 * NT)
        steps.add(g.memset(MASKC[:, :], 0.0))
        steps.add(g.memset(MASKS[:, :, :], 0.0))
        steps.add(g.memset(SEL[:, :], 1.0))
        steps.add(g.memset(NSEL[:, :], -1.0))
        steps.add(g.memset(ONES[:, :], 1.0))
        steps.add(g.memset(QM[:, :, :], 0.0))
        steps.add(g.memset(PP[:, :, 0:NS], 0.0))
        steps.wait()
        steps.add(g.affine_select(out=MASKC[:, :], in_=MASKC[:, :], compare_op=ALU.is_ge, fill=LOW,
                                  base=0, pattern=[[-1, TT]], channel_multiplier=1))
        steps.add(g.affine_select(out=MASKS[:, :, :], in_=MASKS[:, :, :], compare_op=ALU.is_equal, fill=LOW,
                                  base=0, pattern=[[1, DB], [-1, DB], [0, DS]], channel_multiplier=0))
        steps.wait()
        steps.add(g.affine_select(out=MASKS[:, :, :], in_=MASKS[:, :, :], compare_op=ALU.is_ge, fill=LOW,
                                  base=0, pattern=[[0, DB], [0, DB], [-H, DS]], channel_multiplier=1))
        steps.add(g.affine_select(out=SEL[:, :], in_=SEL[:, :], compare_op=ALU.is_equal, fill=0.0,
                                  base=0, pattern=[[0, DS], [-1, H]], channel_multiplier=1))
        steps.add(g.affine_select(out=NSEL[:, :], in_=NSEL[:, :], compare_op=ALU.is_equal, fill=0.0,
                                  base=0, pattern=[[0, DS], [-1, H]], channel_multiplier=1))
        steps.wait()
        g.sem_inc(consts_ready, 1)
        for i in range(NT):
            computed(g, ("vn", i, 1))
        for m in range(H):
            moved(g, ("qf", m))
        g.wait_ge(c_ready, 1)
        for bb in range(DB):
            for kv, src in enumerate((k_dram, cv_dram)):
                if bb >= 2:
                    computed(g, ("O", H * NT + bb - 2) if kv else ("kc", bb - 2, 3))
                for pg in range(PAGES):
                    n = bb * PAGES + pg
                    g.indirect_dma_start(out=CACHE[:, bb % 2, kv, pg, :], out_offset=None, in_=src,
                                         in_offset=bass.IndirectOffsetOnAxis(ap=PIDX[:, n:n + 1], axis=0)).then_inc(cache_loaded[kv][bb % 2], 16)
            qm = QM[:, bb % 2, :].rearrange("p (h x) -> p h x", h=H)[:, :, 0:NS:H]
            g.tensor_copy(qm, QF[:, :, bb * DS:(bb + 1) * DS])
            g.tensor_tensor(CQ[:, bb % 2, :].rearrange("p (s h) -> p s h", h=H), SEL[:, :].rearrange("p (s h) -> p s h", h=H),
                            CS[:, bb, PAST:PAST + DS].unsqueeze(2).to_broadcast([H, DS, H]), ALU.mult).then_inc(q_masked, 1)
        computed(g, ("out", 1, NT - 1, 1))
        experts(1)

    @block.tensor
    def _(pe):
        def done(name, ins):
            ins.then_inc(mm_done[at[name][0]], 1)

        def transposes(name, pieces):
            begin(pe, name)
            for rows, col, src in pieces:
                k = src.shape[0]
                last = pe.transpose(ps(name, rows, col, col + k), src, IDENT[0:k, 0:k])
            done(name, last)

        def x_transposes(n):
            for i in range(NT):
                if n:
                    pe.wait_ge(ln_done, NT * (n - 1) + i + 1)
                for hf in range(2):
                    transposes(("xt", n, i, hf), [(128, q * TT, X[:, i, (4 * hf + q) * 128:(4 * hf + q + 1) * 128]) for q in range(4)])

        def product(name, rows, pairs, lo=0):
            begin(pe, name)
            pairs = list(pairs)
            for n, (lhsT, rhs) in enumerate(pairs):
                last = pe.matmul(ps(name, rows, lo, lo + rhs.shape[-1]), lhsT=lhsT, rhs=rhs, start=n == 0, stop=n == len(pairs) - 1)
            done(name, last)

        def x_transposed(n):
            for i in range(NT):
                for hf in range(2):
                    moved(pe, ("xt", n, i, hf))

        def mixer_out(layer, src):
            pe.wait_ge(wo_loaded, 16 * (layer + 1))
            for i in range(NT):
                for hf in range(2):
                    product(("out", layer, i, hf), TT, [(src[:, c, i * TT:(i + 1) * TT], WO[:, c, hf * 512:hf * 512 + 512]) for c in range(C)])

        pe.wait_ge(ident_ready, 1)
        pe.wait_ge(small_loaded, 16 * 7)
        transposes(("small",), [(128, c * SMALL, SMN[:, c * 128:c * 128 + 128]) for c in range(C)])
        pe.wait_ge(x_loaded, 16 * 5)
        x_transposes(0)
        x_transposed(0)
        for kind, first in (("rec", C), ("gate", 0)):
            for m in range(C):
                col = first + m
                pe.wait_ge(win_loaded[col // 4], 16)
                product((kind, m), 128, [(WIN[:, c, col * 128:col * 128 + 128], XT[:, c, :]) for c in range(C)])
        pe.wait_ge(wg_loaded, 32)
        for m in range(C):
            pe.wait_ge(conv_done, m + 1)
            for w, kind in enumerate(("ra", "ix")):
                product((kind, m), 128, [(WG[:, w, m, :], CONV[:, m * PADW:(m + 1) * PADW])])
        pe.wait_ge(state_cols, 1)
        for j in range(2):
            transposes(("st", j), [(NST, q * 128, ST[:, 4 * j + q, :]) for q in range(4)])
        pe.wait_ge(y_ready, 1)
        mixer_out(0, Y)

        def v_loop(layer, i, use, halves, step):
            first = (layer * NT + i) * V_BODIES
            with pe.Fori(0, V_BODIES) as j:
                for s in range(2):
                    half = halves[s]
                    use_s = step * j + (use + (s if step == 2 else 0))
                    pe.wait_ge(diag_ready, 2 * j + (2 * first + s + 1))
                    for k in range(HALF):
                        pe.wait_ge(row_in[half * HALF + k], 16 * use_s + 16)
                        for hf in range(2):
                            last = pe.matmul(VB[s][0:HALF, hf, :], lhsT=DG[:, s, k * HALF:(k + 1) * HALF],
                                             rhs=RINGB[:, half * HALF + k, hf * 512:hf * 512 + 512], start=k == 0, stop=k == HALF - 1)
                        last.then_inc(half_used[half], 1)

        def experts(layer):
            pe.wait_ge(keys_loaded, 32 * (layer + 1))
            for j in range(4):
                half, h0 = j // 2, (j % 2) * 4
                transposes(("kt", layer, j), [(128, q * 128, KN[:, half, h0 + q, :]) for q in range(4)])
            x_transposed(2 * layer + 1)
            for m in range(2 * PH):
                pe.wait_ge(wq_loaded[m // 4], 16 * (layer + 1))
                product(("q", layer, m), 128, [(WQ[:, c, m * 128:m * 128 + 128], XT[:, c, :]) for c in range(C)])
            for j in range(4):
                moved(pe, ("kt", layer, j))
            for i in range(NT):
                for j in range(4):
                    name = ("s", layer, i, j)
                    begin(pe, name)
                    for q in range(4):
                        m = 4 * j + q
                        moved(pe, ("q", layer, m))
                        last = pe.matmul(ps(name, TT, q * 128, q * 128 + 128), lhsT=QT[:, m, i * TT:(i + 1) * TT],
                                         rhs=KT[:, m % 2, m // 2, :], start=True, stop=True)
                    done(name, last)

            def index_columns(i):
                pe.wait_ge(idxf_ready, layer * NT + i + 1)
                transposes(("ixT", layer, i), [(128, 0, IDXF[:, i, :])])

            def weight_columns(i):
                pe.wait_ge(w_ready, layer * NT + i + 1)
                transposes(("wT", layer, i), [(128, 0, WN[:, :])])

            use = layer * USES_PER_LAYER + U_BODIES
            index_columns(0)
            index_columns(1)
            weight_columns(0)
            index_columns(2)
            v_loop(layer, 0, use + 1, (1, 1), 2)
            use += 1 + 2 * V_BODIES
            weight_columns(1)
            v_loop(layer, 1, use + 1, (1, 1), 2)
            use += 1 + 2 * V_BODIES
            weight_columns(2)
            v_loop(layer, 2, use, (0, 1), 1)

        x_transposes(1)
        experts(0)
        x_transposes(2)

        pe.wait_ge(y_rows_ready, 2 * NT * V_BODIES)
        x_transposed(2)
        pe.wait_ge(wff_loaded, 32)
        product(("f",), H, [(WFF[:, c, :], XT[:, c, :]) for c in range(C)])
        for m in range(H):
            pe.wait_ge(wf_loaded[m // 4], 16)
            product(("qf", m), 128, [(WF[:, m // 4, c, (m % 4) * 128:(m % 4) * 128 + 128], XT[:, c, :]) for c in range(C)])
        for n, kind in enumerate(("kn", "vn")):
            for hf in range(2):
                blk = 2 + 2 * n + hf
                pe.wait_ge(wf_loaded[blk], 16)
                for i in range(NT):
                    product((kind, i, hf), TT, [(XT[:, c, i * TT:(i + 1) * TT], WF[:, blk % 4, c, :]) for c in range(C)])
        for i in range(NT):
            for hf in range(2):
                moved(pe, ("kn", i, hf))
                transposes(("kf", i, hf), [(128, q * TT, KNF[:, i, (4 * hf + q) * 128:(4 * hf + q + 1) * 128]) for q in range(4)])
        pe.wait_ge(f_ready, 1)
        transposes(("lfT",), [(TT, i * H, LF[6][:, i * TT:(i + 1) * TT]) for i in range(NT)])
        pe.wait_ge(logf_loaded, 16 * DB * PAGES)
        for j in range(4):
            transposes(("lpT", j), [(H, q * 128, LPN[:, 4 * j + q, :]) for q in range(4)])
        for i in range(NT):
            for hf in range(2):
                moved(pe, ("kf", i, hf))
                moved(pe, ("vn", i, hf))
        for m in range(H):
            moved(pe, ("qf", m))
        pe.wait_ge(c_ready, 1)
        pe.wait_ge(consts_ready, 1)
        pe.wait_ge(ident_ready, 1)

        def scores(n):
            kind, x, t = ITEMS[n]
            name = ("S", n)
            if kind == "p":
                nq, nk, q0 = QROWS[t], KEYS[t], QCOL[t]
                pick = IDENT[0:H, x:x + 1]
                product(name, nq, [(QF[:, x, q0:q0 + nq], KF[:, x, NS:NS + nk]),
                                   (CP[:, q0 - NS:q0 - NS + nq], pick.to_broadcast([H, nk])),
                                   (pick.to_broadcast([H, nq]), NCP[:, 0:nk])])
                return
            for j in range(4):
                moved(pe, ("kc", x, j))
            pe.wait_ge(q_masked, x + 1)
            pe.wait_ge(kc_new, 1)
            begin(pe, name)
            pe.matmul(ps(name, NS, 0, NKEYS), lhsT=CQ[:, x % 2, :], rhs=ONES[:, :], start=True, stop=False)
            pe.matmul(ps(name, NS, 0, PAST), lhsT=NSEL[:, :], rhs=CS[:, x, 0:PAST], start=False, stop=False)
            pe.matmul(ps(name, NS, PAST, NKEYS), lhsT=NSEL[:, :], rhs=CSN[:, :], start=False, stop=False)
            for h in range(H):
                last = pe.matmul(ps(name, NS, 0, NKEYS), lhsT=QM[:, x % 2, h * NS:(h + 1) * NS], rhs=KC[:, x % 2, h, :],
                                 start=False, stop=h == H - 1)
            done(name, last)

        def probs_t(n):
            kind, x, t = ITEMS[n]
            pe.wait_ge(probs_ready, n + 1)
            if kind == "p":
                nq = QROWS[t]
                transposes(("T", n), [(TT, j * TT, PP[0:nq, n % 2, j * TT:(j + 1) * TT]) for j in range(t + 1)])
            else:
                transposes(("T", n), [(128, 0, PS[:, x % 2, 0:128]), (128, NS, PS[:, x % 2, 128:256]), (NS, 2 * NS, PS[:, x % 2, 256:NKEYS])])

        def attend(n):
            kind, x, t = ITEMS[n]
            moved(pe, ("T", n))
            if kind == "p":
                nq = QROWS[t]
                product(("O", n), 128, [(VN[:, j, x * 128:(x + 1) * 128], PT[:, n % 2, j, 0:nq]) for j in range(t + 1)])
                return
            name = ("O", n)
            begin(pe, name)
            pe.wait_ge(cache_loaded[1][x % 2], 16 * PAGES * (x // 2 + 1))
            for h in range(H):
                cols = slice(h * 128, h * 128 + 128)
                for j in range(3):
                    lhsT = CACHE[:, x % 2, 1, j, cols] if j < 2 else VN[0:NS, 0, cols]
                    k = 128 if j < 2 else NS
                    last = pe.matmul(ps(name, 128, h * DS, (h + 1) * DS), lhsT=lhsT, rhs=PTS[0:k, x % 2, j, h:NS:H], start=j == 0, stop=j == 2)
            done(name, last)

        for n in range(len(ITEMS) + 2):
            if n >= 2:
                attend(n - 2)
            if n < len(ITEMS):
                kind, x, _ = ITEMS[n]
                if kind == "s":
                    pe.wait_ge(cache_loaded[0][x % 2], 16 * PAGES * (x // 2 + 1))
                    for j in range(4):
                        pg, h0 = j // 2, (j % 2) * 4
                        transposes(("kc", x, j), [(128, q * 128, CACHE[:, x % 2, 0, pg, (h0 + q) * 128:(h0 + q + 1) * 128]) for q in range(4)])
                scores(n)
            if 0 <= n - 1 < len(ITEMS):
                probs_t(n - 1)
        for n in range(len(ITEMS) - 8, len(ITEMS)):
            moved(pe, ("O", n))
        mixer_out(1, OT)
        x_transposes(3)
        experts(1)

    @block.scalar
    def _(act):
        steps = Chain(act, act_steps)

        def out_of(name, dst, src):
            computed(act, name)
            act.copy(dst, src).then_inc(bank_free[at[name][0]], 1)

        def x_transposed(n):
            for i in range(NT):
                out_of(("xt", n, i, 0), XT[:, 0:4, i * TT:(i + 1) * TT], ps(("xt", n, i, 0), 128, 0, 4 * TT).rearrange("p (c t) -> p c t", c=4))

        def std(n, i):
            act.wait_ge(var_ready, NT * n + i + 1)
            act.activation(STD[:, i, :], MV[:, i, 1:2], ACT.Sqrt).then_inc(std_ready, 1)

        act.wait_ge(lam_in, 1)
        act.activation(LSG[1][:, :], LSG[0][:, :], ACT.Exp).then_inc(lam_exp, 1)
        act.wait_ge(lam_u, 1)
        act.activation(LSG[3][:, :], LSG[2][:, :], ACT.Ln).then_inc(lam_ln, 1)
        x_transposed(0)
        for m in range(C):
            computed(act, ("rec", m))
            name = ("rec", m)
            act.copy(REC[:, m, CW - 1:CW - 1 + TP], ps(name, 128, NS, T))
            act.copy(REC[:, m, S0:RECW].rearrange("p (b t) -> p b t", b=DB)[:, :, CW - 1:SEQW],
                     ps(name, 128, 0, NS).rearrange("p (b t) -> p b t", b=DB)).then_inc(bank_free[at[name][0]], 1)
        for m in range(C):
            name = ("gate", m)
            computed(act, name)
            act.activation(GATE[:, m, :], ps(name, 128, 0, T), ACT.Gelu_apprx_tanh).then_inc(bank_free[at[name][0]], 1)
        moved(act, ("small",))
        for m in range(C):
            for kind, row, dst in (("ra", R_BA, RA), ("ix", R_BX, IB)):
                name = (kind, m)
                computed(act, name)
                act.activation(dst[:, m * PADW:(m + 1) * PADW], ps(name, 128, 0, PADW), ACT.Sigmoid,
                               bias=SMT[:, m, row:row + 1]).then_inc(bank_free[at[name][0]], 1)
        act.wait_ge(lam_scaled, 1)
        for m in range(C):
            moved(act, ("ra", m))
            act.activation(TH[:, m * PADW:(m + 1) * PADW], RA[:, m * PADW:(m + 1) * PADW], ACT.Tanh, scale=POSS[:, m:m + 1])
            act.activation(RA[:, m * PADW:(m + 1) * PADW], RA[:, m * PADW:(m + 1) * PADW], ACT.Exp, scale=NEGS[:, m:m + 1]).then_inc(gates_ready, 1)
        act.wait_ge(sq_in, 1)
        act.activation(TH[:, :], CONV[:, :], ACT.Sqrt).then_inc(sq_ready, 1)
        for j in range(2):
            out_of(("st", j), STN[:, j * 512:(j + 1) * 512], ps(("st", j), NST, 0, 512))
        for i in range(NT):
            std(0, i)

        def v_side(layer, i, use, halves, step):
            first = (layer * NT + i) * V_BODIES
            moved(act, ("wT", layer, i))
            with act.Fori(0, V_BODIES) as j:
                for s in range(2):
                    act.copy(DG[:, s, 0:HALF * HALF:HALF + 1], WT[:, i, bass.ds(j * RING + s * HALF, HALF)]).then_inc(diag_ready, 1)
                for s in range(2):
                    use_s = step * j + (use + (s if step == 2 else 0))
                    act.wait_ge(half_used[halves[s]], HALF * use_s + HALF)
                    act.wait_ge(y_written[s], 16 * j + 16 * first)
                    act.copy(YO[:, s, :].rearrange("p (a d) -> p a d", a=2), VB[s][0:HALF, :, :]).then_inc(y_rows_ready, 1)

        def experts(layer):
            for m in range(0, 2 * PH, 2):
                out_of(("q", layer, m), QT[:, m, :], ps(("q", layer, m), 128, 0, T))
            for i in range(NT):
                for j in range(0, 4, 2):
                    name = ("s", layer, i, j)
                    out_of(name, S[:, i, 4 * j:4 * j + 4, :].rearrange("p m k -> p (m k)"), ps(name, TT, 0, 512))

            def g_exp(i):
                act.wait_ge(sc_ready, layer * NT + i + 1)
                act.activation(G[:, i, :, :], SUBM[:, :, :], ACT.Exp).then_inc(exp_ready, 1)

            def index_columns(i):
                out_of(("ixT", layer, i), IDXT[:, i, :], ps(("ixT", layer, i), 128, 0, TT))

            def weights(i):
                act.wait_ge(dots_kept, 2 * U_BODIES * (layer * NT + i + 1))
                act.activation(GELU[:, :], ACTV[:, :], ACT.Gelu_apprx_tanh).then_inc(act_ready, 1)
                out_of(("wT", layer, i), WT[:, i, :], ps(("wT", layer, i), 128, 0, TT))

            n = 2 * layer + 1
            use = layer * USES_PER_LAYER + U_BODIES
            for i in range(2):
                g_exp(i)
                index_columns(i)
            act.wait_ge(diag_zero, layer + 1)
            weights(0)
            g_exp(2)
            index_columns(2)
            v_side(layer, 0, use + 1, (1, 1), 2)
            use += 1 + 2 * V_BODIES
            weights(1)
            std(n, 0)
            v_side(layer, 1, use + 1, (1, 1), 2)
            use += 1 + 2 * V_BODIES
            weights(2)
            std(n, 1)
            v_side(layer, 2, use, (0, 1), 1)
            std(n, 2)

        x_transposed(1)
        experts(0)
        x_transposed(2)

        act.wait_ge(f_in, 1)
        act.activation(LF[1][:, :], LF[0][:, :], ACT.Exp).then_inc(f_exp, 1)
        act.wait_ge(f_u, 1)
        act.activation(LF[3][:, :], LF[2][:, :], ACT.Ln).then_inc(f_ln, 1)
        for m in range(H):
            name = ("qf", m)
            computed(act, name)
            act.mul(QF[:, m, :], ps(name, 128, 0, T), SCALE).then_inc(bank_free[at[name][0]], 1)
        for hf in range(2):
            for i in range(NT):
                out_of(("vn", i, hf), VN[:, i, hf * 512:hf * 512 + 512], ps(("vn", i, hf), TT, 0, 512))
        for n in range(len(ITEMS) + 1):
            if n < len(ITEMS):
                kind, x, t = ITEMS[n]
                if kind == "s":
                    for j in (0, 2):
                        out_of(("kc", x, j), KC[:, x % 2, 0:4, (j // 2) * 128:(j // 2) * 128 + 128],
                               ps(("kc", x, j), 128, 0, 512).rearrange("p (h k) -> p h k", h=4))
                act.wait_ge(nmax_ready, n + 1)
                name = ("S", n)
                if kind == "p":
                    nq, nk = QROWS[t], KEYS[t]
                    dst, src = PP[0:nq, n % 2, NS:NS + nk], ps(name, nq, 0, nk)
                else:
                    nq = NS
                    dst, src = PS[:, x % 2, :], ps(name, NS, 0, NKEYS)
                act.activation(dst, src, ACT.Exp, bias=NMX[0:nq, n % 2:n % 2 + 1], accum_out=SUMS[0:nq, n % 2:n % 2 + 1]).then_inc(bank_free[at[name][0]], 1)
            if n >= 1:
                kind, x, t = ITEMS[n - 1]
                name = ("T", n - 1)
                computed(act, name)
                if kind == "p":
                    nq = QROWS[t]
                    act.copy(PT[:, (n - 1) % 2, 0:t + 1, 0:nq], ps(name, TT, 0, (t + 1) * TT).rearrange("p (j q) -> p j q", q=TT)[:, :, 0:nq])\
                        .then_inc(bank_free[at[name][0]], 1)
                else:
                    act.copy(PTS[:, x % 2, 0:2, :], ps(name, 128, 0, 2 * NS).rearrange("p (j q) -> p j q", q=NS))
                    act.copy(PTS[0:NS, x % 2, 2, :], ps(name, NS, 2 * NS, 3 * NS)).then_inc(bank_free[at[name][0]], 1)
        for i in range(NT):
            std(2, i)
        x_transposed(3)
        experts(1)

    @block.vector
    def _(v):
        steps = Chain(v, dve_steps)

        def out_of(name, dst, src):
            computed(v, name)
            v.tensor_copy(dst, src).then_inc(bank_free[at[name][0]], 1)

        def x_transposed(n):
            for i in range(NT):
                out_of(("xt", n, i, 1), XT[:, 4:8, i * TT:(i + 1) * TT], ps(("xt", n, i, 1), 128, 0, 4 * TT).rearrange("p (c t) -> p c t", c=4))

        def log_sigmoid(z, t, into, sent_in, got_exp, sent_u, got_ln):
            v.scalar_tensor_tensor(out=t[0], in0=z, scalar=-1.0, in1=z, op0=ALU.mult, op1=ALU.min).then_inc(sent_in, 1)
            v.wait_ge(got_exp, 1)
            v.tensor_scalar(t[2], t[1], 1.0, None, ALU.add).then_inc(sent_u, 1)
            v.wait_ge(sent_u, 1)
            steps.add(v.tensor_scalar(t[0], t[2], 1.0, None, ALU.subtract))
            steps.wait()
            steps.add(v.tensor_tensor(t[0], t[1], t[0], ALU.subtract))
            steps.add(v.reciprocal(t[4], t[2]))
            steps.wait()
            steps.add(v.tensor_tensor(t[0], t[0], t[4], ALU.mult))
            v.wait_ge(got_ln, 1)
            steps.wait()
            steps.add(v.tensor_tensor(t[0], t[0], t[3], ALU.add))
            steps.wait()
            steps.add(v.scalar_tensor_tensor(out=into, in0=z, scalar=0.0, in1=t[0], op0=ALU.min, op1=ALU.subtract))
            steps.wait()

        def layer_norm(n, i):
            v.wait_ge(ln_loaded, 32 * (n + 1))
            for hf in range(2):
                k = steps.add(v.bn_stats(STATS[:, i, hf, :], X[:, i, hf * 512:hf * 512 + 512]))
            steps.wait()
            steps.add(v.bn_aggr(MV[:, i, :], STATS[:, i, :, :].rearrange("p a b -> p (a b)")))
            steps.wait()
            v.tensor_scalar(MV[:, i, 1:2], MV[:, i, 1:2], EPS, None, ALU.add).then_inc(var_ready, 1)
            v.wait_ge(std_ready, NT * n + i + 1)
            steps.add(v.reciprocal(RSTD[:, i, :], STD[:, i, :]))
            steps.wait()
            steps.add(v.tensor_scalar(X[:, i, :], X[:, i, :], MV[:, i, 0:1], RSTD[:, i, 0:1], ALU.subtract, ALU.mult))
            steps.wait()
            steps.add(v.tensor_tensor(X[:, i, :], X[:, i, :], LNG[:, :], ALU.mult))
            steps.wait()
            v.tensor_tensor(X[:, i, :], X[:, i, :], LNB[:, :], ALU.add).then_inc(ln_done, 1)
            v.wait_ge(ln_done, NT * n + i + 1)

        def mixer_residual(layer):
            for i in range(NT):
                for hf in range(2):
                    name = ("out", layer, i, hf)
                    computed(v, name)
                    x = X[:, i, hf * 512:hf * 512 + 512]
                    v.scalar_tensor_tensor(out=x, in0=x, scalar=ALPHA, in1=ps(name, TT, 0, 512), op0=ALU.mult, op1=ALU.add)\
                        .then_inc(bank_free[at[name][0]], 1)
                for hf in range(2):
                    moved(v, ("out", layer, i, hf))
                layer_norm(2 * layer, i)

        v.wait_ge(table_loaded, 16)
        v.wait_ge(iota_ready, 2)
        steps.add(v.tensor_copy(PTF[:, :], PTI[:, :]))
        steps.wait()
        steps.add(v.tensor_scalar(PTF[:, :], PTF[:, :], float(PAGE), IOP[:, 0:1], ALU.mult, ALU.add))
        steps.wait()
        v.tensor_copy(PIDX[:, :], PTF[:, :]).then_inc(page_rows_ready, 1)
        out_of(("small",), SMT[:, :, :].rearrange("p c r -> p (c r)"), ps(("small",), 128, 0, C * SMALL))
        moved(v, ("small",))
        steps.add(v.memset(REC[:, :, 0:CW - 1], 0.0))
        for m in range(C):
            steps.add(v.tensor_copy(REC[:, m, S0:RECW].rearrange("p (b t) -> p b t", b=DB)[:, :, 0:CW - 1],
                                    SMT[:, m, R_CS:R_CW].rearrange("p (b j) -> p b j", b=DB)))
        steps.add(v.tensor_copy(LSG[5][:, :], SMT[:, :, R_LAM]))
        steps.wait()
        log_sigmoid(LSG[5][:, :], [LSG[n][:, :] for n in range(5)], LSG[6][:, :], lam_in, lam_exp, lam_u, lam_ln)
        steps.add(v.tensor_scalar(POSS[:, :], LSG[6][:, :], -RG_C, None, ALU.mult))
        v.tensor_scalar(NEGS[:, :], LSG[6][:, :], RG_C, None, ALU.mult).then_inc(lam_scaled, 1)
        x_transposed(0)
        conv = padded(CONV)
        last = [0] * C
        for k in range(CW):
            for m in range(C):
                w = SMT[:, m, R_CW + k:R_CW + k + 1]
                if k == 0:
                    moved(v, ("rec", m))
                    last[m] = steps.add(v.tensor_scalar(conv[:, m, :], REC[:, m, 0:PADW], w, SMT[:, m, R_CB:R_CB + 1], ALU.mult, ALU.add))
                    continue
                steps.wait(last[m])
                ins = v.scalar_tensor_tensor(out=conv[:, m, :], in0=REC[:, m, k:k + PADW], scalar=w, in1=conv[:, m, :], op0=ALU.mult, op1=ALU.add)
                if k < CW - 1:
                    last[m] = steps.add(ins)
                else:
                    ins.then_inc(conv_done, 1)
        v.wait_ge(conv_done, C)
        a3, b3, h3 = padded(RA), padded(IB), padded(CONV)
        for m in range(C):
            moved(v, ("ix", m))
        n_ib = steps.add(v.tensor_tensor(IB[:, :], IB[:, :], CONV[:, :], ALU.mult))
        v.wait_ge(gates_ready, C)
        steps.wait(n_ib)
        steps.add(v.tensor_tensor(CONV[:, :], RA[:, :], RA[:, :], ALU.mult))
        steps.wait()
        v.scalar_tensor_tensor(out=CONV[:, :], in0=CONV[:, :], scalar=1.0, in1=TH[:, :], op0=ALU.add, op1=ALU.mult).then_inc(sq_in, 1)
        v.wait_ge(sq_ready, 1)
        steps.add(v.tensor_tensor(IB[:, :], IB[:, :], TH[:, :], ALU.mult))
        starts = a3[:, :, S0:S0 + (DB - 1) * SEQW + 1:SEQW]
        steps.wait()
        steps.add(v.tensor_tensor(SMT[:, :, 0:DB], SMT[:, :, 0:DB], starts, ALU.mult))
        steps.wait()
        b_starts = b3[:, :, S0:S0 + (DB - 1) * SEQW + 1:SEQW]
        steps.add(v.tensor_tensor(b_starts, b_starts, SMT[:, :, 0:DB], ALU.add))
        steps.add(v.memset(starts, 0.0))
        steps.add(v.memset(a3[:, :, 0:1], 0.0))
        steps.wait()
        steps.add(v.tensor_tensor_scan(CONV[:, :], RA[:, :], IB[:, :], 0.0, ALU.mult, ALU.add))
        steps.wait()
        steps.add(v.tensor_tensor(Y[:, :, NS:T], h3[:, :, 0:TP], GATE[:, :, NS:T], ALU.mult))
        for t in range(DS):
            cols = slice(S0 + t, S0 + t + (DB - 1) * SEQW + 1, SEQW)
            ins = v.tensor_tensor(Y[:, :, t:NS:DS], h3[:, :, cols], GATE[:, :, t:NS:DS], ALU.mult)
            if t < DS - 1:
                steps.add(ins)
        ins.then_inc(y_ready, 1)
        steps.add(v.tensor_copy(ST[:, :, 0:1], h3[:, :, TP - 1:TP]))
        steps.add(v.tensor_copy(ST[:, :, 1:1 + DB], h3[:, :, S0 + DS - 1:S0 + DS - 1 + (DB - 1) * SEQW + 1:SEQW]))
        steps.add(v.tensor_copy(ST[:, :, 1 + DB:DB + CW], REC[:, :, TP:TP + CW - 1]))
        for m in range(C):
            ins = v.tensor_copy(ST[:, m, DB + CW:NST].rearrange("p (b j) -> p b j", b=DB),
                                REC[:, m, S0:RECW].rearrange("p (b t) -> p b t", b=DB)[:, :, DS:SEQW])
            if m < C - 1:
                steps.add(ins)
        ins.then_inc(state_cols, 1)
        mixer_residual(0)

        def dots(tile, half, group, use, col):
            for k in range(HALF):
                slot = half * HALF + k
                v.wait_ge(row_in[slot], 16 * use + 16)
                v.tensor_tensor_reduce(out=RINGB[0:TT, slot, :], in0=RINGB[0:TT, slot, :], in1=X[:, tile, :], scale=1.0, scalar=0.0,
                                       op0=ALU.mult, op1=ALU.add, accum_out=ACC[:, group, k:k + 1]).then_inc(half_used[half], 1)
            v.wait_ge(half_used[half], HALF * use + HALF)
            v.tensor_copy(ACTV[:, bass.ds(col, HALF)], ACC[:, group, :]).then_inc(dots_kept, 1)

        def u_bodies(i, n, use, kept):
            with v.Fori(0, n) as j:
                for half in range(2):
                    dots(i, half, half, j + use, j * RING + half * HALF)
            v.wait_ge(dots_kept, kept + 2 * n)

        def uv_bodies(i, use, kept):
            with v.Fori(0, V_BODIES) as j:
                for s in range(2):
                    dots(i + 1, 0, s, 2 * j + (use + s), j * RING + (RING + s * HALF))
            v.wait_ge(dots_kept, kept + 2 * V_BODIES)

        def pick(layer, i):
            for j in range(4):
                moved(v, ("s", layer, i, j))

            def top16(vals, val16, idx16, count):
                for r in range(count):
                    steps.add(v.max(val16(r, 0), vals(r)))
                steps.wait()
                for r in range(count):
                    steps.add(v.max_index(idx16(r, 0), val16(r, 0), vals(r)))
                steps.wait()
                for r in range(count):
                    steps.add(v.match_replace(vals(r), val16(r, 0), vals(r), GONE))
                steps.wait()
                for r in range(count):
                    steps.add(v.max(val16(r, 1), vals(r)))
                steps.wait()
                for r in range(count):
                    steps.add(v.max_index(idx16(r, 1), val16(r, 1), vals(r)))
                steps.wait()

            top16(lambda r: S[:, i, r, :], lambda r, e: V16[:, r, 8 * e:8 * e + 8], lambda r, e: I16[:, r, 8 * e:8 * e + 8], 2 * PH)
            steps.add(v.tensor_copy(I16F[:, :, :], I16[:, :, :]))
            cand = CAND[:, :, :].rearrange("p h (a b) -> p h a b", a=TK)
            steps.add(v.tensor_tensor(cand, V16[:, 0:2 * PH:2, :].unsqueeze(3).to_broadcast([TT, PH, TK, TK]),
                                      V16[:, 1:2 * PH:2, :].unsqueeze(2).to_broadcast([TT, PH, TK, TK]), ALU.add))
            steps.wait()
            jj = J[:, :].rearrange("p (h k) -> p h k", h=PH)
            top16(lambda r: CAND[:, r, :], lambda r, e: SC[:, r, 8 * e:8 * e + 8], lambda r, e: jj[:, r, 8 * e:8 * e + 8], PH)
            v.tensor_tensor(SUBM[:, :, :], SC[:, :, :], SC[:, :, 0:1].to_broadcast([TT, PH, TK]), ALU.subtract).then_inc(sc_ready, 1)
            steps.add(v.tensor_scalar(JA[:, :], J[:, :], 4, None, ALU.logical_shift_right))
            steps.add(v.tensor_scalar(JB[:, :], J[:, :], 15, None, ALU.bitwise_and))
            steps.wait()
            steps.add(v.tensor_copy(JAF[:, :], JA[:, :]))
            steps.add(v.tensor_copy(JBF[:, :], JB[:, :]))
            steps.wait()
            iota = IOTA16[:, :].unsqueeze(1).to_broadcast([TT, PH * TK, TK])
            eq4 = EQ[:, :, :].rearrange("p (h k) a -> p h k a", h=PH)
            for half, jf, e in ((0, JAF, E1), (1, JBF, E2)):
                steps.add(v.tensor_tensor(EQ[:, :, :], jf[:, :].unsqueeze(2).to_broadcast([TT, PH * TK, TK]), iota, ALU.is_equal))
                steps.wait()
                steps.add(v.tensor_tensor(eq4, eq4, I16F[:, half:2 * PH:2, :].unsqueeze(2).to_broadcast([TT, PH, TK, TK]), ALU.mult))
                steps.wait()
                steps.add(v.tensor_reduce(out=e[:, :], in_=EQ[:, :, :], axis=AXX, op=ALU.add))
                steps.wait()
            steps.add(v.tensor_scalar(E1[:, :], E1[:, :], float(NK), float(layer * NE), ALU.mult, ALU.add))
            steps.wait()
            v.tensor_tensor(IDXF[:, i, :], E1[:, :], E2[:, :], ALU.add).then_inc(idxf_ready, 1)
            v.wait_ge(idxf_ready, layer * NT + i + 1)
            v.tensor_copy(IDX[:, i, :], IDXF[:, i, :]).then_inc(idx_ready, 1)
            v.wait_ge(exp_ready, layer * NT + i + 1)
            steps.add(v.tensor_reduce(out=GS[:, :], in_=G[:, i, :, :], axis=AXX, op=ALU.add))
            steps.wait()
            steps.add(v.reciprocal(GS[:, :], GS[:, :]))
            steps.wait()
            steps.add(v.tensor_tensor(G[:, i, :, :], G[:, i, :, :], GS[:, :].unsqueeze(2).to_broadcast([TT, PH, TK]), ALU.mult))
            steps.wait()

        def weigh(layer, i):
            v.wait_ge(act_ready, layer * NT + i + 1)
            if i:
                computed(v, ("wT", layer, i - 1))
            v.tensor_tensor(WN[:, :], GELU[:, :], G[:, i, :, :].rearrange("p h k -> p (h k)"), ALU.mult).then_inc(w_ready, 1)

        def expert_norm(layer, i):
            v.wait_ge(y_loaded, 16 * (layer * NT + i + 1))
            steps.add(v.scalar_tensor_tensor(out=X[:, i, :], in0=X[:, i, :], scalar=ALPHA, in1=YT[:, :], op0=ALU.mult, op1=ALU.add))
            steps.wait()
            layer_norm(2 * layer + 1, i)

        def experts(layer):
            x_transposed(2 * layer + 1)
            for j in range(4):
                half, h0 = j // 2, (j % 2) * 4
                out_of(("kt", layer, j), KT[:, half, h0:h0 + 4, :].rearrange("p h k -> p (h k)"), ps(("kt", layer, j), 128, 0, 512))
            v.memset(DG[:, :, :], 0.0).then_inc(diag_zero, 1)
            for m in range(1, 2 * PH, 2):
                out_of(("q", layer, m), QT[:, m, :], ps(("q", layer, m), 128, 0, T))
            for i in range(NT):
                for j in range(1, 4, 2):
                    name = ("s", layer, i, j)
                    out_of(name, S[:, i, 4 * j:4 * j + 4, :].rearrange("p m k -> p (m k)"), ps(name, TT, 0, 512))
            use = layer * USES_PER_LAYER
            kept = [layer * NT * 2 * U_BODIES]
            pick(layer, 0)
            pick(layer, 1)
            u_bodies(0, U_BODIES, use, kept[0])
            kept[0] += 2 * U_BODIES
            use += U_BODIES
            weigh(layer, 0)
            pick(layer, 2)
            for i in range(NT - 1):
                u_bodies(i + 1, 1, use, kept[0])
                kept[0] += 2
                use += 1
                uv_bodies(i, use, kept[0])
                kept[0] += 2 * V_BODIES
                use += 2 * V_BODIES
                weigh(layer, i + 1)
                expert_norm(layer, i)
            expert_norm(layer, NT - 1)

        experts(0)
        x_transposed(2)

        v.wait_ge(wff_loaded, 32)
        computed(v, ("f",))
        v.tensor_scalar(LF[4][:, :], ps(("f",), H, 0, T), BF[:, 0:1], None, ALU.add).then_inc(bank_free[at[("f",)][0]], 1)
        moved(v, ("f",))
        log_sigmoid(LF[4][:, :], [LF[n][:, :] for n in (0, 1, 2, 3, 5)], LF[6][:, :], f_in, f_exp, f_u, f_ln)
        v.sem_inc(f_ready, 1)
        for hf in range(2):
            for i in range(NT):
                out_of(("kn", i, hf), KNF[:, i, hf * 512:hf * 512 + 512], ps(("kn", i, hf), TT, 0, 512))
        for i in range(NT):
            for hf in range(2):
                out_of(("kf", i, hf), KF[:, 4 * hf:4 * hf + 4, i * TT:(i + 1) * TT],
                       ps(("kf", i, hf), 128, 0, 4 * TT).rearrange("p (c t) -> p c t", c=4))
        out_of(("lfT",), LFN[:, :, :].rearrange("p i h -> p (i h)"), ps(("lfT",), TT, 0, NT * H))
        for j in range(4):
            out_of(("lpT", j), LPX[:, 2 * j:2 * j + 2, 0:PAST], ps(("lpT", j), H, 0, 512).rearrange("p (b t) -> p b t", b=2))
        steps.add(v.tensor_copy(LPX[:, :, PAST:PAST + DS], LF[6][:, 0:NS].rearrange("p (b t) -> p b t", b=DB)))
        v.wait_ge(consts_ready, 1)
        for j in range(4):
            moved(v, ("lpT", j))
        steps.wait()
        for bb in range(DB):
            steps.add(v.tensor_tensor_scan(CS[:, bb, :], ONES[:, 0:PAST + DS], LPX[:, bb, :], 0.0, ALU.mult, ALU.add))
        steps.add(v.tensor_tensor_scan(CP[:, :], ONES[:, 0:TP], LF[6][:, NS:T], 0.0, ALU.mult, ALU.add))
        steps.wait()
        steps.add(v.tensor_copy(CSN[:, :].rearrange("p (b t) -> p b t", b=DB), CS[:, :, PAST:PAST + DS]))
        v.tensor_scalar(NCP[:, :], CP[:, :], -1.0, None, ALU.mult).then_inc(c_ready, 1)
        moved(v, ("lfT",))
        for i in range(NT):
            for hf in range(2):
                moved(v, ("kf", i, hf))
        for s in range(2):
            ins = v.tensor_copy(KC[:, s, :, PAST:NKEYS], KF[:, :, 0:NS])
            if s == 0:
                steps.add(ins)
        ins.then_inc(kc_new, 1)
        for n in range(len(ITEMS) + 2):
            if n >= 2:
                m = n - 2
                kind, x, t = ITEMS[m]
                if kind == "p":
                    out_of(("O", m), OT[:, x, QCOL[t]:QCOL[t] + QROWS[t]], ps(("O", m), 128, 0, QROWS[t]))
                else:
                    out_of(("O", m), OT[:, :, x * DS:(x + 1) * DS], ps(("O", m), 128, 0, NS).rearrange("p (h s) -> p h s", h=H))
            if n < len(ITEMS):
                kind, x, t = ITEMS[n]
                name = ("S", n)
                if kind == "s":
                    for j in (1, 3):
                        out_of(("kc", x, j), KC[:, x % 2, 4:8, (j // 2) * 128:(j // 2) * 128 + 128],
                               ps(("kc", x, j), 128, 0, 512).rearrange("p (h k) -> p h k", h=4))
                computed(v, name)
                if kind == "p":
                    nq, nk = QROWS[t], KEYS[t]
                    masked, mask, whole = ps(name, nq, nk - nq, nk), MASKC[0:nq, 0:nq], ps(name, nq, 0, nk)
                else:
                    nq = NS
                    masked, mask, whole = ps(name, NS, PAST, NKEYS), MASKS[:, x, :], ps(name, NS, 0, NKEYS)
                steps.add(v.tensor_tensor(masked, masked, mask, ALU.add))
                steps.wait()
                v.tensor_reduce(out=NMX[0:nq, n % 2:n % 2 + 1], in_=whole, axis=AXX, op=ALU.max, negate=True).then_inc(nmax_ready, 1)
            if 0 <= n - 1 < len(ITEMS):
                m = n - 1
                kind, x, t = ITEMS[m]
                nq = QROWS[t] if kind == "p" else NS
                moved(v, ("S", m))
                steps.add(v.reciprocal(RSUM[0:nq, m % 2:m % 2 + 1], SUMS[0:nq, m % 2:m % 2 + 1]))
                steps.wait()
                p = PP[0:nq, m % 2, NS:NS + KEYS[t]] if kind == "p" else PS[:, x % 2, :]
                v.tensor_scalar(p, p, RSUM[0:nq, m % 2:m % 2 + 1], None, ALU.mult).then_inc(probs_ready, 1)
        mixer_residual(1)
        experts(1)

    ctx.close()


INS = ["x_prompt", "x_sample", "cache_k", "cache_v", "cache_logf", "state_h", "state_conv", "page_table", "meta_tokens",
       "rg_w_in", "rg_conv_w", "rg_conv_b", "rg_w_a", "rg_b_a", "rg_w_x", "rg_b_x", "rg_lambda", "rg_w_out", "fox_w_in",
       "fox_b_f", "fox_w_o", "peer_w_q", "peer_keys1", "peer_keys2", "peer_u", "peer_v", "ln_mix_g", "ln_mix_b",
       "ln_ffn_g", "ln_ffn_b"]
OUTS = [("y_prompt", (1, SEQ, D)), ("y_sample", (DB, DS, D)), ("state_h_prompt", (1, 1, D)),
        ("state_conv_prompt", (1, 1, CW - 1, D)), ("k_prompt", (1, 1, TP, H, HD)), ("v_prompt", (1, 1, TP, H, HD)),
        ("logf_prompt", (1, 1, TP, H)), ("state_h_sample", (1, DB, D)), ("state_conv_sample", (1, DB, CW - 1, D)),
        ("k_sample", (1, DB, DS, H, HD)), ("v_sample", (1, DB, DS, H, HD)), ("logf_sample", (1, DB, DS, H))]


def kernel(**inputs):
    import concourse.bacc as bacc
    from concourse.bass_utils import run_bass_kernel_spmd

    nc = bacc.Bacc("TRN2", target_bir_lowering=False, num_devices=1)
    arrays = {name: np.ascontiguousarray(inputs[name]) for name in INS}
    a = {name: nc.dram_tensor(name, x.shape, mybir.dt.from_np(x.dtype), kind="ExternalInput").ap() for name, x in arrays.items()}
    o = {name: nc.dram_tensor("out_" + name, shape, F32, kind="ExternalOutput").ap() for name, shape in OUTS}
    trunk(nc, a, o)
    r = run_bass_kernel_spmd(nc, [arrays], core_ids=[0])
    return tuple(r.results[0]["out_" + name] for name, _ in OUTS)
```

```python
from contextlib import ExitStack

import numpy as np

import concourse.bass as bass
from concourse import mybir
from concourse.alu_op_type import AluOpType as ALU

F32, I32, U32 = mybir.dt.float32, mybir.dt.int32, mybir.dt.uint32
ACT = mybir.ActivationFunctionType
AXX = mybir.AxisListType.X

D = 1024
C = D // 128
DB, DS = 8, 8
NS = DB * DS
META, SEQ = 16, 256
TP = META + SEQ
T = NS + TP
TT, NT = 112, 3
P0 = TT - NS
CW = 4
RG_C = 8.0
H, HD = 8, 128
PAGE, PAGES = 128, 2
PAST = PAGE * PAGES
PH, TK, NK = 8, 16, 128
NE = NK * NK
SLOTS = PH * TK
DEPTH = 2
ALPHA = (2.0 * DEPTH) ** 0.25
SCALE = HD ** -0.5
EPS = 1e-5
LOW = -1e30
GONE = -3e38

SEQW = CW - 1 + DS
RECW = CW - 1 + TP + DB * SEQW
PADW = RECW - (CW - 1)
S0 = TP + CW - 1
SMALL = DB + DB * (CW - 1) + CW + 4
R_H, R_CS, R_CW = 0, DB, DB + DB * (CW - 1)
R_CB = R_CW + CW
R_BA, R_BX, R_LAM = R_CB + 1, R_CB + 2, R_CB + 3
NST = 1 + DB + (CW - 1) + DB * (CW - 1)

UNITS = PH // 2
PARTS = [(0, 1), (1, 2), (3, 2), (5, 2)]
HALF = 8
RING = 2 * HALF
U_BODIES = SLOTS // RING
V_BODIES = TT // RING
USES_PER_LAYER = U_BODIES + 2 * (1 + 2 * V_BODIES) + V_BODIES

QCOL = [NS, TT, 2 * TT]
QROWS = [P0, TT, TT]
KEYS = [P0, P0 + TT, P0 + 2 * TT]
NKEYS = PAST + NS
CSLOTS = 4
TLAG, OLAG = 2, 3
NP = 3
ITEMS = [("p", h, t) for h in range(H) for t in range(NT)] + [("s", b, 0) for b in range(DB)]


class Banks:

    def __init__(self):
        self.at, self.count, self.turn = {}, [0] * 8, 0

    def add(self, name, width):
        b = self.turn % width
        self.turn += 1
        self.at[name] = (b, self.count[b])
        self.count[b] += 1


def psum_plan():
    k = Banks()

    def xt(n, width):
        for i in range(NT):
            for hf in range(2):
                k.add(("xt", n, i, hf), width)

    def out(layer, tiles):
        for i in tiles:
            for hf in range(2):
                k.add(("out", layer, i, hf), 4)

    def peer(layer):
        for i in range(NT):
            for hf in range(2):
                k.add(("xt", 2 * layer + 1, i, hf), 4)
            if i == 0:
                for j in range(4):
                    k.add(("kt", layer, j), 4)
            for j in range(4):
                k.add(("q", layer, i, j), 4)
            for j in range(4):
                k.add(("s", layer, i, j), 4)
            if i == 0:
                out(layer, [NT - 1])
        for i in range(NT):
            k.add(("ixT", layer, i), 4)
            k.add(("wT", layer, i), 4)

    k.add(("small",), 8)
    xt(0, 8)
    for kind in ("rec", "gate"):
        for m in range(C):
            k.add((kind, m), 8)
    for m in range(C):
        k.add(("ra", m), 8)
        k.add(("ix", m), 8)
    for j in range(2):
        k.add(("st", j), 8)
    out(0, range(NT - 1))
    peer(0)
    xt(2, 4)
    k.add(("f",), 8)
    for m in range(C):
        k.add(("qf", m), 8)
    for kind in ("kn", "vn"):
        for hf in range(2):
            for i in range(NT):
                k.add((kind, i, hf), 8)
    for i in range(NT):
        for hf in range(2):
            k.add(("kf", i, hf), 8)
    k.add(("lfT",), 8)
    for j in range(4):
        k.add(("lpT", j), 8)
    for n in range(len(ITEMS) + OLAG):
        if n >= OLAG:
            k.add(("O", n - OLAG), 8)
        if n < len(ITEMS):
            if ITEMS[n][0] == "s":
                for j in range(4):
                    k.add(("kc", ITEMS[n][1], j), 8)
            k.add(("S", n), 8)
        if 0 <= n - TLAG < len(ITEMS):
            k.add(("T", n - TLAG), 8)
    out(1, range(NT - 1))
    peer(1)
    return k.at


class Chain:

    def __init__(self, eng, sem):
        self.eng, self.sem, self.n = eng, sem, 0

    def add(self, ins):
        ins.then_inc(self.sem, 1)
        self.n += 1
        return self.n

    def wait(self, n=None):
        self.eng.wait_ge(self.sem, self.n if n is None else n)


def trunk(nc, a, o):
    at = psum_plan()
    ctx = ExitStack()
    base = [(nc.sbuf_base + 31) // 32 * 32]

    def place(name, shape, dt=F32, cell=base):
        size = 4 * int(np.prod(shape[1:]))
        t = nc.alloc_sbuf_tensor_at(name, shape, dt, offset=cell[0])
        cell[0] += (size + 31) // 32 * 32
        return t

    X = place("x_nat", [TT, NT, D])
    XT = place("x_transposed", [128, C, T])
    Y = XT
    IDENT = place("ident", [128, 128])
    WFF = place("fox_w_f", [128, C, H])
    BF = place("b_f", [H, 1])
    LNG = place("ln_gain", [TT, D])
    LNB = place("ln_bias", [TT, D])
    IOTA16 = place("iota16", [TT, TK])
    PIDX = place("page_rows", [128, DB * PAGES], I32)
    PTI = place("page_table_all", [128, DB * PAGES], I32)
    PTF = place("page_table_f", [128, DB * PAGES])
    IOP = place("iota_partition", [128, 1])
    LPN = place("page_logf", [128, DB * PAGES, H])
    STATS = place("ln_stats", [TT, NT, 2, 6])
    MV = place("ln_mean_var", [TT, NT, 2])
    STD = place("ln_std", [TT, NT, 1])
    RSTD = place("ln_rstd", [TT, NT, 1])

    RA0 = base[0]
    RB0 = RA0 + 4 * 16 * D
    RC0 = RB0 + 4 * 16 * D

    WIN = place("rg_w_in", [128, C, 2 * D], cell=[RA0])
    WO = [place("rg_w_out", [128, C, D], cell=[RA0]), place("fox_w_o", [128, C, D], cell=[RB0])]
    b = [RB0]
    REC = place("rec", [128, C, RECW], cell=b)
    CONV = place("conv", [128, C * PADW], cell=b)
    RA = place("rg_a", [128, C * PADW], cell=b)
    IB = place("rg_i", [128, C * PADW], cell=b)
    TH = place("rg_th", [128, C * PADW], cell=b)
    SMN = place("small_nat", [SMALL, D], cell=b)
    SMT = place("small_t", [128, C, SMALL], cell=b)
    ST = place("state_t", [128, C, NST], cell=b)
    assert b[0] <= RC0
    c = [RC0]
    GATE = place("gate", [128, C, T], cell=c)
    WG = place("rg_gate_w", [128, 2, C, 128], cell=c)
    STN = place("state_nat", [NST, D], cell=c)
    LSG = [place(f"lam_{n}", [128, C], cell=c) for n in range(7)]
    NEGS = place("a_scale", [128, C], cell=c)
    POSS = place("a_scale_neg", [128, C], cell=c)
    cmax = c[0]

    RINGS, WQS, YOS, YTS = [], [], [], []
    for layer, (ring_at, wq_at) in enumerate(((RA0, RB0), (RB0, RA0))):
        RINGS.append(place(f"expert_rows{layer}", [128, RING, D], cell=[ring_at]))
        WQS.append(place(f"peer_w_q{layer}", [128, C, 2 * D], cell=[wq_at]))
        b = [wq_at]
        YOS.append(place(f"y_rows{layer}", [HALF, 2, D], cell=b))
        YTS.append(place(f"y_tile{layer}", [TT, D], cell=b))
    c = [RC0]
    QT = place("peer_q", [128, 2 * PH, TT], cell=c)
    KT = place("keys_t", [128, 2, PH, 128], cell=c)
    S = place("scores", [TT, 2, 2 * PH, NK], cell=c)
    KN = place("keys_nat", [128, 2, PH, 128], cell=[c[0] - 4 * 2 * PH * NK])
    CAND = place("cand", [TT, 2, TK * TK], cell=c)
    EQ = place("hit", [TT, 2 * TK, TK], cell=c)
    V16 = place("top_val", [TT, 4, TK], cell=c)
    I16 = place("top_idx", [TT, 4, TK], U32, cell=c)
    I16F = place("top_idx_f", [TT, 4, TK], cell=c)
    SC = place("pair_val", [TT, 2, TK], cell=c)
    J = place("pair_idx", [TT, 2 * TK], U32, cell=c)
    JA = place("pair_a", [TT, 2 * TK], U32, cell=c)
    JB = place("pair_b", [TT, 2 * TK], U32, cell=c)
    JAF = place("pair_a_f", [TT, 2 * TK], cell=c)
    JBF = place("pair_b_f", [TT, 2 * TK], cell=c)
    E1 = place("expert_hi", [TT, 2 * TK], cell=c)
    E2 = place("expert_lo", [TT, 2 * TK], cell=c)
    G = place("g", [TT, NT, PH, TK], cell=c)
    GS = place("g_sum", [TT, PH], cell=c)
    IDXF = place("idx_f", [TT, NT, SLOTS], cell=c)
    IDX = place("idx", [TT, NT, SLOTS], I32, cell=c)
    IDXT = place("idx_t", [128, NT, TT], I32, cell=c)
    ACTV = place("u_dot_x", [TT, SLOTS], cell=c)
    GELU = place("act", [TT, SLOTS], cell=c)
    WN = place("w_nat", [TT, SLOTS], cell=c)
    WT = place("w_t", [128, NT, TT], cell=c)
    DG = place("w_diag", [128, 2, HALF * HALF], cell=c)
    ACC = place("dots", [TT, 2, HALF], cell=c)
    STG = place("idx_stage", [128, 2, HALF], I32, cell=c)
    cmax = max(cmax, c[0])

    WF = place("fox_w_in", [128, 3, C, 512], cell=[RB0 + 4 * 3 * D])
    CACHE = place("cache_rows", [128, CSLOTS, 2, PAGES, D], cell=[RB0])
    b = [RA0]
    QF = place("q_t", [128, H, T], cell=b)
    KF = place("k_t", [128, H, T], cell=b)
    KNF = place("k_nat", [TT, NT, D], cell=b)
    VN = place("v_nat", [TT, NT, D], cell=b)
    PT = place("probs_t", [TT, 2, NT, TT], cell=b)
    PTS = place("probs_t_s", [128, 2, 3, NS], cell=b)
    LFN = place("logf_nat", [TT, NT, H], cell=b)
    QM = place("q_masked", [128, 2, H * (NS + 1)], cell=b)
    CS = place("c_sample", [H, DB, PAST + DS], cell=b)
    assert b[0] <= RB0
    c = [RC0]
    KC = place("cache_k_t", [128, 2, H, NKEYS], cell=c)
    PS = place("probs_s", [NS, NP, NKEYS], cell=c)
    PP = place("probs", [TT, NP, T], cell=c)
    ONES = place("ones", [H, NKEYS], cell=c)
    CP = place("c_prompt", [H, TP], cell=c)
    NCP = place("c_prompt_neg", [H, TP], cell=c)
    MASKC = place("causal", [TT, TT], cell=c)
    MASKS = place("causal_s", [NS, DB, NS], cell=c)
    CSN = place("c_new", [H, NS], cell=c)
    SEL = place("head_sel", [H, NS], cell=c)
    NSEL = place("head_sel_neg", [H, NS], cell=c)
    CQ = place("c_query", [H, DB, NS], cell=c)
    NMX = place("neg_max", [TT, NP], cell=c)
    SUMS = place("sums", [TT, NP], cell=c)
    RSUM = place("inv_sums", [TT, NP], cell=c)
    cmax = max(cmax, c[0])
    c = [RC0]
    LF = [place(f"logf_{n}", [H, T], cell=c) for n in range(7)]
    LPX = place("logf_sample", [H, DB, PAST + DS], cell=c)
    assert c[0] <= RC0 + 4 * 2 * H * NKEYS
    assert cmax <= nc.sbuf_usable_end, (cmax, nc.sbuf_usable_end)
    BANK = [ctx.enter_context(nc.psum_tensor(f"bank{n}", [128, 512], F32)) for n in range(4)]
    VB = [ctx.enter_context(nc.psum_tensor(f"banks_v{n}", [128, 2, 512], F32)) for n in range(2)]

    def sem(name):
        return ctx.enter_context(nc.semaphore(name))

    mm_done = [sem(f"mm_done{n}") for n in range(8)]
    bank_free = [sem(f"bank_free{n}") for n in range(8)]
    x_loaded, small_loaded, table_loaded = sem("x_loaded"), sem("small_loaded"), sem("table_loaded")
    win_loaded = [sem(f"win_loaded{n}") for n in range(4)]
    wg_loaded, wo_loaded, ln_loaded = sem("wg_loaded"), sem("wo_loaded"), sem("ln_loaded")
    wq_loaded = [sem(f"wq_loaded{n}") for n in range(4)]
    keys_loaded, wff_loaded = sem("keys_loaded"), sem("wff_loaded")
    wf_loaded = [sem(f"wf_loaded{n}") for n in range(6)]
    logf_loaded = sem("logf_loaded")
    cache_loaded = [[sem(f"cache_{kv}_loaded{n}") for n in range(CSLOTS)] for kv in "kv"]
    y_loaded = sem("y_loaded")
    ident_ready, iota_ready, consts_ready = sem("ident_ready"), sem("iota_ready"), sem("consts_ready")
    pool_steps, page_rows_ready = sem("pool_steps"), sem("page_rows_ready")
    dve_steps, act_steps = sem("dve_steps"), sem("act_steps")
    lam_in, lam_exp, lam_u, lam_ln, lam_scaled = (sem(x) for x in ("lam_in", "lam_exp", "lam_u", "lam_ln", "lam_scaled"))
    conv_done, gates_ready, sq_in, sq_ready, y_ready, state_cols = (
        sem(x) for x in ("conv_done", "gates_ready", "sq_in", "sq_ready", "y_ready", "state_cols"))
    var_ready, std_ready, ln_done = sem("var_ready"), sem("std_ready"), sem("ln_done")
    idxf_ready, idx_ready, sc_ready, exp_ready = (sem(x) for x in ("idxf_ready", "idx_ready", "sc_ready", "exp_ready"))
    staged, issue = sem("staged"), sem("issue")
    row_in = [sem(f"row_in{n}") for n in range(RING)]
    half_used = [sem("half_a_used"), sem("half_b_used")]
    dots_kept, act_ready, w_ready = sem("dots_kept"), sem("act_ready"), sem("w_ready")
    diag_zero, diag_ready, y_rows_ready = sem("diag_zero"), sem("diag_ready"), sem("y_rows_ready")
    y_written = [sem("y_written0"), sem("y_written1")]
    y_row_free = sem("y_row_free")
    f_in, f_exp, f_u, f_ln, f_ready, c_ready, kc_new = (
        sem(x) for x in ("f_in", "f_exp", "f_u", "f_ln", "f_ready", "c_ready", "kc_new"))
    cq_ready = sem("cq_ready")
    q_masked, nmax_ready, probs_exp, probs_ready = (
        sem(x) for x in ("q_masked", "nmax_ready", "probs_exp", "probs_ready"))
    stored = sem("stored")
    STORES = [0]

    y_dram = nc.dram_tensor("y_scratch", (T, D), F32, kind="Internal").ap()
    u_dram = a["peer_u"].rearrange("l e d -> (l e) d")
    v_dram = a["peer_v"].rearrange("l e d -> (l e) d")
    k_dram = a["cache_k"].rearrange("l n p h d -> (l n p) (h d)")
    cv_dram = a["cache_v"].rearrange("l n p h d -> (l n p) (h d)")
    cl_dram = a["cache_logf"].rearrange("l n p h -> (l n p) h")

    def bank(name):
        n = at[name][0]
        return BANK[n] if n < 4 else VB[(n - 4) // 2][:, (n - 4) % 2, :]

    def ps(name, rows, lo, hi):
        n = at[name][0]
        return BANK[n][0:rows, lo:hi] if n < 4 else VB[(n - 4) // 2][0:rows, (n - 4) % 2, lo:hi]

    def begin(pe, name):
        n, uses = at[name]
        if uses:
            pe.wait_ge(bank_free[n], uses)

    def computed(eng, name):
        n, uses = at[name]
        eng.wait_ge(mm_done[n], uses + 1)

    def moved(eng, name):
        n, uses = at[name]
        eng.wait_ge(bank_free[n], uses + 1)

    def padded(t):
        return t[:, :].rearrange("p (m t) -> p m t", m=C)

    block = ctx.enter_context(nc.Block())

    @block.sync
    def _(sp):
        def store(dst, src):
            sp.dma_start(dst, src).then_inc(stored, 16)
            STORES[0] += 16

        xs = a["x_sample"].rearrange("b s d -> (b s) d")
        xp = a["x_prompt"].rearrange("b s d -> (b s) d")
        n0 = P0 - META
        sp.dma_start(X[0:NS, 0, :], xs).then_inc(x_loaded, 16)
        sp.dma_start(X[NS:NS + META, 0, :], a["meta_tokens"]).then_inc(x_loaded, 16)
        sp.dma_start(X[NS + META:TT, 0, :], xp[0:n0, :]).then_inc(x_loaded, 16)
        for i in (1, 2):
            sp.dma_start(X[:, i, :], xp[n0 + (i - 1) * TT:n0 + i * TT, :]).then_inc(x_loaded, 16)
        for row, src in ((R_H, a["state_h"][0]), (R_CS, a["state_conv"][0].rearrange("b j d -> (b j) d")),
                         (R_CW, a["rg_conv_w"][0]), (R_CB, a["rg_conv_b"]), (R_BA, a["rg_b_a"]),
                         (R_BX, a["rg_b_x"]), (R_LAM, a["rg_lambda"])):
            sp.dma_start(SMN[row:row + src.shape[0], :], src).then_inc(small_loaded, 16)
        pt = a["page_table"].rearrange("b j -> (b j)")
        sp.dma_start(PTI[:, :], pt.partition_broadcast(128)).then_inc(table_loaded, 16)
        win = a["rg_w_in"][0].rearrange("(c p) n -> p c n", p=128)
        for blk in (2, 3, 0, 1):
            sp.dma_start(WIN[:, :, blk * 512:blk * 512 + 512], win[:, :, blk * 512:blk * 512 + 512]).then_inc(win_loaded[blk], 16)
        sp.dma_start(WG[:, 0, :, :], a["rg_w_a"][0].rearrange("n c d -> c n d")).then_inc(wg_loaded, 16)
        sp.dma_start(WG[:, 1, :, :], a["rg_w_x"][0].rearrange("n c d -> c n d")).then_inc(wg_loaded, 16)

        def load_ln(n, g, bb):
            if n:
                sp.wait_ge(ln_done, NT * n)
            sp.dma_start(LNG[:, :], g.partition_broadcast(TT)).then_inc(ln_loaded, 16)
            sp.dma_start(LNB[:, :], bb.partition_broadcast(TT)).then_inc(ln_loaded, 16)

        load_ln(0, a["ln_mix_g"][0], a["ln_mix_b"][0])
        computed(sp, ("gate", C - 1))
        sp.dma_start(WO[0][:, :, :], a["rg_w_out"][0].rearrange("(c p) n -> p c n", p=128)).then_inc(wo_loaded, 16)
        def load_wq(layer):
            wq = a["peer_w_q"][layer].rearrange("(c p) n -> p c n", p=128)
            for blk in range(4):
                sp.dma_start(WQS[layer][:, :, blk * 512:blk * 512 + 512], wq[:, :, blk * 512:blk * 512 + 512]).then_inc(wq_loaded[blk], 16)

        def load_keys(layer):
            for half, keys in enumerate((a["peer_keys1"], a["peer_keys2"])):
                sp.dma_start(KN[:, half, :, :], keys[layer].rearrange("h k c -> k h c")).then_inc(keys_loaded, 16)

        sp.wait_ge(y_ready, 1)
        computed(sp, ("st", 1))
        load_wq(0)
        for j in range(2):
            moved(sp, ("st", j))
        store(o["state_h_prompt"][0], STN[0:1, :])
        store(o["state_h_sample"][0], STN[1:1 + DB, :])
        store(o["state_conv_prompt"][0, 0], STN[1 + DB:DB + CW, :])
        store(o["state_conv_sample"][0].rearrange("b j d -> (b j) d"), STN[DB + CW:NST, :])
        sp.wait_ge(stored, STORES[0])
        load_keys(0)
        load_ln(1, a["ln_ffn_g"][0], a["ln_ffn_b"][0])

        wf = a["fox_w_in"][0].rearrange("(c p) n -> p c n", p=128)

        def load_wf(blk):
            sp.dma_start(WF[:, blk % 3, :, :], wf[:, :, blk * 512:blk * 512 + 512]).then_inc(wf_loaded[blk], 16)

        def y_rows(layer):
            for i in range(NT):
                if layer == 0 and i == NT - 1:
                    computed(sp, ("q", 0, NT - 1, 3))
                    sp.dma_start(WFF[:, :, :], wf[:, :, 3 * D:3 * D + H]).then_inc(wff_loaded, 16)
                    sp.dma_start(BF[:, :], a["fox_b_f"].rearrange("l h -> h l")).then_inc(wff_loaded, 16)
                    for blk in range(3):
                        load_wf(blk)
                first = (layer * NT + i) * V_BODIES
                with sp.Fori(0, V_BODIES) as j:
                    for s in range(2):
                        sp.wait_ge(y_rows_ready, 2 * j + (2 * first + s + 1))
                        sp.dma_start(y_dram[bass.ds(j * RING + (i * TT + s * HALF), HALF), :], YOS[layer][:, s, :]).then_inc(y_written[s], 16)
                    for s in range(2):
                        sp.wait_ge(y_written[s], 16 * j + 16 * (first + 1))
                        sp.sem_inc(y_row_free, 1)
                for s in range(2):
                    sp.wait_ge(y_written[s], 16 * (first + V_BODIES))
                done = NT * (2 * layer + 1) + i
                sp.wait_ge(ln_done, done)
                sp.dma_start(YTS[layer][:, :], y_dram[i * TT:(i + 1) * TT, :]).then_inc(y_loaded, 16)

        sp.sem_inc(y_row_free, 2)
        y_rows(0)

        for blk, name in ((3, ("qf", 3)), (4, ("qf", 7)), (5, ("kn", NT - 1, 0))):
            computed(sp, name)
            load_wf(blk)
        load_ln(2, a["ln_mix_g"][1], a["ln_mix_b"][1])
        rows = [(0, TT), (TT - NS, TT), (2 * TT - NS, TT)]
        for kind, buf, prompt, sample in (("kn", KNF, o["k_prompt"], o["k_sample"]), ("vn", VN, o["v_prompt"], o["v_sample"])):
            for i in range(NT):
                for hf in range(2):
                    moved(sp, (kind, i, hf))
            prompt = prompt.rearrange("l b t h d -> (l b t) (h d)")
            sample = sample.rearrange("l b t h d -> (l b t) (h d)")
            store(sample, buf[0:NS, 0, :])
            store(prompt[0:P0, :], buf[NS:TT, 0, :])
            for i in (1, 2):
                store(prompt[rows[i][0]:rows[i][0] + TT, :], buf[:, i, :])
        moved(sp, ("lfT",))
        lp = o["logf_prompt"].rearrange("l b t h -> (l b t) h")
        store(o["logf_sample"].rearrange("l b t h -> (l b t) h"), LFN[0:NS, 0, :])
        store(lp[0:P0, :], LFN[NS:TT, 0, :])
        for i in (1, 2):
            store(lp[rows[i][0]:rows[i][0] + TT, :], LFN[:, i, :])
        for bb in (4, 5):
            computed(sp, ("kc", bb, 3))
            computed(sp, ("O", H * NT + bb))
        sp.dma_start(WO[1][:, :, :], a["fox_w_o"][0].rearrange("(c p) n -> p c n", p=128)).then_inc(wo_loaded, 16)
        computed(sp, ("O", len(ITEMS) - 1))
        sp.wait_ge(stored, STORES[0])
        load_wq(1)
        load_keys(1)
        load_ln(3, a["ln_ffn_g"][1], a["ln_ffn_b"][1])
        y_rows(1)
        sp.wait_ge(ln_done, NT * 3 + 1)
        store(o["y_sample"].rearrange("b s d -> (b s) d"), X[0:NS, 0, :])
        yp = o["y_prompt"].rearrange("b s d -> (b s) d")
        store(yp[0:n0, :], X[NS + META:TT, 0, :])
        for i in (1, 2):
            sp.wait_ge(ln_done, NT * 3 + i + 1)
            store(yp[n0 + (i - 1) * TT:n0 + i * TT, :], X[:, i, :])
        sp.wait_ge(stored, STORES[0])

    @block.gpsimd
    def _(g):
        steps = Chain(g, pool_steps)
        steps.add(g.memset(IDENT[:, :], 0.0))
        steps.wait()
        g.affine_select(out=IDENT[:, :], in_=IDENT[:, :], compare_op=ALU.not_equal, fill=1.0,
                        base=0, pattern=[[-1, 128]], channel_multiplier=1).then_inc(ident_ready, 1)
        g.iota(IOP[:, :], pattern=[[0, 1]], base=0, channel_multiplier=1,
               allow_small_or_imprecise_dtypes=True).then_inc(iota_ready, 1)
        g.iota(IOTA16[:, :], pattern=[[1, TK]], base=0, channel_multiplier=0,
               allow_small_or_imprecise_dtypes=True).then_inc(iota_ready, 1)
        g.wait_ge(page_rows_ready, 1)
        for n in range(DB * PAGES):
            g.indirect_dma_start(out=LPN[:, n, :], out_offset=None, in_=cl_dram,
                                 in_offset=bass.IndirectOffsetOnAxis(ap=PIDX[:, n:n + 1], axis=0)).then_inc(logf_loaded, 16)

        def gather(ring, half, k, table, rows, stage):
            slot = half * HALF + k
            g.indirect_dma_start(out=ring[0:rows, slot, :], out_offset=None, in_=table,
                                 in_offset=bass.IndirectOffsetOnAxis(ap=STG[0:rows, stage, k:k + 1], axis=0)).then_inc(row_in[slot], 16)

        staged_n = [0]

        def half_ring(ring, half, use, idx_cols, rows, table, stage_count):
            g.wait_ge(half_used[half], HALF * use + HALF)
            g.tensor_copy(STG[0:rows, half, :], idx_cols).then_inc(staged, 1)
            g.wait_ge(staged, stage_count)
            g.sem_inc(issue, 1)
            for k in range(HALF):
                gather(ring, half, k, table, rows, half)

        def experts(layer):
            use = layer * USES_PER_LAYER

            def u_bodies(i, col, n, use):
                base_n = staged_n[0]
                with g.Fori(0, n) as j:
                    for half in range(2):
                        half_ring(RINGS[layer], half, j + use, IDX[:, i, bass.ds(j * RING + (col + half * HALF), HALF)], TT, u_dram,
                                  2 * j + (base_n + half + 1))
                staged_n[0] += 2 * n

            def uv_bodies(i, first, n, use):
                base_n = staged_n[0]
                with g.Fori(0, n) as j:
                    for s in range(2):
                        half_ring(RINGS[layer], 0, 2 * j + (use + s), IDX[:, i + 1, bass.ds(j * RING + ((first + 1) * RING + s * HALF), HALF)], TT, u_dram,
                                  4 * j + (base_n + 2 * s + 1))
                        half_ring(RINGS[layer], 1, 2 * j + (use + s), IDXT[:, i, bass.ds(j * RING + (first * RING + s * HALF), HALF)], 128, v_dram,
                                  4 * j + (base_n + 2 * s + 2))
                staged_n[0] += 4 * n

            def picked(i, unit):
                g.wait_ge(idx_ready, UNITS * (layer * NT + i) + unit + 1)

            for unit in range(UNITS):
                picked(0, unit)
                u_bodies(0, 2 * unit * RING, 2, use)
                use += 2
            for i in range(NT - 1):
                moved(g, ("ixT", layer, i))
                picked(i + 1, 0)
                u_bodies(i + 1, 0, 1, use)
                use += 1
                for unit, (first, n) in enumerate(PARTS):
                    picked(i + 1, unit)
                    uv_bodies(i, first, n, use)
                    use += 2 * n
            moved(g, ("ixT", layer, NT - 1))
            base_n = staged_n[0]
            with g.Fori(0, V_BODIES) as j:
                for s in range(2):
                    half_ring(RINGS[layer], s, j + use, IDXT[:, NT - 1, bass.ds(j * RING + s * HALF, HALF)], 128, v_dram,
                              2 * j + (base_n + s + 1))
            staged_n[0] += 2 * V_BODIES

        for half in range(2):
            g.sem_inc(half_used[half], HALF)
        computed(g, ("out", 0, NT - 1, 1))
        experts(0)

        g.wait_ge(ln_done, 2 * NT)
        steps.add(g.memset(MASKC[:, :], 0.0))
        steps.add(g.memset(MASKS[:, :, :], 0.0))
        steps.add(g.memset(SEL[:, :], 1.0))
        steps.add(g.memset(NSEL[:, :], -1.0))
        steps.add(g.memset(ONES[:, :], 1.0))
        steps.add(g.memset(QM[:, :, :], 0.0))
        steps.add(g.memset(PP[:, :, 0:NS], 0.0))
        steps.wait()
        steps.add(g.affine_select(out=MASKC[:, :], in_=MASKC[:, :], compare_op=ALU.is_ge, fill=LOW,
                                  base=0, pattern=[[-1, TT]], channel_multiplier=1))
        steps.add(g.affine_select(out=MASKS[:, :, :], in_=MASKS[:, :, :], compare_op=ALU.is_equal, fill=LOW,
                                  base=0, pattern=[[1, DB], [-1, DB], [0, DS]], channel_multiplier=0))
        steps.wait()
        steps.add(g.affine_select(out=MASKS[:, :, :], in_=MASKS[:, :, :], compare_op=ALU.is_ge, fill=LOW,
                                  base=0, pattern=[[0, DB], [0, DB], [-H, DS]], channel_multiplier=1))
        steps.add(g.affine_select(out=SEL[:, :], in_=SEL[:, :], compare_op=ALU.is_equal, fill=0.0,
                                  base=0, pattern=[[0, DS], [-1, H]], channel_multiplier=1))
        steps.add(g.affine_select(out=NSEL[:, :], in_=NSEL[:, :], compare_op=ALU.is_equal, fill=0.0,
                                  base=0, pattern=[[0, DS], [-1, H]], channel_multiplier=1))
        steps.wait()
        g.sem_inc(consts_ready, 1)

        def pages(bb):
            if bb < CSLOTS:
                computed(g, (("kn", NT - 1, 1), ("vn", NT - 1, 0), ("vn", NT - 1, 1), ("vn", NT - 1, 1))[bb])
            for kv, src in enumerate((k_dram, cv_dram)):
                if bb >= CSLOTS:
                    computed(g, ("O", H * NT + bb - CSLOTS) if kv else ("kc", bb - CSLOTS, 3))
                for pg in range(PAGES):
                    n = bb * PAGES + pg
                    g.indirect_dma_start(out=CACHE[:, bb % CSLOTS, kv, pg, :], out_offset=None, in_=src,
                                         in_offset=bass.IndirectOffsetOnAxis(ap=PIDX[:, n:n + 1], axis=0)).then_inc(cache_loaded[kv][bb % CSLOTS], 16)

        for bb in range(CSLOTS):
            pages(bb)
        g.wait_ge(c_ready, 1)
        for bb in range(DB):
            ins = g.tensor_tensor(CQ[:, bb, :].rearrange("p (s h) -> p s h", h=H), SEL[:, :].rearrange("p (s h) -> p s h", h=H),
                                  CS[:, bb, PAST:PAST + DS].unsqueeze(2).to_broadcast([H, DS, H]), ALU.mult)
        ins.then_inc(cq_ready, 1)
        for bb in range(CSLOTS, DB):
            pages(bb)
        computed(g, ("out", 1, NT - 1, 1))
        experts(1)

    @block.tensor
    def _(pe):
        def done(name, ins):
            ins.then_inc(mm_done[at[name][0]], 1)

        def transposes(name, pieces):
            begin(pe, name)
            for rows, col, src in pieces:
                k = src.shape[0]
                last = pe.transpose(ps(name, rows, col, col + k), src, IDENT[0:k, 0:k])
            done(name, last)

        def x_transposes(n, tiles=range(NT)):
            for i in tiles:
                if n:
                    pe.wait_ge(ln_done, NT * (n - 1) + i + 1)
                for hf in range(2):
                    transposes(("xt", n, i, hf), [(128, q * TT, X[:, i, (4 * hf + q) * 128:(4 * hf + q + 1) * 128]) for q in range(4)])

        def product(name, rows, pairs, lo=0):
            begin(pe, name)
            pairs = list(pairs)
            for n, (lhsT, rhs) in enumerate(pairs):
                last = pe.matmul(ps(name, rows, lo, lo + rhs.shape[-1]), lhsT=lhsT, rhs=rhs, start=n == 0, stop=n == len(pairs) - 1)
            done(name, last)

        def x_transposed(n, tiles=range(NT)):
            for i in tiles:
                for hf in range(2):
                    moved(pe, ("xt", n, i, hf))

        def mixer_out(layer, tiles):
            pe.wait_ge(wo_loaded, 16 * (layer + 1))
            for i in tiles:
                for hf in range(2):
                    product(("out", layer, i, hf), TT, [(Y[:, c, i * TT:(i + 1) * TT], WO[layer][:, c, hf * 512:hf * 512 + 512]) for c in range(C)])

        pe.wait_ge(ident_ready, 1)
        pe.wait_ge(small_loaded, 16 * 7)
        transposes(("small",), [(128, c * SMALL, SMN[:, c * 128:c * 128 + 128]) for c in range(C)])
        pe.wait_ge(x_loaded, 16 * 5)
        x_transposes(0)
        x_transposed(0)
        for kind, first in (("rec", C), ("gate", 0)):
            for m in range(C):
                col = first + m
                pe.wait_ge(win_loaded[col // 4], 16)
                product((kind, m), 128, [(WIN[:, c, col * 128:col * 128 + 128], XT[:, c, :]) for c in range(C)])
        pe.wait_ge(wg_loaded, 32)
        for m in range(C):
            pe.wait_ge(conv_done, m + 1)
            for w, kind in enumerate(("ra", "ix")):
                product((kind, m), 128, [(WG[:, w, m, :], CONV[:, m * PADW:(m + 1) * PADW])])
        pe.wait_ge(state_cols, 1)
        for j in range(2):
            transposes(("st", j), [(NST, q * 128, ST[:, 4 * j + q, :]) for q in range(4)])
        pe.wait_ge(y_ready, 1)
        mixer_out(0, range(NT - 1))

        def v_loop(layer, i, use, halves, step):
            first = (layer * NT + i) * V_BODIES
            with pe.Fori(0, V_BODIES) as j:
                for s in range(2):
                    half = halves[s]
                    use_s = step * j + (use + (s if step == 2 else 0))
                    pe.wait_ge(diag_ready, 2 * j + (2 * first + s + 1))
                    for k in range(HALF):
                        pe.wait_ge(row_in[half * HALF + k], 16 * use_s + 16)
                        for hf in range(2):
                            last = pe.matmul(VB[s][0:HALF, hf, :], lhsT=DG[:, s, k * HALF:(k + 1) * HALF],
                                             rhs=RINGS[layer][:, half * HALF + k, hf * 512:hf * 512 + 512], start=k == 0, stop=k == HALF - 1)
                        last.then_inc(half_used[half], 1)

        def experts(layer):
            n = 2 * layer + 1
            for i in range(NT):
                x_transposes(n, [i])
                if i == 0:
                    pe.wait_ge(keys_loaded, 32 * (layer + 1))
                    for j in range(4):
                        half, h0 = j // 2, (j % 2) * 4
                        transposes(("kt", layer, j), [(128, q * 128, KN[:, half, h0 + q, :]) for q in range(4)])
                x_transposed(n, [i])
                for j in range(4):
                    name = ("q", layer, i, j)
                    pe.wait_ge(wq_loaded[j], 16 * (layer + 1))
                    begin(pe, name)
                    for q in range(4):
                        m = 4 * j + q
                        for c in range(C):
                            last = pe.matmul(ps(name, 128, q * TT, (q + 1) * TT), lhsT=WQS[layer][:, c, m * 128:m * 128 + 128],
                                             rhs=XT[:, c, i * TT:(i + 1) * TT], start=c == 0, stop=c == C - 1)
                    done(name, last)
                for j in range(4):
                    moved(pe, ("kt", layer, j))
                for j in range(4):
                    name = ("s", layer, i, j)
                    begin(pe, name)
                    moved(pe, ("q", layer, i, j))
                    for q in range(4):
                        m = 4 * j + q
                        last = pe.matmul(ps(name, TT, q * 128, q * 128 + 128), lhsT=QT[:, m, :],
                                         rhs=KT[:, m % 2, m // 2, :], start=True, stop=True)
                    done(name, last)
                if i == 0:
                    mixer_out(layer, [NT - 1])

            def index_columns(i):
                pe.wait_ge(idxf_ready, UNITS * (layer * NT + i + 1))
                transposes(("ixT", layer, i), [(128, 0, IDXF[:, i, :])])

            def weight_columns(i):
                pe.wait_ge(w_ready, layer * NT + i + 1)
                transposes(("wT", layer, i), [(128, 0, WN[:, :])])

            use = layer * USES_PER_LAYER + U_BODIES
            index_columns(0)
            weight_columns(0)
            v_loop(layer, 0, use + 1, (1, 1), 2)
            use += 1 + 2 * V_BODIES
            index_columns(1)
            weight_columns(1)
            v_loop(layer, 1, use + 1, (1, 1), 2)
            use += 1 + 2 * V_BODIES
            index_columns(2)
            weight_columns(2)
            v_loop(layer, 2, use, (0, 1), 1)

        experts(0)
        x_transposes(2)

        pe.wait_ge(y_rows_ready, 2 * NT * V_BODIES)
        x_transposed(2)
        pe.wait_ge(wff_loaded, 32)
        product(("f",), H, [(WFF[:, c, :], XT[:, c, :]) for c in range(C)])
        for m in range(H):
            pe.wait_ge(wf_loaded[m // 4], 16)
            product(("qf", m), 128, [(WF[:, m // 4, c, (m % 4) * 128:(m % 4) * 128 + 128], XT[:, c, :]) for c in range(C)])
        for n, kind in enumerate(("kn", "vn")):
            for hf in range(2):
                blk = 2 + 2 * n + hf
                pe.wait_ge(wf_loaded[blk], 16)
                for i in range(NT):
                    product((kind, i, hf), TT, [(XT[:, c, i * TT:(i + 1) * TT], WF[:, blk % 3, c, :]) for c in range(C)])
        for i in range(NT):
            for hf in range(2):
                moved(pe, ("kn", i, hf))
                transposes(("kf", i, hf), [(128, q * TT, KNF[:, i, (4 * hf + q) * 128:(4 * hf + q + 1) * 128]) for q in range(4)])
        pe.wait_ge(f_ready, 1)
        transposes(("lfT",), [(TT, i * H, LF[6][:, i * TT:(i + 1) * TT]) for i in range(NT)])
        pe.wait_ge(logf_loaded, 16 * DB * PAGES)
        for j in range(4):
            transposes(("lpT", j), [(H, q * 128, LPN[:, 4 * j + q, :]) for q in range(4)])
        for i in range(NT):
            for hf in range(2):
                moved(pe, ("kf", i, hf))
                moved(pe, ("vn", i, hf))
        for m in range(H):
            moved(pe, ("qf", m))
        pe.wait_ge(c_ready, 1)
        pe.wait_ge(consts_ready, 1)
        pe.wait_ge(ident_ready, 1)

        def scores(n):
            kind, x, t = ITEMS[n]
            name = ("S", n)
            if kind == "p":
                nq, nk, q0 = QROWS[t], KEYS[t], QCOL[t]
                pick = IDENT[0:H, x:x + 1]
                product(name, nq, [(QF[:, x, q0:q0 + nq], KF[:, x, NS:NS + nk]),
                                   (CP[:, q0 - NS:q0 - NS + nq], pick.to_broadcast([H, nk])),
                                   (pick.to_broadcast([H, nq]), NCP[:, 0:nk])])
                return
            for j in range(4):
                moved(pe, ("kc", x, j))
            pe.wait_ge(cq_ready, 1)
            pe.wait_ge(q_masked, x + 1)
            pe.wait_ge(kc_new, 1)
            begin(pe, name)
            pe.matmul(ps(name, NS, 0, NKEYS), lhsT=CQ[:, x, :], rhs=ONES[:, :], start=True, stop=False)
            pe.matmul(ps(name, NS, 0, PAST), lhsT=NSEL[:, :], rhs=CS[:, x, 0:PAST], start=False, stop=False)
            pe.matmul(ps(name, NS, PAST, NKEYS), lhsT=NSEL[:, :], rhs=CSN[:, :], start=False, stop=False)
            for h in range(H):
                last = pe.matmul(ps(name, NS, 0, NKEYS), lhsT=QM[:, x % 2, h * NS:(h + 1) * NS], rhs=KC[:, x % 2, h, :],
                                 start=False, stop=h == H - 1)
            done(name, last)

        def probs_t(n):
            kind, x, t = ITEMS[n]
            pe.wait_ge(probs_ready, n + 1)
            if kind == "p":
                nq = QROWS[t]
                transposes(("T", n), [(TT, j * TT, PP[0:nq, n % NP, j * TT:(j + 1) * TT]) for j in range(t + 1)])
            else:
                transposes(("T", n), [(128, 0, PS[:, n % NP, 0:128]), (128, NS, PS[:, n % NP, 128:256]), (NS, 2 * NS, PS[:, n % NP, 256:NKEYS])])

        def attend(n):
            kind, x, t = ITEMS[n]
            moved(pe, ("T", n))
            if kind == "p":
                nq = QROWS[t]
                product(("O", n), 128, [(VN[:, j, x * 128:(x + 1) * 128], PT[:, n % 2, j, 0:nq]) for j in range(t + 1)])
                return
            name = ("O", n)
            begin(pe, name)
            pe.wait_ge(cache_loaded[1][x % CSLOTS], 16 * PAGES * (x // CSLOTS + 1))
            for h in range(H):
                cols = slice(h * 128, h * 128 + 128)
                for j in range(3):
                    lhsT = CACHE[:, x % CSLOTS, 1, j, cols] if j < 2 else VN[0:NS, 0, cols]
                    k = 128 if j < 2 else NS
                    last = pe.matmul(ps(name, 128, h * DS, (h + 1) * DS), lhsT=lhsT, rhs=PTS[0:k, n % 2, j, h:NS:H], start=j == 0, stop=j == 2)
            done(name, last)

        for n in range(len(ITEMS) + OLAG):
            if n >= OLAG:
                attend(n - OLAG)
            if n < len(ITEMS):
                kind, x, _ = ITEMS[n]
                if kind == "s":
                    pe.wait_ge(cache_loaded[0][x % CSLOTS], 16 * PAGES * (x // CSLOTS + 1))
                    for j in range(4):
                        pg, h0 = j // 2, (j % 2) * 4
                        transposes(("kc", x, j), [(128, q * 128, CACHE[:, x % CSLOTS, 0, pg, (h0 + q) * 128:(h0 + q + 1) * 128]) for q in range(4)])
                scores(n)
            if 0 <= n - TLAG < len(ITEMS):
                probs_t(n - TLAG)
        for n in range(len(ITEMS) - 8, len(ITEMS)):
            moved(pe, ("O", n))
        mixer_out(1, range(NT - 1))
        experts(1)

    @block.scalar
    def _(act):
        steps = Chain(act, act_steps)

        def out_of(name, dst, src):
            computed(act, name)
            act.copy(dst, src).then_inc(bank_free[at[name][0]], 1)

        def x_transposed(n):
            for i in range(NT):
                out_of(("xt", n, i, 0), XT[:, 0:4, i * TT:(i + 1) * TT], ps(("xt", n, i, 0), 128, 0, 4 * TT).rearrange("p (c t) -> p c t", c=4))

        def std(n, i):
            act.wait_ge(var_ready, NT * n + i + 1)
            act.activation(STD[:, i, :], MV[:, i, 1:2], ACT.Sqrt).then_inc(std_ready, 1)

        act.wait_ge(lam_in, 1)
        act.activation(LSG[1][:, :], LSG[0][:, :], ACT.Exp).then_inc(lam_exp, 1)
        act.wait_ge(lam_u, 1)
        act.activation(LSG[3][:, :], LSG[2][:, :], ACT.Ln).then_inc(lam_ln, 1)
        x_transposed(0)
        for m in range(C):
            computed(act, ("rec", m))
            name = ("rec", m)
            act.copy(REC[:, m, CW - 1:CW - 1 + TP], ps(name, 128, NS, T))
            act.copy(REC[:, m, S0:RECW].rearrange("p (b t) -> p b t", b=DB)[:, :, CW - 1:SEQW],
                     ps(name, 128, 0, NS).rearrange("p (b t) -> p b t", b=DB)).then_inc(bank_free[at[name][0]], 1)
        for m in range(C):
            name = ("gate", m)
            computed(act, name)
            act.activation(GATE[:, m, :], ps(name, 128, 0, T), ACT.Gelu_apprx_tanh).then_inc(bank_free[at[name][0]], 1)
        moved(act, ("small",))
        for m in range(C):
            for kind, row, dst in (("ra", R_BA, RA), ("ix", R_BX, IB)):
                name = (kind, m)
                computed(act, name)
                act.activation(dst[:, m * PADW:(m + 1) * PADW], ps(name, 128, 0, PADW), ACT.Sigmoid,
                               bias=SMT[:, m, row:row + 1]).then_inc(bank_free[at[name][0]], 1)
        act.wait_ge(lam_scaled, 1)
        for m in range(C):
            moved(act, ("ra", m))
            act.activation(TH[:, m * PADW:(m + 1) * PADW], RA[:, m * PADW:(m + 1) * PADW], ACT.Tanh, scale=POSS[:, m:m + 1])
            act.activation(RA[:, m * PADW:(m + 1) * PADW], RA[:, m * PADW:(m + 1) * PADW], ACT.Exp, scale=NEGS[:, m:m + 1]).then_inc(gates_ready, 1)
        act.wait_ge(sq_in, 1)
        act.activation(TH[:, :], CONV[:, :], ACT.Sqrt).then_inc(sq_ready, 1)
        for j in range(2):
            out_of(("st", j), STN[:, j * 512:(j + 1) * 512], ps(("st", j), NST, 0, 512))
        for i in range(NT - 1):
            std(0, i)

        def v_side(layer, i, use, halves, step):
            first = (layer * NT + i) * V_BODIES
            moved(act, ("wT", layer, i))
            with act.Fori(0, V_BODIES) as j:
                for s in range(2):
                    act.copy(DG[:, s, 0:HALF * HALF:HALF + 1], WT[:, i, bass.ds(j * RING + s * HALF, HALF)]).then_inc(diag_ready, 1)
                for s in range(2):
                    use_s = step * j + (use + (s if step == 2 else 0))
                    act.wait_ge(half_used[halves[s]], HALF * use_s + 2 * HALF)
                    act.wait_ge(y_row_free, 2 * j + (2 * first + s + 1))
                    act.copy(YOS[layer][:, s, :].rearrange("p (a d) -> p a d", a=2), VB[s][0:HALF, :, :]).then_inc(y_rows_ready, 1)

        def experts(layer):
            for i in range(NT):
                for hf in range(2):
                    name = ("xt", 2 * layer + 1, i, hf)
                    out_of(name, XT[:, 4 * hf:4 * hf + 4, i * TT:(i + 1) * TT], ps(name, 128, 0, 4 * TT).rearrange("p (c t) -> p c t", c=4))
                for j in range(4):
                    name = ("q", layer, i, j)
                    out_of(name, QT[:, 4 * j:4 * j + 4, :].rearrange("p m t -> p (m t)"), ps(name, 128, 0, 4 * TT))
                if i == 2:
                    act.wait_ge(idx_ready, UNITS * (layer * NT + 1))
                for j in range(4):
                    name = ("s", layer, i, j)
                    out_of(name, S[:, i % 2, 4 * j:4 * j + 4, :].rearrange("p m k -> p (m k)"), ps(name, TT, 0, 512))
                if i == 0:
                    std(2 * layer, NT - 1)

            def g_exp(i):
                act.wait_ge(sc_ready, layer * NT + i + 1)
                act.activation(G[:, i, :, :], G[:, i, :, :], ACT.Exp).then_inc(exp_ready, 1)

            def index_columns(i):
                out_of(("ixT", layer, i), IDXT[:, i, :], ps(("ixT", layer, i), 128, 0, TT))

            def weights(i):
                act.wait_ge(dots_kept, 2 * U_BODIES * (layer * NT + i + 1))
                act.activation(GELU[:, :], ACTV[:, :], ACT.Gelu_apprx_tanh).then_inc(act_ready, 1)
                out_of(("wT", layer, i), WT[:, i, :], ps(("wT", layer, i), 128, 0, TT))

            n = 2 * layer + 1
            use = layer * USES_PER_LAYER + U_BODIES
            act.wait_ge(diag_zero, layer + 1)
            index_columns(0)
            g_exp(0)
            weights(0)
            v_side(layer, 0, use + 1, (1, 1), 2)
            use += 1 + 2 * V_BODIES
            index_columns(1)
            g_exp(1)
            weights(1)
            std(n, 0)
            v_side(layer, 1, use + 1, (1, 1), 2)
            use += 1 + 2 * V_BODIES
            index_columns(2)
            g_exp(2)
            weights(2)
            std(n, 1)
            v_side(layer, 2, use, (0, 1), 1)
            std(n, 2)

        experts(0)
        x_transposed(2)

        act.wait_ge(f_in, 1)
        act.activation(LF[1][:, :], LF[0][:, :], ACT.Exp).then_inc(f_exp, 1)
        act.wait_ge(f_u, 1)
        act.activation(LF[3][:, :], LF[2][:, :], ACT.Ln).then_inc(f_ln, 1)
        for m in range(H):
            name = ("qf", m)
            computed(act, name)
            act.mul(QF[:, m, :], ps(name, 128, 0, T), SCALE).then_inc(bank_free[at[name][0]], 1)
        for hf in range(2):
            for i in range(NT):
                out_of(("vn", i, hf), VN[:, i, hf * 512:hf * 512 + 512], ps(("vn", i, hf), TT, 0, 512))
        for m in range(H):
            moved(act, ("qf", m))
        act.wait_ge(consts_ready, 1)
        for n in range(len(ITEMS) + TLAG):
            if n < len(ITEMS):
                kind, x, t = ITEMS[n]
                if kind == "s":
                    if x >= 2:
                        computed(act, ("S", n - 2))
                    act.copy(QM[:, x % 2, :].rearrange("p (h x) -> p h x", h=H)[:, :, 0:NS:H],
                             QF[:, :, x * DS:(x + 1) * DS]).then_inc(q_masked, 1)
                    for j in (0, 2):
                        out_of(("kc", x, j), KC[:, x % 2, 0:4, (j // 2) * 128:(j // 2) * 128 + 128],
                               ps(("kc", x, j), 128, 0, 512).rearrange("p (h k) -> p h k", h=4))
                act.wait_ge(nmax_ready, n + 1)
                name = ("S", n)
                if kind == "p":
                    nq, nk = QROWS[t], KEYS[t]
                    dst, src = PP[0:nq, n % NP, NS:NS + nk], ps(name, nq, 0, nk)
                else:
                    nq = NS
                    dst, src = PS[:, n % NP, :], ps(name, NS, 0, NKEYS)
                act.activation(dst, src, ACT.Exp, bias=NMX[0:nq, n % NP:n % NP + 1], accum_out=SUMS[0:nq, n % NP:n % NP + 1]).then_inc(bank_free[at[name][0]], 1)
            if n >= TLAG:
                m = n - TLAG
                kind, x, t = ITEMS[m]
                name = ("T", m)
                computed(act, name)
                if kind == "p":
                    nq = QROWS[t]
                    act.copy(PT[:, m % 2, 0:t + 1, 0:nq], ps(name, TT, 0, (t + 1) * TT).rearrange("p (j q) -> p j q", q=TT)[:, :, 0:nq])\
                        .then_inc(bank_free[at[name][0]], 1)
                else:
                    act.copy(PTS[:, m % 2, 0:2, :], ps(name, 128, 0, 2 * NS).rearrange("p (j q) -> p j q", q=NS))
                    act.copy(PTS[0:NS, m % 2, 2, :], ps(name, NS, 2 * NS, 3 * NS)).then_inc(bank_free[at[name][0]], 1)
        for i in range(NT - 1):
            std(2, i)
        experts(1)

    @block.vector
    def _(v):
        steps = Chain(v, dve_steps)

        def out_of(name, dst, src):
            computed(v, name)
            v.tensor_copy(dst, src).then_inc(bank_free[at[name][0]], 1)

        def x_transposed(n):
            for i in range(NT):
                out_of(("xt", n, i, 1), XT[:, 4:8, i * TT:(i + 1) * TT], ps(("xt", n, i, 1), 128, 0, 4 * TT).rearrange("p (c t) -> p c t", c=4))

        def log_sigmoid(z, t, into, sent_in, got_exp, sent_u, got_ln):
            v.scalar_tensor_tensor(out=t[0], in0=z, scalar=-1.0, in1=z, op0=ALU.mult, op1=ALU.min).then_inc(sent_in, 1)
            v.wait_ge(got_exp, 1)
            v.tensor_scalar(t[2], t[1], 1.0, None, ALU.add).then_inc(sent_u, 1)
            v.wait_ge(sent_u, 1)
            steps.add(v.tensor_scalar(t[0], t[2], 1.0, None, ALU.subtract))
            steps.wait()
            steps.add(v.tensor_tensor(t[0], t[1], t[0], ALU.subtract))
            steps.add(v.reciprocal(t[4], t[2]))
            steps.wait()
            steps.add(v.tensor_tensor(t[0], t[0], t[4], ALU.mult))
            v.wait_ge(got_ln, 1)
            steps.wait()
            steps.add(v.tensor_tensor(t[0], t[0], t[3], ALU.add))
            steps.wait()
            steps.add(v.scalar_tensor_tensor(out=into, in0=z, scalar=0.0, in1=t[0], op0=ALU.min, op1=ALU.subtract))
            steps.wait()

        def layer_norm(n, i):
            v.wait_ge(ln_loaded, 32 * (n + 1))
            for hf in range(2):
                k = steps.add(v.bn_stats(STATS[:, i, hf, :], X[:, i, hf * 512:hf * 512 + 512]))
            steps.wait()
            steps.add(v.bn_aggr(MV[:, i, :], STATS[:, i, :, :].rearrange("p a b -> p (a b)")))
            steps.wait()
            v.tensor_scalar(MV[:, i, 1:2], MV[:, i, 1:2], EPS, None, ALU.add).then_inc(var_ready, 1)
            v.wait_ge(std_ready, NT * n + i + 1)
            steps.add(v.reciprocal(RSTD[:, i, :], STD[:, i, :]))
            steps.wait()
            steps.add(v.tensor_scalar(X[:, i, :], X[:, i, :], MV[:, i, 0:1], RSTD[:, i, 0:1], ALU.subtract, ALU.mult))
            steps.wait()
            steps.add(v.tensor_tensor(X[:, i, :], X[:, i, :], LNG[:, :], ALU.mult))
            steps.wait()
            v.tensor_tensor(X[:, i, :], X[:, i, :], LNB[:, :], ALU.add).then_inc(ln_done, 1)
            v.wait_ge(ln_done, NT * n + i + 1)

        def mixer_residual(layer, tiles):
            for i in tiles:
                for hf in range(2):
                    name = ("out", layer, i, hf)
                    computed(v, name)
                    x = X[:, i, hf * 512:hf * 512 + 512]
                    v.scalar_tensor_tensor(out=x, in0=x, scalar=ALPHA, in1=ps(name, TT, 0, 512), op0=ALU.mult, op1=ALU.add)\
                        .then_inc(bank_free[at[name][0]], 1)
                for hf in range(2):
                    moved(v, ("out", layer, i, hf))
                layer_norm(2 * layer, i)

        v.wait_ge(table_loaded, 16)
        v.wait_ge(iota_ready, 2)
        steps.add(v.tensor_copy(PTF[:, :], PTI[:, :]))
        steps.wait()
        steps.add(v.tensor_scalar(PTF[:, :], PTF[:, :], float(PAGE), IOP[:, 0:1], ALU.mult, ALU.add))
        steps.wait()
        v.tensor_copy(PIDX[:, :], PTF[:, :]).then_inc(page_rows_ready, 1)
        out_of(("small",), SMT[:, :, :].rearrange("p c r -> p (c r)"), ps(("small",), 128, 0, C * SMALL))
        moved(v, ("small",))
        steps.add(v.memset(REC[:, :, 0:CW - 1], 0.0))
        for m in range(C):
            steps.add(v.tensor_copy(REC[:, m, S0:RECW].rearrange("p (b t) -> p b t", b=DB)[:, :, 0:CW - 1],
                                    SMT[:, m, R_CS:R_CW].rearrange("p (b j) -> p b j", b=DB)))
        steps.add(v.tensor_copy(LSG[5][:, :], SMT[:, :, R_LAM]))
        steps.wait()
        log_sigmoid(LSG[5][:, :], [LSG[n][:, :] for n in range(5)], LSG[6][:, :], lam_in, lam_exp, lam_u, lam_ln)
        steps.add(v.tensor_scalar(POSS[:, :], LSG[6][:, :], -RG_C, None, ALU.mult))
        v.tensor_scalar(NEGS[:, :], LSG[6][:, :], RG_C, None, ALU.mult).then_inc(lam_scaled, 1)
        x_transposed(0)
        conv = padded(CONV)
        last = [0] * C
        for k in range(CW):
            for m in range(C):
                w = SMT[:, m, R_CW + k:R_CW + k + 1]
                if k == 0:
                    moved(v, ("rec", m))
                    last[m] = steps.add(v.tensor_scalar(conv[:, m, :], REC[:, m, 0:PADW], w, SMT[:, m, R_CB:R_CB + 1], ALU.mult, ALU.add))
                    continue
                steps.wait(last[m])
                ins = v.scalar_tensor_tensor(out=conv[:, m, :], in0=REC[:, m, k:k + PADW], scalar=w, in1=conv[:, m, :], op0=ALU.mult, op1=ALU.add)
                if k < CW - 1:
                    last[m] = steps.add(ins)
                else:
                    ins.then_inc(conv_done, 1)
        v.wait_ge(conv_done, C)
        a3, b3, h3 = padded(RA), padded(IB), padded(CONV)
        for m in range(C):
            moved(v, ("ix", m))
        n_ib = steps.add(v.tensor_tensor(IB[:, :], IB[:, :], CONV[:, :], ALU.mult))
        v.wait_ge(gates_ready, C)
        steps.wait(n_ib)
        steps.add(v.tensor_tensor(CONV[:, :], RA[:, :], RA[:, :], ALU.mult))
        steps.wait()
        v.scalar_tensor_tensor(out=CONV[:, :], in0=CONV[:, :], scalar=1.0, in1=TH[:, :], op0=ALU.add, op1=ALU.mult).then_inc(sq_in, 1)
        v.wait_ge(sq_ready, 1)
        steps.add(v.tensor_tensor(IB[:, :], IB[:, :], TH[:, :], ALU.mult))
        starts = a3[:, :, S0:S0 + (DB - 1) * SEQW + 1:SEQW]
        steps.wait()
        steps.add(v.tensor_tensor(SMT[:, :, 0:DB], SMT[:, :, 0:DB], starts, ALU.mult))
        steps.wait()
        b_starts = b3[:, :, S0:S0 + (DB - 1) * SEQW + 1:SEQW]
        steps.add(v.tensor_tensor(b_starts, b_starts, SMT[:, :, 0:DB], ALU.add))
        steps.add(v.memset(starts, 0.0))
        steps.add(v.memset(a3[:, :, 0:1], 0.0))
        steps.wait()
        steps.add(v.tensor_tensor_scan(CONV[:, :], RA[:, :], IB[:, :], 0.0, ALU.mult, ALU.add))
        steps.wait()
        steps.add(v.tensor_tensor(Y[:, :, NS:T], h3[:, :, 0:TP], GATE[:, :, NS:T], ALU.mult))
        for t in range(DS):
            cols = slice(S0 + t, S0 + t + (DB - 1) * SEQW + 1, SEQW)
            ins = v.tensor_tensor(Y[:, :, t:NS:DS], h3[:, :, cols], GATE[:, :, t:NS:DS], ALU.mult)
            if t < DS - 1:
                steps.add(ins)
        ins.then_inc(y_ready, 1)
        steps.add(v.tensor_copy(ST[:, :, 0:1], h3[:, :, TP - 1:TP]))
        steps.add(v.tensor_copy(ST[:, :, 1:1 + DB], h3[:, :, S0 + DS - 1:S0 + DS - 1 + (DB - 1) * SEQW + 1:SEQW]))
        steps.add(v.tensor_copy(ST[:, :, 1 + DB:DB + CW], REC[:, :, TP:TP + CW - 1]))
        for m in range(C):
            ins = v.tensor_copy(ST[:, m, DB + CW:NST].rearrange("p (b j) -> p b j", b=DB),
                                REC[:, m, S0:RECW].rearrange("p (b t) -> p b t", b=DB)[:, :, DS:SEQW])
            if m < C - 1:
                steps.add(ins)
        ins.then_inc(state_cols, 1)
        mixer_residual(0, range(NT - 1))

        def dots(ring, tile, half, group, use, col):
            for k in range(HALF):
                slot = half * HALF + k
                v.wait_ge(row_in[slot], 16 * use + 16)
                v.tensor_tensor_reduce(out=ring[0:TT, slot, :], in0=ring[0:TT, slot, :], in1=X[:, tile, :], scale=1.0, scalar=0.0,
                                       op0=ALU.mult, op1=ALU.add, accum_out=ACC[:, group, k:k + 1]).then_inc(half_used[half], 1)
            v.wait_ge(half_used[half], HALF * use + 2 * HALF)
            v.tensor_copy(ACTV[:, bass.ds(col, HALF)], ACC[:, group, :]).then_inc(dots_kept, 1)

        def u_bodies(ring, i, col, n, use, kept):
            with v.Fori(0, n) as j:
                for half in range(2):
                    dots(ring, i, half, half, j + use, j * RING + (col + half * HALF))
            v.wait_ge(dots_kept, kept + 2 * n)

        def uv_bodies(ring, i, first, n, use, kept):
            with v.Fori(0, n) as j:
                for s in range(2):
                    dots(ring, i + 1, 0, s, 2 * j + (use + s), j * RING + ((first + 1) * RING + s * HALF))
            v.wait_ge(dots_kept, kept + 2 * n)

        def pick(layer, i, unit):
            moved(v, ("s", layer, i, unit))

            def top16(vals, val16, idx16, count):
                rows = range(count)
                at1 = [steps.add(v.max(val16(r, 0), vals(r))) for r in rows]
                at2 = []
                for r in rows:
                    steps.wait(at1[r])
                    at2.append(steps.add(v.max_index(idx16(r, 0), val16(r, 0), vals(r))))
                at3 = []
                for r in rows:
                    steps.wait(at2[r])
                    at3.append(steps.add(v.match_replace(vals(r), val16(r, 0), vals(r), GONE)))
                at4 = []
                for r in rows:
                    steps.wait(at3[r])
                    at4.append(steps.add(v.max(val16(r, 1), vals(r))))
                for r in rows:
                    steps.wait(at4[r])
                    steps.add(v.max_index(idx16(r, 1), val16(r, 1), vals(r)))

            top16(lambda r: S[:, i % 2, 4 * unit + r, :], lambda r, e: V16[:, r, 8 * e:8 * e + 8], lambda r, e: I16[:, r, 8 * e:8 * e + 8], 4)
            cand = CAND[:, :, :].rearrange("p h (a b) -> p h a b", a=TK)
            steps.wait()
            steps.add(v.tensor_tensor(cand, V16[:, 0:4:2, :].unsqueeze(3).to_broadcast([TT, 2, TK, TK]),
                                      V16[:, 1:4:2, :].unsqueeze(2).to_broadcast([TT, 2, TK, TK]), ALU.add))
            steps.add(v.tensor_copy(I16F[:, :, :], I16[:, :, :]))
            steps.wait()
            jj = J[:, :].rearrange("p (h k) -> p h k", h=2)
            top16(lambda r: CAND[:, r, :], lambda r, e: SC[:, r, 8 * e:8 * e + 8], lambda r, e: jj[:, r, 8 * e:8 * e + 8], 2)
            steps.wait()
            steps.add(v.tensor_scalar(JA[:, :], J[:, :], 4, None, ALU.logical_shift_right))
            steps.add(v.tensor_scalar(JB[:, :], J[:, :], 15, None, ALU.bitwise_and))
            ins = v.tensor_tensor(G[:, i, 2 * unit:2 * unit + 2, :], SC[:, :, :], SC[:, :, 0:1].to_broadcast([TT, 2, TK]), ALU.subtract)
            if unit == UNITS - 1:
                ins.then_inc(sc_ready, 1)
            else:
                steps.add(ins)
            steps.wait()
            steps.add(v.tensor_copy(JAF[:, :], JA[:, :]))
            steps.add(v.tensor_copy(JBF[:, :], JB[:, :]))
            steps.wait()
            iota = IOTA16[:, :].unsqueeze(1).to_broadcast([TT, 2 * TK, TK])
            eq4 = EQ[:, :, :].rearrange("p (h k) a -> p h k a", h=2)
            for half, jf, e in ((0, JAF, E1), (1, JBF, E2)):
                steps.add(v.tensor_tensor(EQ[:, :, :], jf[:, :].unsqueeze(2).to_broadcast([TT, 2 * TK, TK]), iota, ALU.is_equal))
                steps.wait()
                steps.add(v.tensor_tensor(eq4, eq4, I16F[:, half:4:2, :].unsqueeze(2).to_broadcast([TT, 2, TK, TK]), ALU.mult))
                steps.wait()
                steps.add(v.tensor_reduce(out=e[:, :], in_=EQ[:, :, :], axis=AXX, op=ALU.add))
                steps.wait()
            steps.add(v.tensor_scalar(E1[:, :], E1[:, :], float(NK), float(layer * NE), ALU.mult, ALU.add))
            steps.wait()
            cols = slice(2 * unit * TK, 2 * (unit + 1) * TK)
            v.tensor_tensor(IDXF[:, i, cols], E1[:, :], E2[:, :], ALU.add).then_inc(idxf_ready, 1)
            v.wait_ge(idxf_ready, UNITS * (layer * NT + i) + unit + 1)
            v.tensor_copy(IDX[:, i, cols], IDXF[:, i, cols]).then_inc(idx_ready, 1)

        def weigh(layer, i):
            v.wait_ge(exp_ready, layer * NT + i + 1)
            steps.add(v.tensor_reduce(out=GS[:, :], in_=G[:, i, :, :], axis=AXX, op=ALU.add))
            steps.wait()
            steps.add(v.reciprocal(GS[:, :], GS[:, :]))
            steps.wait()
            steps.add(v.tensor_tensor(G[:, i, :, :], G[:, i, :, :], GS[:, :].unsqueeze(2).to_broadcast([TT, PH, TK]), ALU.mult))
            steps.wait()
            v.wait_ge(act_ready, layer * NT + i + 1)
            if i:
                computed(v, ("wT", layer, i - 1))
            v.tensor_tensor(WN[:, :], GELU[:, :], G[:, i, :, :].rearrange("p h k -> p (h k)"), ALU.mult).then_inc(w_ready, 1)

        def expert_norm(layer, i):
            v.wait_ge(y_loaded, 16 * (layer * NT + i + 1))
            steps.add(v.scalar_tensor_tensor(out=X[:, i, :], in0=X[:, i, :], scalar=ALPHA, in1=YTS[layer][:, :], op0=ALU.mult, op1=ALU.add))
            steps.wait()
            layer_norm(2 * layer + 1, i)

        def experts(layer):
            for j in range(4):
                half, h0 = j // 2, (j % 2) * 4
                out_of(("kt", layer, j), KT[:, half, h0:h0 + 4, :].rearrange("p h k -> p (h k)"), ps(("kt", layer, j), 128, 0, 512))
            v.memset(DG[:, :, :], 0.0).then_inc(diag_zero, 1)
            ring = RINGS[layer]
            use = layer * USES_PER_LAYER
            kept = layer * NT * 2 * U_BODIES
            pick(layer, 0, 0)
            mixer_residual(layer, [NT - 1])
            for unit in range(1, UNITS):
                pick(layer, 0, unit)
            for unit in range(UNITS):
                u_bodies(ring, 0, 2 * unit * RING, 2, use, kept)
                kept += 4
                use += 2
                if unit % 2:
                    pick(layer, 1, unit // 2)
            for i in range(NT - 1):
                weigh(layer, i)
                if i:
                    expert_norm(layer, i - 1)
                u_bodies(ring, i + 1, 0, 1, use, kept)
                kept += 2
                use += 1
                for unit, (first, n) in enumerate(PARTS):
                    uv_bodies(ring, i, first, n, use, kept)
                    kept += 2 * n
                    use += 2 * n
                    if unit < 2:
                        pick(layer, i + 1, unit + 2)
                    elif i + 2 < NT:
                        pick(layer, i + 2, unit - 2)
            weigh(layer, NT - 1)
            expert_norm(layer, NT - 2)
            expert_norm(layer, NT - 1)

        experts(0)
        x_transposed(2)

        v.wait_ge(wff_loaded, 32)
        computed(v, ("f",))
        v.tensor_scalar(LF[4][:, :], ps(("f",), H, 0, T), BF[:, 0:1], None, ALU.add).then_inc(bank_free[at[("f",)][0]], 1)
        moved(v, ("f",))
        log_sigmoid(LF[4][:, :], [LF[n][:, :] for n in (0, 1, 2, 3, 5)], LF[6][:, :], f_in, f_exp, f_u, f_ln)
        v.sem_inc(f_ready, 1)
        for hf in range(2):
            for i in range(NT):
                out_of(("kn", i, hf), KNF[:, i, hf * 512:hf * 512 + 512], ps(("kn", i, hf), TT, 0, 512))
        for i in range(NT):
            for hf in range(2):
                out_of(("kf", i, hf), KF[:, 4 * hf:4 * hf + 4, i * TT:(i + 1) * TT],
                       ps(("kf", i, hf), 128, 0, 4 * TT).rearrange("p (c t) -> p c t", c=4))
        out_of(("lfT",), LFN[:, :, :].rearrange("p i h -> p (i h)"), ps(("lfT",), TT, 0, NT * H))
        for j in range(4):
            out_of(("lpT", j), LPX[:, 2 * j:2 * j + 2, 0:PAST], ps(("lpT", j), H, 0, 512).rearrange("p (b t) -> p b t", b=2))
        steps.add(v.tensor_copy(LPX[:, :, PAST:PAST + DS], LF[6][:, 0:NS].rearrange("p (b t) -> p b t", b=DB)))
        v.wait_ge(consts_ready, 1)
        for j in range(4):
            moved(v, ("lpT", j))
        steps.wait()
        for bb in range(DB):
            steps.add(v.tensor_tensor_scan(CS[:, bb, :], ONES[:, 0:PAST + DS], LPX[:, bb, :], 0.0, ALU.mult, ALU.add))
        steps.add(v.tensor_tensor_scan(CP[:, :], ONES[:, 0:TP], LF[6][:, NS:T], 0.0, ALU.mult, ALU.add))
        steps.wait()
        steps.add(v.tensor_copy(CSN[:, :].rearrange("p (b t) -> p b t", b=DB), CS[:, :, PAST:PAST + DS]))
        v.tensor_scalar(NCP[:, :], CP[:, :], -1.0, None, ALU.mult).then_inc(c_ready, 1)
        moved(v, ("lfT",))
        for i in range(NT):
            for hf in range(2):
                moved(v, ("kf", i, hf))
        for s in range(2):
            ins = v.tensor_copy(KC[:, s, :, PAST:NKEYS], KF[:, :, 0:NS])
            if s == 0:
                steps.add(ins)
        ins.then_inc(kc_new, 1)
        for n in range(len(ITEMS) + OLAG):
            if n >= OLAG:
                m = n - OLAG
                kind, x, t = ITEMS[m]
                if kind == "p":
                    out_of(("O", m), Y[:, x, QCOL[t]:QCOL[t] + QROWS[t]], ps(("O", m), 128, 0, QROWS[t]))
                else:
                    out_of(("O", m), Y[:, :, x * DS:(x + 1) * DS], ps(("O", m), 128, 0, NS).rearrange("p (h s) -> p h s", h=H))
            if n < len(ITEMS):
                kind, x, t = ITEMS[n]
                name = ("S", n)
                if kind == "s":
                    for j in (1, 3):
                        out_of(("kc", x, j), KC[:, x % 2, 4:8, (j // 2) * 128:(j // 2) * 128 + 128],
                               ps(("kc", x, j), 128, 0, 512).rearrange("p (h k) -> p h k", h=4))
                computed(v, name)
                if kind == "p":
                    nq, nk = QROWS[t], KEYS[t]
                    masked, mask, whole = ps(name, nq, nk - nq, nk), MASKC[0:nq, 0:nq], ps(name, nq, 0, nk)
                else:
                    nq = NS
                    masked, mask, whole = ps(name, NS, PAST, NKEYS), MASKS[:, x, :], ps(name, NS, 0, NKEYS)
                steps.add(v.tensor_tensor(masked, masked, mask, ALU.add))
                steps.wait()
                v.tensor_reduce(out=NMX[0:nq, n % NP:n % NP + 1], in_=whole, axis=AXX, op=ALU.max, negate=True).then_inc(nmax_ready, 1)
            if 0 <= n - 1 < len(ITEMS):
                m = n - 1
                kind, x, t = ITEMS[m]
                nq = QROWS[t] if kind == "p" else NS
                moved(v, ("S", m))
                steps.add(v.reciprocal(RSUM[0:nq, m % NP:m % NP + 1], SUMS[0:nq, m % NP:m % NP + 1]))
                steps.wait()
                p = PP[0:nq, m % NP, NS:NS + KEYS[t]] if kind == "p" else PS[:, m % NP, :]
                v.tensor_scalar(p, p, RSUM[0:nq, m % NP:m % NP + 1], None, ALU.mult).then_inc(probs_ready, 1)
        mixer_residual(1, range(NT - 1))
        experts(1)

    ctx.close()


INS = ["x_prompt", "x_sample", "cache_k", "cache_v", "cache_logf", "state_h", "state_conv", "page_table", "meta_tokens",
       "rg_w_in", "rg_conv_w", "rg_conv_b", "rg_w_a", "rg_b_a", "rg_w_x", "rg_b_x", "rg_lambda", "rg_w_out", "fox_w_in",
       "fox_b_f", "fox_w_o", "peer_w_q", "peer_keys1", "peer_keys2", "peer_u", "peer_v", "ln_mix_g", "ln_mix_b",
       "ln_ffn_g", "ln_ffn_b"]
OUTS = [("y_prompt", (1, SEQ, D)), ("y_sample", (DB, DS, D)), ("state_h_prompt", (1, 1, D)),
        ("state_conv_prompt", (1, 1, CW - 1, D)), ("k_prompt", (1, 1, TP, H, HD)), ("v_prompt", (1, 1, TP, H, HD)),
        ("logf_prompt", (1, 1, TP, H)), ("state_h_sample", (1, DB, D)), ("state_conv_sample", (1, DB, CW - 1, D)),
        ("k_sample", (1, DB, DS, H, HD)), ("v_sample", (1, DB, DS, H, HD)), ("logf_sample", (1, DB, DS, H))]


def kernel(**inputs):
    import concourse.bacc as bacc
    from concourse.bass_utils import run_bass_kernel_spmd

    nc = bacc.Bacc("TRN2", target_bir_lowering=False, num_devices=1)
    arrays = {name: np.ascontiguousarray(inputs[name]) for name in INS}
    a = {name: nc.dram_tensor(name, x.shape, mybir.dt.from_np(x.dtype), kind="ExternalInput").ap() for name, x in arrays.items()}
    o = {name: nc.dram_tensor("out_" + name, shape, F32, kind="ExternalOutput").ap() for name, shape in OUTS}
    trunk(nc, a, o)
    r = run_bass_kernel_spmd(nc, [arrays], core_ids=[0])
    return tuple(r.results[0]["out_" + name] for name, _ in OUTS)
```

```python
from contextlib import ExitStack

import numpy as np

import concourse.bass as bass
from concourse import mybir
from concourse.alu_op_type import AluOpType as ALU

F32, I32, U32 = mybir.dt.float32, mybir.dt.int32, mybir.dt.uint32
ACT = mybir.ActivationFunctionType
AXX = mybir.AxisListType.X

D = 1024
C = D // 128
DB, DS = 8, 8
NS = DB * DS
META, SEQ = 16, 256
TP = META + SEQ
T = NS + TP
TT, NT = 112, 3
P0 = TT - NS
CW = 4
RG_C = 8.0
H, HD = 8, 128
PAGE, PAGES = 128, 2
PAST = PAGE * PAGES
PH, TK, NK = 8, 16, 128
NE = NK * NK
SLOTS = PH * TK
DEPTH = 2
ALPHA = (2.0 * DEPTH) ** 0.25
SCALE = HD ** -0.5
EPS = 1e-5
LOW = -1e30
GONE = -3e38

SEQW = CW - 1 + DS
RECW = CW - 1 + TP + DB * SEQW
PADW = RECW - (CW - 1)
S0 = TP + CW - 1
SMALL = DB + DB * (CW - 1) + CW + 4
R_H, R_CS, R_CW = 0, DB, DB + DB * (CW - 1)
R_CB = R_CW + CW
R_BA, R_BX, R_LAM = R_CB + 1, R_CB + 2, R_CB + 3
NST = 1 + DB + (CW - 1) + DB * (CW - 1)

EARLY_GATES = 3

UNITS = PH // 2
UCOLS = SLOTS // UNITS
ALL = NT * UNITS
HALF = 8
RING = 2 * HALF
PER_UNIT = UCOLS // HALF
LONE = PER_UNIT // 2
V_PARTS = (ALL - 1) * PER_UNIT + LONE
USES_PER_LAYER = LONE + V_PARTS

NORM_AT = [UNITS + 2, 2 * UNITS + 2]

QCOL = [NS, TT, 2 * TT]
QROWS = [P0, TT, TT]
KEYS = [P0, P0 + TT, P0 + 2 * TT]
NKEYS = PAST + NS
CSLOTS = 4
TLAG, OLAG = 2, 4
NP = 3
ITEMS = [item for n in range(H) for item in (("s", n, 0), ("p", n, 0), ("p", n, 1), ("p", n, 2))]
SAMPLE = [ITEMS.index(("s", b, 0)) for b in range(DB)]
WF_BLOCKS = [2, 3, 0, 1, 4, 5]


class Banks:

    def __init__(self):
        self.at, self.count, self.turn = {}, [0] * 8, 0

    def add(self, name, width):
        b = self.turn % width
        self.turn += 1
        self.at[name] = (b, self.count[b])
        self.count[b] += 1


def psum_plan():
    k = Banks()

    def xt(n, width, tiles=range(NT)):
        for i in tiles:
            for hf in range(2):
                k.add(("xt", n, i, hf), width)

    def out(layer, tiles):
        for i in tiles:
            for hf in range(2):
                k.add(("out", layer, i, hf), 4)

    def peer(layer):
        for i in range(NT):
            for hf in range(2):
                k.add(("xt", 2 * layer + 1, i, hf), 4)
            if i == 0:
                for j in range(4):
                    k.add(("kt", layer, j), 4)
            for j in range(4):
                k.add(("q", layer, i, j), 4)
                k.add(("s", layer, i, j), 4)
                if i == 0 and j == 1:
                    out(layer, [NT - 1])

    k.add(("small",), 8)
    xt(0, 8)
    for m in range(C):
        k.add(("rec", m), 8)
    for m in range(EARLY_GATES):
        k.add(("gate", m), 8)
    for m in range(C):
        k.add(("ra", m), 8)
        k.add(("ix", m), 8)
    for m in range(EARLY_GATES, C):
        k.add(("gate", m), 8)
    for j in range(2):
        k.add(("st", j), 8)
    out(0, range(NT - 1))
    peer(0)
    xt(2, 4, range(NT - 1))
    k.turn = 0
    for hf in range(2):
        for i in range(NT - 1):
            k.add(("kn", i, hf), 8)
    xt(2, 8, [NT - 1])
    k.add(("f",), 8)
    for hf in range(2):
        k.add(("kn", NT - 1, hf), 8)
    for m in range(C):
        k.add(("qf", m), 8)
    for hf in range(2):
        for i in range(NT):
            k.add(("vn", i, hf), 8)
    for i in range(NT):
        for hf in range(2):
            k.add(("kf", i, hf), 8)
    k.add(("lfT",), 8)
    for j in range(4):
        k.add(("lpT", j), 8)
    for n in range(-1, len(ITEMS) + OLAG):
        if n >= OLAG:
            k.add(("O", n - OLAG), 8)
        if 0 <= n < len(ITEMS):
            k.add(("S", n), 8)
        if 0 <= n - TLAG < len(ITEMS):
            k.add(("T", n - TLAG), 8)
        if n + 1 in SAMPLE:
            for j in range(4):
                k.add(("kc", SAMPLE.index(n + 1), j), 8)
    out(1, range(NT - 1))
    peer(1)
    return k.at


class Chain:

    def __init__(self, eng, sem):
        self.eng, self.sem, self.n = eng, sem, 0

    def add(self, ins):
        ins.then_inc(self.sem, 1)
        self.n += 1
        return self.n

    def wait(self, n=None):
        self.eng.wait_ge(self.sem, self.n if n is None else n)


def trunk(nc, a, o):
    at = psum_plan()
    ctx = ExitStack()
    base = [(nc.sbuf_base + 31) // 32 * 32]

    def place(name, shape, dt=F32, cell=base):
        size = 4 * int(np.prod(shape[1:]))
        t = nc.alloc_sbuf_tensor_at(name, shape, dt, offset=cell[0])
        cell[0] += (size + 31) // 32 * 32
        return t

    X = place("x_nat", [TT, NT, D])
    XT = place("x_transposed", [128, C, T])
    Y = XT
    IDENT = place("ident", [128, 128])
    WFF = place("fox_w_f", [128, C, H])
    BF = place("b_f", [H, 1])
    LNG = place("ln_gain", [TT, D])
    LNB = place("ln_bias", [TT, D])
    IOTA16 = place("iota16", [TT, TK])
    PIDX = place("page_rows", [128, DB * PAGES], I32)
    PTI = place("page_table_all", [128, DB * PAGES], I32)
    PTF = place("page_table_f", [128, DB * PAGES])
    IOP = place("iota_partition", [128, 1])
    LPN = place("page_logf", [128, DB * PAGES, H])
    STATS = place("ln_stats", [TT, NT, 2, 6])
    MV = place("ln_mean_var", [TT, NT, 2])
    STD = place("ln_std", [TT, NT, 1])
    RSTD = place("ln_rstd", [TT, NT, 1])

    RA0 = base[0]
    RB0 = RA0 + 4 * 16 * D
    RC0 = RB0 + 4 * 16 * D

    WIN = place("rg_w_in", [128, C, 2 * D], cell=[RA0])
    WO = [place("rg_w_out", [128, C, D], cell=[RA0]), place("fox_w_o", [128, C, D], cell=[RB0])]
    b = [RB0]
    REC = place("rec", [128, C, RECW], cell=b)
    CONV = place("conv", [128, C * PADW], cell=b)
    RA = place("rg_a", [128, C * PADW], cell=b)
    IB = place("rg_i", [128, C * PADW], cell=b)
    TH = place("rg_th", [128, C * PADW], cell=b)
    SMN = place("small_nat", [SMALL, D], cell=b)
    SMT = place("small_t", [128, C, SMALL], cell=b)
    ST = place("state_t", [128, C, NST], cell=b)
    assert b[0] <= RC0
    c = [RC0]
    GATE = place("gate", [128, C, T], cell=c)
    WG = place("rg_gate_w", [128, 2, C, 128], cell=c)
    STN = place("state_nat", [NST, D], cell=c)
    LSG = [place(f"lam_{n}", [128, C], cell=c) for n in range(7)]
    NEGS = place("a_scale", [128, C], cell=c)
    POSS = place("a_scale_neg", [128, C], cell=c)
    cmax = c[0]

    RINGS, WQS = [], []
    for layer, (ring_at, wq_at) in enumerate(((RA0, RB0), (RB0, RA0))):
        RINGS.append(place(f"expert_rows{layer}", [TT, RING, D], cell=[ring_at]))
        WQS.append(place(f"peer_w_q{layer}", [128, C, 2 * D], cell=[wq_at]))
    c = [RC0]
    QT = place("peer_q", [128, 2 * PH, TT], cell=c)
    KT = place("keys_t", [128, 2, PH, 128], cell=c)
    S = place("scores", [TT, 2, 2 * PH, NK], cell=c)
    KN = place("keys_nat", [128, 2, PH, 128], cell=[c[0] - 4 * 2 * PH * NK])
    CAND = place("cand", [TT, 2, TK * TK], cell=c)
    EQ = place("hit", [TT, 2 * TK, TK], cell=[c[0] - 4 * 2 * TK * TK])
    V16 = place("top_val", [TT, 4, TK], cell=c)
    I16 = place("top_idx", [TT, 4, TK], U32, cell=c)
    I16F = place("top_idx_f", [TT, 4, TK], cell=c)
    SC = place("pair_val", [TT, 2, TK], cell=c)
    J = place("pair_idx", [TT, 2 * TK], U32, cell=c)
    JA = place("pair_a", [TT, 2 * TK], U32, cell=c)
    JB = place("pair_b", [TT, 2 * TK], U32, cell=c)
    JAF = place("pair_a_f", [TT, 2 * TK], cell=c)
    JBF = place("pair_b_f", [TT, 2 * TK], cell=c)
    E1 = place("expert_hi", [TT, 2 * TK], cell=c)
    E2 = place("expert_lo", [TT, 2 * TK], cell=c)
    G = place("g", [TT, NT, PH, TK], cell=c)
    GS = place("g_sum", [TT, PH], cell=c)
    IDXF = place("idx_f", [TT, UCOLS], cell=c)
    IDX = place("idx", [TT, NT * SLOTS], I32, cell=c)
    ACTV = place("u_dot_x", [TT, SLOTS], cell=c)
    GELU = place("act", [TT, SLOTS], cell=c)
    WN = place("w_nat", [TT, SLOTS], cell=c)
    WSTG = place("w_stage", [TT, 2, HALF], cell=c)
    DG = place("w_diag", [TT, 2, HALF, TT], cell=c)
    ACC = place("dots", [TT, 2, HALF], cell=c)
    STG = place("idx_stage", [TT, 2, 2, HALF], I32, cell=c)
    cmax = max(cmax, c[0])

    WF = place("fox_w_in", [128, 3, C, 512], cell=[RB0 + 4 * 3 * D])
    CACHE = place("cache_rows", [128, CSLOTS, 2, PAGES, D], cell=[RB0])
    b = [RA0]
    QF = place("q_t", [128, H, T], cell=b)
    KF = place("k_t", [128, H, T], cell=b)
    KNF = place("k_nat", [TT, NT, D], cell=b)
    VN = place("v_nat", [TT, NT, D], cell=b)
    PT = place("probs_t", [TT, 2, NT, TT], cell=b)
    PTS = place("probs_t_s", [128, 2, 3, NS], cell=b)
    LFN = place("logf_nat", [TT, NT, H], cell=b)
    QM = place("q_masked", [128, 2, H * (NS + 1)], cell=b)
    CS = place("c_sample", [H, DB, PAST + DS], cell=b)
    assert b[0] <= RB0
    c = [RC0]
    KC = place("cache_k_t", [128, 2, H, NKEYS], cell=c)
    PS = place("probs_s", [NS, NP, NKEYS], cell=c)
    PP = place("probs", [TT, NP, T], cell=c)
    ONES = place("ones", [H, NKEYS], cell=c)
    CP = place("c_prompt", [H, TP], cell=c)
    NCP = place("c_prompt_neg", [H, TP], cell=c)
    MASKC = place("causal", [TT, TT], cell=c)
    MASKS = place("causal_s", [NS, DB, NS], cell=c)
    CSN = place("c_new", [H, NS], cell=c)
    SEL = place("head_sel", [H, NS], cell=c)
    NSEL = place("head_sel_neg", [H, NS], cell=c)
    CQ = place("c_query", [H, DB, NS], cell=c)
    NMX = place("neg_max", [TT, NP], cell=c)
    SUMS = place("sums", [TT, NP], cell=c)
    RSUM = place("inv_sums", [TT, NP], cell=c)
    cmax = max(cmax, c[0])
    c = [RC0]
    LF = [place(f"logf_{n}", [H, T], cell=c) for n in range(7)]
    LPX = place("logf_sample", [H, DB, PAST + DS], cell=c)
    assert c[0] <= RC0 + 4 * 2 * H * NKEYS
    assert cmax <= nc.sbuf_usable_end, (cmax, nc.sbuf_usable_end)
    BANK = [ctx.enter_context(nc.psum_tensor(f"bank{n}", [128, 512], F32)) for n in range(4)]
    VB = [ctx.enter_context(nc.psum_tensor(f"banks_v{n}", [128, 2, 512], F32)) for n in range(2)]

    def sem(name):
        return ctx.enter_context(nc.semaphore(name))

    mm_done = [sem(f"mm_done{n}") for n in range(8)]
    bank_free = [sem(f"bank_free{n}") for n in range(8)]
    x_loaded, small_loaded, table_loaded = sem("x_loaded"), sem("small_loaded"), sem("table_loaded")
    win_loaded = [sem(f"win_loaded{n}") for n in range(4)]
    wg_loaded, wo_loaded, ln_loaded = sem("wg_loaded"), sem("wo_loaded"), sem("ln_loaded")
    wq_loaded = [sem(f"wq_loaded{n}") for n in range(4)]
    keys_loaded, wff_loaded = sem("keys_loaded"), sem("wff_loaded")
    wf_loaded = [sem(f"wf_loaded{n}") for n in range(6)]
    logf_loaded = sem("logf_loaded")
    cache_loaded = [[sem(f"cache_{kv}_loaded{n}") for n in range(CSLOTS)] for kv in "kv"]
    ident_ready, iota_ready, consts_ready = sem("ident_ready"), sem("iota_ready"), sem("consts_ready")
    pool_steps, page_rows_ready = sem("pool_steps"), sem("page_rows_ready")
    dve_steps, act_steps = sem("dve_steps"), sem("act_steps")
    lam_in, lam_exp, lam_u, lam_ln, lam_scaled = (sem(x) for x in ("lam_in", "lam_exp", "lam_u", "lam_ln", "lam_scaled"))
    conv_done, gates_ready, sq_in, sq_ready, y_ready, state_cols = (
        sem(x) for x in ("conv_done", "gates_ready", "sq_in", "sq_ready", "y_ready", "state_cols"))
    var_ready, std_ready, ln_done = sem("var_ready"), sem("std_ready"), sem("ln_done")
    idxf_ready, idx_ready, sc_ready, exp_ready = (sem(x) for x in ("idxf_ready", "idx_ready", "sc_ready", "exp_ready"))
    staged, issue = sem("staged"), sem("issue")
    row_in = [sem(f"row_in{n}") for n in range(RING)]
    half_used = [sem("half_a_used"), sem("half_b_used")]
    w_staged = sem("w_staged")
    dots_kept, act_ready, w_ready = sem("dots_kept"), sem("act_ready"), sem("w_ready")
    diag_ready, y_summed, y_taken = sem("diag_ready"), sem("y_summed"), sem("y_taken")
    f_in, f_exp, f_u, f_ln, f_ready, c_ready, kc_new = (
        sem(x) for x in ("f_in", "f_exp", "f_u", "f_ln", "f_ready", "c_ready", "kc_new"))
    cq_ready = sem("cq_ready")
    q_masked, nmax_ready, probs_exp, probs_ready = (
        sem(x) for x in ("q_masked", "nmax_ready", "probs_exp", "probs_ready"))
    stored = sem("stored")
    STORES = [0]

    u_dram = a["peer_u"].rearrange("l e d -> (l e) d")
    v_dram = a["peer_v"].rearrange("l e d -> (l e) d")
    k_dram = a["cache_k"].rearrange("l n p h d -> (l n p) (h d)")
    cv_dram = a["cache_v"].rearrange("l n p h d -> (l n p) (h d)")
    cl_dram = a["cache_logf"].rearrange("l n p h -> (l n p) h")

    def bank(name):
        n = at[name][0]
        return BANK[n] if n < 4 else VB[(n - 4) // 2][:, (n - 4) % 2, :]

    def ps(name, rows, lo, hi):
        n = at[name][0]
        return BANK[n][0:rows, lo:hi] if n < 4 else VB[(n - 4) // 2][0:rows, (n - 4) % 2, lo:hi]

    def begin(pe, name):
        n, uses = at[name]
        if uses:
            pe.wait_ge(bank_free[n], uses)

    def computed(eng, name):
        n, uses = at[name]
        eng.wait_ge(mm_done[n], uses + 1)

    def moved(eng, name):
        n, uses = at[name]
        eng.wait_ge(bank_free[n], uses + 1)

    def padded(t):
        return t[:, :].rearrange("p (m t) -> p m t", m=C)

    block = ctx.enter_context(nc.Block())

    @block.sync
    def _(sp):
        def store(dst, src):
            sp.dma_start(dst, src).then_inc(stored, 16)
            STORES[0] += 16

        xs = a["x_sample"].rearrange("b s d -> (b s) d")
        xp = a["x_prompt"].rearrange("b s d -> (b s) d")
        n0 = P0 - META
        sp.dma_start(X[0:NS, 0, :], xs).then_inc(x_loaded, 16)
        sp.dma_start(X[NS:NS + META, 0, :], a["meta_tokens"]).then_inc(x_loaded, 16)
        sp.dma_start(X[NS + META:TT, 0, :], xp[0:n0, :]).then_inc(x_loaded, 16)
        for i in (1, 2):
            sp.dma_start(X[:, i, :], xp[n0 + (i - 1) * TT:n0 + i * TT, :]).then_inc(x_loaded, 16)
        for row, src in ((R_H, a["state_h"][0]), (R_CS, a["state_conv"][0].rearrange("b j d -> (b j) d")),
                         (R_CW, a["rg_conv_w"][0]), (R_CB, a["rg_conv_b"]), (R_BA, a["rg_b_a"]),
                         (R_BX, a["rg_b_x"]), (R_LAM, a["rg_lambda"])):
            sp.dma_start(SMN[row:row + src.shape[0], :], src).then_inc(small_loaded, 16)
        pt = a["page_table"].rearrange("b j -> (b j)")
        sp.dma_start(PTI[:, :], pt.partition_broadcast(128)).then_inc(table_loaded, 16)
        win = a["rg_w_in"][0].rearrange("(c p) n -> p c n", p=128)
        for blk in (2, 3, 0, 1):
            sp.dma_start(WIN[:, :, blk * 512:blk * 512 + 512], win[:, :, blk * 512:blk * 512 + 512]).then_inc(win_loaded[blk], 16)
        sp.dma_start(WG[:, 0, :, :], a["rg_w_a"][0].rearrange("n c d -> c n d")).then_inc(wg_loaded, 16)
        sp.dma_start(WG[:, 1, :, :], a["rg_w_x"][0].rearrange("n c d -> c n d")).then_inc(wg_loaded, 16)

        def load_ln(n, g, bb):
            if n:
                sp.wait_ge(ln_done, NT * n)
            sp.dma_start(LNG[:, :], g.partition_broadcast(TT)).then_inc(ln_loaded, 16)
            sp.dma_start(LNB[:, :], bb.partition_broadcast(TT)).then_inc(ln_loaded, 16)

        load_ln(0, a["ln_mix_g"][0], a["ln_mix_b"][0])
        computed(sp, ("gate", C - 1))
        sp.dma_start(WO[0][:, :, :], a["rg_w_out"][0].rearrange("(c p) n -> p c n", p=128)).then_inc(wo_loaded, 16)

        def load_wq(layer):
            wq = a["peer_w_q"][layer].rearrange("(c p) n -> p c n", p=128)
            for blk in range(4):
                sp.dma_start(WQS[layer][:, :, blk * 512:blk * 512 + 512], wq[:, :, blk * 512:blk * 512 + 512]).then_inc(wq_loaded[blk], 16)

        def load_keys(layer):
            for half, keys in enumerate((a["peer_keys1"], a["peer_keys2"])):
                sp.dma_start(KN[:, half, :, :], keys[layer].rearrange("h k c -> k h c")).then_inc(keys_loaded, 16)

        sp.wait_ge(y_ready, 1)
        computed(sp, ("st", 1))
        load_wq(0)
        for j in range(2):
            moved(sp, ("st", j))
        store(o["state_h_prompt"][0], STN[0:1, :])
        store(o["state_h_sample"][0], STN[1:1 + DB, :])
        store(o["state_conv_prompt"][0, 0], STN[1 + DB:DB + CW, :])
        store(o["state_conv_sample"][0].rearrange("b j d -> (b j) d"), STN[DB + CW:NST, :])
        sp.wait_ge(stored, STORES[0])
        load_keys(0)
        load_ln(1, a["ln_ffn_g"][0], a["ln_ffn_b"][0])

        wf = a["fox_w_in"][0].rearrange("(c p) n -> p c n", p=128)

        def load_wf(blk):
            sp.dma_start(WF[:, WF_BLOCKS.index(blk) % 3, :, :], wf[:, :, blk * 512:blk * 512 + 512]).then_inc(wf_loaded[blk], 16)

        computed(sp, ("q", 0, NT - 1, 3))
        sp.dma_start(WFF[:, :, :], wf[:, :, 3 * D:3 * D + H]).then_inc(wff_loaded, 16)
        sp.dma_start(BF[:, :], a["fox_b_f"].rearrange("l h -> h l")).then_inc(wff_loaded, 16)
        sp.wait_ge(half_used[0], HALF * (USES_PER_LAYER - LONE) + HALF)
        for blk in WF_BLOCKS[:3]:
            load_wf(blk)

        for blk, name in zip(WF_BLOCKS[3:], (("kn", NT - 1, 0), ("kn", NT - 1, 1), ("qf", 3))):
            computed(sp, name)
            load_wf(blk)
        load_ln(2, a["ln_mix_g"][1], a["ln_mix_b"][1])
        rows = [(0, TT), (TT - NS, TT), (2 * TT - NS, TT)]
        for kind, buf, prompt, sample in (("kn", KNF, o["k_prompt"], o["k_sample"]), ("vn", VN, o["v_prompt"], o["v_sample"])):
            for i in range(NT):
                for hf in range(2):
                    moved(sp, (kind, i, hf))
            prompt = prompt.rearrange("l b t h d -> (l b t) (h d)")
            sample = sample.rearrange("l b t h d -> (l b t) (h d)")
            store(sample, buf[0:NS, 0, :])
            store(prompt[0:P0, :], buf[NS:TT, 0, :])
            for i in (1, 2):
                store(prompt[rows[i][0]:rows[i][0] + TT, :], buf[:, i, :])
        moved(sp, ("lfT",))
        lp = o["logf_prompt"].rearrange("l b t h -> (l b t) h")
        store(o["logf_sample"].rearrange("l b t h -> (l b t) h"), LFN[0:NS, 0, :])
        store(lp[0:P0, :], LFN[NS:TT, 0, :])
        for i in (1, 2):
            store(lp[rows[i][0]:rows[i][0] + TT, :], LFN[:, i, :])
        for bb in (4, 5):
            computed(sp, ("kc", bb, 3))
            computed(sp, ("O", SAMPLE[bb]))
        sp.dma_start(WO[1][:, :, :], a["fox_w_o"][0].rearrange("(c p) n -> p c n", p=128)).then_inc(wo_loaded, 16)
        computed(sp, ("O", len(ITEMS) - 1))
        sp.wait_ge(stored, STORES[0])
        load_wq(1)
        load_keys(1)
        load_ln(3, a["ln_ffn_g"][1], a["ln_ffn_b"][1])
        sp.wait_ge(ln_done, NT * 3 + 1)
        store(o["y_sample"].rearrange("b s d -> (b s) d"), X[0:NS, 0, :])
        yp = o["y_prompt"].rearrange("b s d -> (b s) d")
        store(yp[0:n0, :], X[NS + META:TT, 0, :])
        for i in (1, 2):
            sp.wait_ge(ln_done, NT * 3 + i + 1)
            store(yp[n0 + (i - 1) * TT:n0 + i * TT, :], X[:, i, :])
        sp.wait_ge(stored, STORES[0])

    @block.gpsimd
    def _(g):
        steps = Chain(g, pool_steps)
        steps.add(g.memset(IDENT[:, :], 0.0))
        steps.wait()
        g.affine_select(out=IDENT[:, :], in_=IDENT[:, :], compare_op=ALU.not_equal, fill=1.0,
                        base=0, pattern=[[-1, 128]], channel_multiplier=1).then_inc(ident_ready, 1)
        g.iota(IOP[:, :], pattern=[[0, 1]], base=0, channel_multiplier=1,
               allow_small_or_imprecise_dtypes=True).then_inc(iota_ready, 1)
        g.iota(IOTA16[:, :], pattern=[[1, TK]], base=0, channel_multiplier=0,
               allow_small_or_imprecise_dtypes=True).then_inc(iota_ready, 1)
        g.wait_ge(page_rows_ready, 1)
        for n in range(DB * PAGES):
            g.indirect_dma_start(out=LPN[:, n, :], out_offset=None, in_=cl_dram,
                                 in_offset=bass.IndirectOffsetOnAxis(ap=PIDX[:, n:n + 1], axis=0)).then_inc(logf_loaded, 16)

        def half_ring(ring, half, parity, use, idx_cols, table, stage_count):
            for part in range(2):
                g.wait_ge(half_used[half], HALF * use + (part + 1) * (HALF // 2))
                if part == 0:
                    g.tensor_copy(STG[:, half, parity, :], idx_cols).then_inc(staged, 1)
                    g.wait_ge(staged, stage_count)
                g.sem_inc(issue, 1)
                for k in range(part * HALF // 2, (part + 1) * HALF // 2):
                    slot = half * HALF + k
                    g.indirect_dma_start(out=ring[:, slot, :], out_offset=None, in_=table,
                                         in_offset=bass.IndirectOffsetOnAxis(ap=STG[:, half, parity, k:k + 1], axis=0)).then_inc(row_in[slot], 16)

        def experts(layer):
            ring, use, units = RINGS[layer], layer * USES_PER_LAYER, layer * ALL
            count = 2 * use
            g.wait_ge(idx_ready, units + 1)
            for j in range(LONE):
                for half in range(2):
                    half_ring(ring, half, j % 2, j + use, IDX[:, j * RING + half * HALF:j * RING + (half + 1) * HALF], u_dram, 2 * j + count + half + 1)
            use, count = use + LONE, count + 2 * LONE
            with g.Fori(0, ALL - 1) as n:
                g.wait_ge(idx_ready, n + (units + 2))
                for q in range(PER_UNIT):
                    half_ring(ring, 0, q % 2, n * PER_UNIT + (use + q), IDX[:, bass.ds(n * UCOLS + (UCOLS + q * HALF), HALF)], u_dram,
                              n * (2 * PER_UNIT) + (count + 2 * q + 1))
                    half_ring(ring, 1, q % 2, n * PER_UNIT + (use + q), IDX[:, bass.ds(n * UCOLS + q * HALF, HALF)], v_dram,
                              n * (2 * PER_UNIT) + (count + 2 * q + 2))
            use, count = use + (ALL - 1) * PER_UNIT, count + 2 * (ALL - 1) * PER_UNIT
            for j in range(LONE):
                for half in range(2):
                    col = (ALL - 1) * UCOLS + j * RING + half * HALF
                    half_ring(ring, half, j % 2, j + use, IDX[:, col:col + HALF], v_dram, 2 * j + count + half + 1)

        for half in range(2):
            g.sem_inc(half_used[half], HALF)
        computed(g, ("out", 0, NT - 1, 1))
        experts(0)

        g.wait_ge(ln_done, 2 * NT)
        steps.add(g.memset(MASKC[:, :], 0.0))
        steps.add(g.memset(MASKS[:, :, :], 0.0))
        steps.add(g.memset(SEL[:, :], 1.0))
        steps.add(g.memset(NSEL[:, :], -1.0))
        steps.add(g.memset(ONES[:, :], 1.0))
        steps.add(g.memset(QM[:, :, :], 0.0))
        steps.add(g.memset(PP[:, :, 0:NS], 0.0))
        steps.wait()
        steps.add(g.affine_select(out=MASKC[:, :], in_=MASKC[:, :], compare_op=ALU.is_ge, fill=LOW,
                                  base=0, pattern=[[-1, TT]], channel_multiplier=1))
        steps.add(g.affine_select(out=MASKS[:, :, :], in_=MASKS[:, :, :], compare_op=ALU.is_equal, fill=LOW,
                                  base=0, pattern=[[1, DB], [-1, DB], [0, DS]], channel_multiplier=0))
        steps.wait()
        steps.add(g.affine_select(out=MASKS[:, :, :], in_=MASKS[:, :, :], compare_op=ALU.is_ge, fill=LOW,
                                  base=0, pattern=[[0, DB], [0, DB], [-H, DS]], channel_multiplier=1))
        steps.add(g.affine_select(out=SEL[:, :], in_=SEL[:, :], compare_op=ALU.is_equal, fill=0.0,
                                  base=0, pattern=[[0, DS], [-1, H]], channel_multiplier=1))
        steps.add(g.affine_select(out=NSEL[:, :], in_=NSEL[:, :], compare_op=ALU.is_equal, fill=0.0,
                                  base=0, pattern=[[0, DS], [-1, H]], channel_multiplier=1))
        steps.wait()
        g.sem_inc(consts_ready, 1)

        def pages(bb):
            if bb < CSLOTS:
                computed(g, (("qf", H - 1), ("vn", NT - 1, 0), ("vn", NT - 1, 1), ("vn", NT - 1, 1))[bb])
            for kv, src in enumerate((k_dram, cv_dram)):
                if bb >= CSLOTS:
                    computed(g, ("O", SAMPLE[bb - CSLOTS]) if kv else ("kc", bb - CSLOTS, 3))
                for pg in range(PAGES):
                    n = bb * PAGES + pg
                    g.indirect_dma_start(out=CACHE[:, bb % CSLOTS, kv, pg, :], out_offset=None, in_=src,
                                         in_offset=bass.IndirectOffsetOnAxis(ap=PIDX[:, n:n + 1], axis=0)).then_inc(cache_loaded[kv][bb % CSLOTS], 16)

        for bb in range(CSLOTS):
            pages(bb)
        g.wait_ge(c_ready, 1)
        for bb in range(DB):
            ins = g.tensor_tensor(CQ[:, bb, :].rearrange("p (s h) -> p s h", h=H), SEL[:, :].rearrange("p (s h) -> p s h", h=H),
                                  CS[:, bb, PAST:PAST + DS].unsqueeze(2).to_broadcast([H, DS, H]), ALU.mult)
        ins.then_inc(cq_ready, 1)
        for bb in range(CSLOTS, DB):
            pages(bb)
        computed(g, ("out", 1, NT - 1, 1))
        experts(1)

    @block.tensor
    def _(pe):
        def done(name, ins):
            ins.then_inc(mm_done[at[name][0]], 1)

        def transposes(name, pieces):
            begin(pe, name)
            for rows, col, src in pieces:
                k = src.shape[0]
                last = pe.transpose(ps(name, rows, col, col + k), src, IDENT[0:k, 0:k])
            done(name, last)

        def x_transposes(n, tiles=range(NT)):
            for i in tiles:
                if n:
                    pe.wait_ge(ln_done, NT * (n - 1) + i + 1)
                for hf in range(2):
                    transposes(("xt", n, i, hf), [(128, q * TT, X[:, i, (4 * hf + q) * 128:(4 * hf + q + 1) * 128]) for q in range(4)])

        def product(name, rows, pairs, lo=0):
            begin(pe, name)
            pairs = list(pairs)
            for n, (lhsT, rhs) in enumerate(pairs):
                last = pe.matmul(ps(name, rows, lo, lo + rhs.shape[-1]), lhsT=lhsT, rhs=rhs, start=n == 0, stop=n == len(pairs) - 1)
            done(name, last)

        def x_transposed(n, tiles=range(NT)):
            for i in tiles:
                for hf in range(2):
                    moved(pe, ("xt", n, i, hf))

        def mixer_out(layer, tiles):
            pe.wait_ge(wo_loaded, 16 * (layer + 1))
            for i in tiles:
                for hf in range(2):
                    product(("out", layer, i, hf), TT, [(Y[:, c, i * TT:(i + 1) * TT], WO[layer][:, c, hf * 512:hf * 512 + 512]) for c in range(C)])

        pe.wait_ge(ident_ready, 1)
        pe.wait_ge(small_loaded, 16 * 7)
        transposes(("small",), [(128, c * SMALL, SMN[:, c * 128:c * 128 + 128]) for c in range(C)])
        pe.wait_ge(x_loaded, 16 * 5)
        x_transposes(0)
        x_transposed(0)
        def in_products(kind, first, chunks):
            for m in chunks:
                col = first + m
                pe.wait_ge(win_loaded[col // 4], 16)
                product((kind, m), 128, [(WIN[:, c, col * 128:col * 128 + 128], XT[:, c, :]) for c in range(C)])

        in_products("rec", C, range(C))
        in_products("gate", 0, range(EARLY_GATES))
        pe.wait_ge(wg_loaded, 32)
        for m in range(C):
            pe.wait_ge(conv_done, m + 1)
            for w, kind in enumerate(("ra", "ix")):
                product((kind, m), 128, [(WG[:, w, m, :], CONV[:, m * PADW:(m + 1) * PADW])])
        in_products("gate", 0, range(EARLY_GATES, C))
        pe.wait_ge(state_cols, 1)
        for j in range(2):
            transposes(("st", j), [(NST, q * 128, ST[:, 4 * j + q, :]) for q in range(4)])
        pe.wait_ge(y_ready, 1)
        mixer_out(0, range(NT - 1))

        def v_part(layer, n, p, s):
            y = VB[(n // UNITS) % 2]
            pe.wait_ge(diag_ready, HALF * p + HALF * (layer * V_PARTS + n * PER_UNIT + 1))
            for k in range(HALF):
                slot = HALF + k
                pe.wait_ge(row_in[slot], 16 * p + 16 * (layer * USES_PER_LAYER + LONE + n * PER_UNIT + 1))
                for hf in range(2):
                    last = pe.matmul(y[0:TT, hf, :], lhsT=DG[:, s, k, :], rhs=RINGS[layer][:, slot, hf * 512:hf * 512 + 512],
                                     start=False, stop=False)
                last.then_inc(half_used[1], 1)

        def y_bounds(i, first):
            for hf in range(2):
                ins = pe.matmul(VB[i % 2][0:TT, hf, :], lhsT=IDENT[0:1, 1:TT + 1], rhs=IDENT[0:1, 0:1].to_broadcast([1, 512]),
                                start=first, stop=not first)
            return ins

        def experts(layer):
            n = 2 * layer + 1

            def queries_and_scores(i, j):
                name = ("q", layer, i, j)
                pe.wait_ge(wq_loaded[j], 16 * (layer + 1))
                begin(pe, name)
                for q in range(4):
                    m = 4 * j + q
                    for c in range(C):
                        last = pe.matmul(ps(name, 128, q * TT, (q + 1) * TT), lhsT=WQS[layer][:, c, m * 128:m * 128 + 128],
                                         rhs=XT[:, c, i * TT:(i + 1) * TT], start=c == 0, stop=c == C - 1)
                done(name, last)
                if i == 0 and j == 0:
                    for n4 in range(4):
                        moved(pe, ("kt", layer, n4))
                name = ("s", layer, i, j)
                begin(pe, name)
                moved(pe, ("q", layer, i, j))
                for q in range(4):
                    m = 4 * j + q
                    last = pe.matmul(ps(name, TT, q * 128, q * 128 + 128), lhsT=QT[:, m, :],
                                     rhs=KT[:, m % 2, m // 2, :], start=True, stop=True)
                done(name, last)

            for i in range(NT - 1):
                x_transposes(n, [i])
                if i == 0:
                    pe.wait_ge(keys_loaded, 32 * (layer + 1))
                    for j in range(4):
                        half, h0 = j // 2, (j % 2) * 4
                        transposes(("kt", layer, j), [(128, q * 128, KN[:, half, h0 + q, :]) for q in range(4)])
                x_transposed(n, [i])
                for j in range(4):
                    queries_and_scores(i, j)
                    if i == 0 and j == 1:
                        mixer_out(layer, [NT - 1])
            for i in range(NT):
                if i >= 2:
                    pe.wait_ge(y_taken, layer * NT + i - 1)
                y_bounds(i, True)
                for unit in range(UNITS):
                    n_unit = i * UNITS + unit
                    if i == 0:
                        for p in range(2):
                            v_part(layer, n_unit, p, p)
                        if unit == 0:
                            x_transposes(n, [NT - 1])
                            x_transposed(n, [NT - 1])
                        queries_and_scores(NT - 1, unit)
                        for p in range(2, PER_UNIT):
                            v_part(layer, n_unit, p, p % 2)
                    elif n_unit < ALL - 1:
                        with pe.Fori(0, PER_UNIT // 2) as j:
                            for p in range(2):
                                v_part(layer, n_unit, 2 * j + p, p)
                    else:
                        for p in range(LONE):
                            v_part(layer, n_unit, p, p)
                y_bounds(i, False).then_inc(y_summed, 1)

        experts(0)

        def rows_product(kind, i, hf):
            blk = {"kn": 2, "vn": 4}[kind] + hf
            pe.wait_ge(wf_loaded[blk], 16)
            product((kind, i, hf), TT, [(XT[:, c, i * TT:(i + 1) * TT], WF[:, WF_BLOCKS.index(blk) % 3, c, :]) for c in range(C)])

        x_transposes(2, range(NT - 1))
        x_transposed(2, range(NT - 1))
        for hf in range(2):
            for i in range(NT - 1):
                rows_product("kn", i, hf)
        pe.wait_ge(y_taken, NT)
        x_transposes(2, [NT - 1])
        x_transposed(2, [NT - 1])
        pe.wait_ge(wff_loaded, 32)
        product(("f",), H, [(WFF[:, c, :], XT[:, c, :]) for c in range(C)])
        for hf in range(2):
            rows_product("kn", NT - 1, hf)
        for m in range(H):
            pe.wait_ge(wf_loaded[m // 4], 16)
            place_m = WF_BLOCKS.index(m // 4) % 3
            product(("qf", m), 128, [(WF[:, place_m, c, (m % 4) * 128:(m % 4) * 128 + 128], XT[:, c, :]) for c in range(C)])
        for hf in range(2):
            for i in range(NT):
                rows_product("vn", i, hf)
        for i in range(NT):
            for hf in range(2):
                moved(pe, ("kn", i, hf))
                transposes(("kf", i, hf), [(128, q * TT, KNF[:, i, (4 * hf + q) * 128:(4 * hf + q + 1) * 128]) for q in range(4)])
        pe.wait_ge(f_ready, 1)
        transposes(("lfT",), [(TT, i * H, LF[6][:, i * TT:(i + 1) * TT]) for i in range(NT)])
        pe.wait_ge(logf_loaded, 16 * DB * PAGES)
        for j in range(4):
            transposes(("lpT", j), [(H, q * 128, LPN[:, 4 * j + q, :]) for q in range(4)])
        for i in range(NT):
            for hf in range(2):
                moved(pe, ("kf", i, hf))
                moved(pe, ("vn", i, hf))
        for m in range(H):
            moved(pe, ("qf", m))
        pe.wait_ge(c_ready, 1)
        pe.wait_ge(consts_ready, 1)
        pe.wait_ge(ident_ready, 1)

        def scores(n):
            kind, x, t = ITEMS[n]
            name = ("S", n)
            if kind == "p":
                nq, nk, q0 = QROWS[t], KEYS[t], QCOL[t]
                pick = IDENT[0:H, x:x + 1]
                product(name, nq, [(QF[:, x, q0:q0 + nq], KF[:, x, NS:NS + nk]),
                                   (CP[:, q0 - NS:q0 - NS + nq], pick.to_broadcast([H, nk])),
                                   (pick.to_broadcast([H, nq]), NCP[:, 0:nk])])
                return
            for j in range(4):
                moved(pe, ("kc", x, j))
            pe.wait_ge(cq_ready, 1)
            pe.wait_ge(q_masked, x + 1)
            pe.wait_ge(kc_new, 1)
            begin(pe, name)
            pe.matmul(ps(name, NS, 0, NKEYS), lhsT=CQ[:, x, :], rhs=ONES[:, :], start=True, stop=False)
            pe.matmul(ps(name, NS, 0, PAST), lhsT=NSEL[:, :], rhs=CS[:, x, 0:PAST], start=False, stop=False)
            pe.matmul(ps(name, NS, PAST, NKEYS), lhsT=NSEL[:, :], rhs=CSN[:, :], start=False, stop=False)
            for h in range(H):
                last = pe.matmul(ps(name, NS, 0, NKEYS), lhsT=QM[:, x % 2, h * NS:(h + 1) * NS], rhs=KC[:, x % 2, h, :],
                                 start=False, stop=h == H - 1)
            done(name, last)

        def probs_t(n):
            kind, x, t = ITEMS[n]
            pe.wait_ge(probs_ready, n + 1)
            if kind == "p":
                nq = QROWS[t]
                transposes(("T", n), [(TT, j * TT, PP[0:nq, n % NP, j * TT:(j + 1) * TT]) for j in range(t + 1)])
            else:
                transposes(("T", n), [(128, 0, PS[:, n % NP, 0:128]), (128, NS, PS[:, n % NP, 128:256]), (NS, 2 * NS, PS[:, n % NP, 256:NKEYS])])

        def attend(n):
            kind, x, t = ITEMS[n]
            moved(pe, ("T", n))
            if kind == "p":
                nq = QROWS[t]
                product(("O", n), 128, [(VN[:, j, x * 128:(x + 1) * 128], PT[:, n % 2, j, 0:nq]) for j in range(t + 1)])
                return
            name = ("O", n)
            begin(pe, name)
            pe.wait_ge(cache_loaded[1][x % CSLOTS], 16 * PAGES * (x // CSLOTS + 1))
            for h in range(H):
                cols = slice(h * 128, h * 128 + 128)
                for j in range(3):
                    lhsT = CACHE[:, x % CSLOTS, 1, j, cols] if j < 2 else VN[0:NS, 0, cols]
                    k = 128 if j < 2 else NS
                    last = pe.matmul(ps(name, 128, h * DS, (h + 1) * DS), lhsT=lhsT, rhs=PTS[0:k, n % 2, j, h:NS:H], start=j == 0, stop=j == 2)
            done(name, last)

        for n in range(-1, len(ITEMS) + OLAG):
            if n >= OLAG:
                attend(n - OLAG)
            if 0 <= n < len(ITEMS):
                scores(n)
            if 0 <= n - TLAG < len(ITEMS):
                probs_t(n - TLAG)
            if n + 1 in SAMPLE:
                x = SAMPLE.index(n + 1)
                pe.wait_ge(cache_loaded[0][x % CSLOTS], 16 * PAGES * (x // CSLOTS + 1))
                for j in range(4):
                    pg, h0 = j // 2, (j % 2) * 4
                    transposes(("kc", x, j), [(128, q * 128, CACHE[:, x % CSLOTS, 0, pg, (h0 + q) * 128:(h0 + q + 1) * 128]) for q in range(4)])
        for n in range(len(ITEMS) - 8, len(ITEMS)):
            moved(pe, ("O", n))
        mixer_out(1, range(NT - 1))
        experts(1)

    @block.scalar
    def _(act):
        steps = Chain(act, act_steps)

        def out_of(name, dst, src):
            computed(act, name)
            act.copy(dst, src).then_inc(bank_free[at[name][0]], 1)

        def x_transposed(n, tiles=range(NT)):
            for i in tiles:
                out_of(("xt", n, i, 0), XT[:, 0:4, i * TT:(i + 1) * TT], ps(("xt", n, i, 0), 128, 0, 4 * TT).rearrange("p (c t) -> p c t", c=4))

        def std(n, i):
            act.wait_ge(var_ready, NT * n + i + 1)
            act.activation(STD[:, i, :], MV[:, i, 1:2], ACT.Sqrt).then_inc(std_ready, 1)

        act.wait_ge(lam_in, 1)
        act.activation(LSG[1][:, :], LSG[0][:, :], ACT.Exp).then_inc(lam_exp, 1)
        act.wait_ge(lam_u, 1)
        act.activation(LSG[3][:, :], LSG[2][:, :], ACT.Ln).then_inc(lam_ln, 1)
        x_transposed(0)
        for m in range(C):
            computed(act, ("rec", m))
            name = ("rec", m)
            act.copy(REC[:, m, CW - 1:CW - 1 + TP], ps(name, 128, NS, T))
            act.copy(REC[:, m, S0:RECW].rearrange("p (b t) -> p b t", b=DB)[:, :, CW - 1:SEQW],
                     ps(name, 128, 0, NS).rearrange("p (b t) -> p b t", b=DB)).then_inc(bank_free[at[name][0]], 1)

        def gates(chunks):
            for m in chunks:
                name = ("gate", m)
                computed(act, name)
                act.activation(GATE[:, m, :], ps(name, 128, 0, T), ACT.Gelu_apprx_tanh).then_inc(bank_free[at[name][0]], 1)

        gates(range(EARLY_GATES))
        moved(act, ("small",))
        for m in range(C):
            for kind, row, dst in (("ra", R_BA, RA), ("ix", R_BX, IB)):
                name = (kind, m)
                computed(act, name)
                act.activation(dst[:, m * PADW:(m + 1) * PADW], ps(name, 128, 0, PADW), ACT.Sigmoid,
                               bias=SMT[:, m, row:row + 1]).then_inc(bank_free[at[name][0]], 1)
        act.wait_ge(lam_scaled, 1)
        for m in range(C):
            moved(act, ("ra", m))
            act.activation(TH[:, m * PADW:(m + 1) * PADW], RA[:, m * PADW:(m + 1) * PADW], ACT.Tanh, scale=POSS[:, m:m + 1])
            act.activation(RA[:, m * PADW:(m + 1) * PADW], RA[:, m * PADW:(m + 1) * PADW], ACT.Exp, scale=NEGS[:, m:m + 1]).then_inc(gates_ready, 1)
        act.wait_ge(sq_in, 1)
        act.activation(TH[:, :], CONV[:, :], ACT.Sqrt).then_inc(sq_ready, 1)
        gates(range(EARLY_GATES, C))
        for j in range(2):
            out_of(("st", j), STN[:, j * 512:(j + 1) * 512], ps(("st", j), NST, 0, 512))
        for i in range(NT - 1):
            std(0, i)

        def diagonals(layer, n, p, s, cols):
            act.wait_ge(half_used[1], HALF * p + HALF * (layer * USES_PER_LAYER + LONE + n * PER_UNIT))
            act.copy(WSTG[:, s, :], WN[:, cols]).then_inc(w_staged, 1)
            act.wait_ge(w_staged, p + (layer * V_PARTS + n * PER_UNIT + 1))
            for k in range(HALF):
                act.mul(DG[:, s, k, :], IDENT[0:TT, 0:TT], WSTG[:, s, k:k + 1]).then_inc(diag_ready, 1)

        def x_out(n, i):
            for hf in range(2):
                name = ("xt", n, i, hf)
                out_of(name, XT[:, 4 * hf:4 * hf + 4, i * TT:(i + 1) * TT], ps(name, 128, 0, 4 * TT).rearrange("p (c t) -> p c t", c=4))

        def queries_and_scores(layer, i, j):
            name = ("q", layer, i, j)
            out_of(name, QT[:, 4 * j:4 * j + 4, :].rearrange("p m t -> p (m t)"), ps(name, 128, 0, 4 * TT))
            if i == NT - 1:
                act.wait_ge(idx_ready, layer * ALL + j + 1)
            name = ("s", layer, i, j)
            out_of(name, S[:, i % 2, 4 * j:4 * j + 4, :].rearrange("p m k -> p (m k)"), ps(name, TT, 0, 512))

        def unit_diagonals(layer, n):
            col = (n % UNITS) * UCOLS
            act.wait_ge(w_ready, layer * ALL + n + 1)
            if n < UNITS:
                for p in range(PER_UNIT):
                    if p == 2:
                        if n == 0:
                            x_out(2 * layer + 1, NT - 1)
                        queries_and_scores(layer, NT - 1, n)
                    diagonals(layer, n, p, p % 2, slice(col + p * HALF, col + (p + 1) * HALF))
            elif n < ALL - 1:
                with act.Fori(0, PER_UNIT // 2) as j:
                    for s in range(2):
                        diagonals(layer, n, 2 * j + s, s, bass.ds(j * RING + (col + s * HALF), HALF))
            else:
                for p in range(LONE):
                    diagonals(layer, n, p, p, slice(col + p * RING + HALF, col + (p + 1) * RING))

        def experts(layer):
            def g_exp(n):
                act.wait_ge(sc_ready, layer * ALL + n + 1)
                g = G[:, n // UNITS, 2 * (n % UNITS):2 * (n % UNITS) + 2, :]
                act.activation(g, g, ACT.Exp).then_inc(exp_ready, 1)

            for i in range(NT - 1):
                x_out(2 * layer + 1, i)
                for j in range(4):
                    queries_and_scores(layer, i, j)
                    if i == 0 and j == 2:
                        std(2 * layer, NT - 1)
            g_exp(0)
            for n in range(ALL):
                cols = slice((n % UNITS) * UCOLS, (n % UNITS + 1) * UCOLS)
                act.wait_ge(dots_kept, PER_UNIT * (layer * ALL + n + 1))
                act.activation(GELU[:, cols], ACTV[:, cols], ACT.Gelu_apprx_tanh).then_inc(act_ready, 1)
                if n + 1 < ALL:
                    g_exp(n + 1)
                if n in NORM_AT:
                    std(2 * layer + 1, NORM_AT.index(n))
                unit_diagonals(layer, n)
            if layer == 0:
                for i in range(NT - 1):
                    x_out(2, i)
            std(2 * layer + 1, NT - 1)

        experts(0)
        x_transposed(2, [NT - 1])

        act.wait_ge(f_in, 1)
        act.activation(LF[1][:, :], LF[0][:, :], ACT.Exp).then_inc(f_exp, 1)
        act.wait_ge(f_u, 1)
        act.activation(LF[3][:, :], LF[2][:, :], ACT.Ln).then_inc(f_ln, 1)
        for m in range(H):
            name = ("qf", m)
            computed(act, name)
            act.mul(QF[:, m, :], ps(name, 128, 0, T), SCALE).then_inc(bank_free[at[name][0]], 1)
        for hf in range(2):
            for i in range(NT):
                out_of(("vn", i, hf), VN[:, i, hf * 512:hf * 512 + 512], ps(("vn", i, hf), TT, 0, 512))
        for m in range(H):
            moved(act, ("qf", m))
        act.wait_ge(consts_ready, 1)
        for n in range(-1, len(ITEMS) + TLAG):
            if 0 <= n < len(ITEMS):
                kind, x, t = ITEMS[n]
                act.wait_ge(nmax_ready, n + 1)
                name = ("S", n)
                if kind == "p":
                    nq, nk = QROWS[t], KEYS[t]
                    dst, src = PP[0:nq, n % NP, NS:NS + nk], ps(name, nq, 0, nk)
                else:
                    nq = NS
                    dst, src = PS[:, n % NP, :], ps(name, NS, 0, NKEYS)
                act.activation(dst, src, ACT.Exp, bias=NMX[0:nq, n % NP:n % NP + 1], accum_out=SUMS[0:nq, n % NP:n % NP + 1]).then_inc(bank_free[at[name][0]], 1)
            if n >= TLAG:
                m = n - TLAG
                kind, x, t = ITEMS[m]
                name = ("T", m)
                computed(act, name)
                if kind == "p":
                    nq = QROWS[t]
                    act.copy(PT[:, m % 2, 0:t + 1, 0:nq], ps(name, TT, 0, (t + 1) * TT).rearrange("p (j q) -> p j q", q=TT)[:, :, 0:nq])\
                        .then_inc(bank_free[at[name][0]], 1)
                else:
                    act.copy(PTS[:, m % 2, 0:2, :], ps(name, 128, 0, 2 * NS).rearrange("p (j q) -> p j q", q=NS))
                    act.copy(PTS[0:NS, m % 2, 2, :], ps(name, NS, 2 * NS, 3 * NS)).then_inc(bank_free[at[name][0]], 1)
            if n + 1 in SAMPLE:
                x = SAMPLE.index(n + 1)
                if x >= 2:
                    computed(act, ("S", SAMPLE[x - 2]))
                act.copy(QM[:, x % 2, :].rearrange("p (h x) -> p h x", h=H)[:, :, 0:NS:H],
                         QF[:, :, x * DS:(x + 1) * DS]).then_inc(q_masked, 1)
                for j in (0, 2):
                    out_of(("kc", x, j), KC[:, x % 2, 0:4, (j // 2) * 128:(j // 2) * 128 + 128],
                           ps(("kc", x, j), 128, 0, 512).rearrange("p (h k) -> p h k", h=4))
        for i in range(NT - 1):
            std(2, i)
        experts(1)

    @block.vector
    def _(v):
        steps = Chain(v, dve_steps)

        def out_of(name, dst, src):
            computed(v, name)
            v.tensor_copy(dst, src).then_inc(bank_free[at[name][0]], 1)

        def kn_out(i, hf):
            out_of(("kn", i, hf), KNF[:, i, hf * 512:hf * 512 + 512], ps(("kn", i, hf), TT, 0, 512))

        def x_transposed(n, tiles=range(NT)):
            for i in tiles:
                out_of(("xt", n, i, 1), XT[:, 4:8, i * TT:(i + 1) * TT], ps(("xt", n, i, 1), 128, 0, 4 * TT).rearrange("p (c t) -> p c t", c=4))

        def log_sigmoid(z, t, into, sent_in, got_exp, sent_u, got_ln):
            v.scalar_tensor_tensor(out=t[0], in0=z, scalar=-1.0, in1=z, op0=ALU.mult, op1=ALU.min).then_inc(sent_in, 1)
            v.wait_ge(got_exp, 1)
            v.tensor_scalar(t[2], t[1], 1.0, None, ALU.add).then_inc(sent_u, 1)
            v.wait_ge(sent_u, 1)
            steps.add(v.tensor_scalar(t[0], t[2], 1.0, None, ALU.subtract))
            steps.wait()
            steps.add(v.tensor_tensor(t[0], t[1], t[0], ALU.subtract))
            steps.add(v.reciprocal(t[4], t[2]))
            steps.wait()
            steps.add(v.tensor_tensor(t[0], t[0], t[4], ALU.mult))
            v.wait_ge(got_ln, 1)
            steps.wait()
            steps.add(v.tensor_tensor(t[0], t[0], t[3], ALU.add))
            steps.wait()
            steps.add(v.scalar_tensor_tensor(out=into, in0=z, scalar=0.0, in1=t[0], op0=ALU.min, op1=ALU.subtract))
            steps.wait()

        def layer_norm(n, i):
            v.wait_ge(ln_loaded, 32 * (n + 1))
            for hf in range(2):
                k = steps.add(v.bn_stats(STATS[:, i, hf, :], X[:, i, hf * 512:hf * 512 + 512]))
            steps.wait()
            steps.add(v.bn_aggr(MV[:, i, :], STATS[:, i, :, :].rearrange("p a b -> p (a b)")))
            steps.wait()
            v.tensor_scalar(MV[:, i, 1:2], MV[:, i, 1:2], EPS, None, ALU.add).then_inc(var_ready, 1)
            v.wait_ge(std_ready, NT * n + i + 1)
            steps.add(v.reciprocal(RSTD[:, i, :], STD[:, i, :]))
            steps.wait()
            steps.add(v.tensor_scalar(X[:, i, :], X[:, i, :], MV[:, i, 0:1], RSTD[:, i, 0:1], ALU.subtract, ALU.mult))
            steps.wait()
            steps.add(v.tensor_tensor(X[:, i, :], X[:, i, :], LNG[:, :], ALU.mult))
            steps.wait()
            v.tensor_tensor(X[:, i, :], X[:, i, :], LNB[:, :], ALU.add).then_inc(ln_done, 1)
            v.wait_ge(ln_done, NT * n + i + 1)

        def mixer_residual(layer, tiles):
            for i in tiles:
                for hf in range(2):
                    name = ("out", layer, i, hf)
                    computed(v, name)
                    x = X[:, i, hf * 512:hf * 512 + 512]
                    v.scalar_tensor_tensor(out=x, in0=x, scalar=ALPHA, in1=ps(name, TT, 0, 512), op0=ALU.mult, op1=ALU.add)\
                        .then_inc(bank_free[at[name][0]], 1)
                for hf in range(2):
                    moved(v, ("out", layer, i, hf))
                layer_norm(2 * layer, i)

        v.wait_ge(table_loaded, 16)
        v.wait_ge(iota_ready, 2)
        steps.add(v.tensor_copy(PTF[:, :], PTI[:, :]))
        steps.wait()
        steps.add(v.tensor_scalar(PTF[:, :], PTF[:, :], float(PAGE), IOP[:, 0:1], ALU.mult, ALU.add))
        steps.wait()
        v.tensor_copy(PIDX[:, :], PTF[:, :]).then_inc(page_rows_ready, 1)
        out_of(("small",), SMT[:, :, :].rearrange("p c r -> p (c r)"), ps(("small",), 128, 0, C * SMALL))
        moved(v, ("small",))
        steps.add(v.memset(REC[:, :, 0:CW - 1], 0.0))
        for m in range(C):
            steps.add(v.tensor_copy(REC[:, m, S0:RECW].rearrange("p (b t) -> p b t", b=DB)[:, :, 0:CW - 1],
                                    SMT[:, m, R_CS:R_CW].rearrange("p (b j) -> p b j", b=DB)))
        steps.add(v.tensor_copy(LSG[5][:, :], SMT[:, :, R_LAM]))
        steps.wait()
        log_sigmoid(LSG[5][:, :], [LSG[n][:, :] for n in range(5)], LSG[6][:, :], lam_in, lam_exp, lam_u, lam_ln)
        steps.add(v.tensor_scalar(POSS[:, :], LSG[6][:, :], -RG_C, None, ALU.mult))
        v.tensor_scalar(NEGS[:, :], LSG[6][:, :], RG_C, None, ALU.mult).then_inc(lam_scaled, 1)
        x_transposed(0)
        conv = padded(CONV)
        last = [0] * C
        for k in range(CW):
            for m in range(C):
                w = SMT[:, m, R_CW + k:R_CW + k + 1]
                if k == 0:
                    moved(v, ("rec", m))
                    last[m] = steps.add(v.tensor_scalar(conv[:, m, :], REC[:, m, 0:PADW], w, SMT[:, m, R_CB:R_CB + 1], ALU.mult, ALU.add))
                    continue
                steps.wait(last[m])
                ins = v.scalar_tensor_tensor(out=conv[:, m, :], in0=REC[:, m, k:k + PADW], scalar=w, in1=conv[:, m, :], op0=ALU.mult, op1=ALU.add)
                if k < CW - 1:
                    last[m] = steps.add(ins)
                else:
                    ins.then_inc(conv_done, 1)
        v.wait_ge(conv_done, C)
        a3, b3, h3 = padded(RA), padded(IB), padded(CONV)
        for m in range(C):
            moved(v, ("ix", m))
        n_ib = steps.add(v.tensor_tensor(IB[:, :], IB[:, :], CONV[:, :], ALU.mult))
        v.wait_ge(gates_ready, C)
        steps.wait(n_ib)
        steps.add(v.tensor_tensor(CONV[:, :], RA[:, :], RA[:, :], ALU.mult))
        steps.wait()
        v.scalar_tensor_tensor(out=CONV[:, :], in0=CONV[:, :], scalar=1.0, in1=TH[:, :], op0=ALU.add, op1=ALU.mult).then_inc(sq_in, 1)
        v.wait_ge(sq_ready, 1)
        steps.add(v.tensor_tensor(IB[:, :], IB[:, :], TH[:, :], ALU.mult))
        starts = a3[:, :, S0:S0 + (DB - 1) * SEQW + 1:SEQW]
        steps.wait()
        steps.add(v.tensor_tensor(SMT[:, :, 0:DB], SMT[:, :, 0:DB], starts, ALU.mult))
        steps.wait()
        b_starts = b3[:, :, S0:S0 + (DB - 1) * SEQW + 1:SEQW]
        steps.add(v.tensor_tensor(b_starts, b_starts, SMT[:, :, 0:DB], ALU.add))
        steps.add(v.memset(starts, 0.0))
        steps.add(v.memset(a3[:, :, 0:1], 0.0))
        steps.wait()
        steps.add(v.tensor_tensor_scan(CONV[:, :], RA[:, :], IB[:, :], 0.0, ALU.mult, ALU.add))
        steps.wait()
        for m in range(C):
            moved(v, ("gate", m))
        steps.add(v.tensor_tensor(Y[:, :, NS:T], h3[:, :, 0:TP], GATE[:, :, NS:T], ALU.mult))
        for t in range(DS):
            cols = slice(S0 + t, S0 + t + (DB - 1) * SEQW + 1, SEQW)
            ins = v.tensor_tensor(Y[:, :, t:NS:DS], h3[:, :, cols], GATE[:, :, t:NS:DS], ALU.mult)
            if t < DS - 1:
                steps.add(ins)
        ins.then_inc(y_ready, 1)
        steps.add(v.tensor_copy(ST[:, :, 0:1], h3[:, :, TP - 1:TP]))
        steps.add(v.tensor_copy(ST[:, :, 1:1 + DB], h3[:, :, S0 + DS - 1:S0 + DS - 1 + (DB - 1) * SEQW + 1:SEQW]))
        steps.add(v.tensor_copy(ST[:, :, 1 + DB:DB + CW], REC[:, :, TP:TP + CW - 1]))
        for m in range(C):
            ins = v.tensor_copy(ST[:, m, DB + CW:NST].rearrange("p (b j) -> p b j", b=DB),
                                REC[:, m, S0:RECW].rearrange("p (b t) -> p b t", b=DB)[:, :, DS:SEQW])
            if m < C - 1:
                steps.add(ins)
        ins.then_inc(state_cols, 1)
        mixer_residual(0, range(NT - 1))

        def dots(ring, tile, half, group, use, col):
            for k in range(HALF):
                slot = half * HALF + k
                v.wait_ge(row_in[slot], 16 * use + 16)
                v.tensor_tensor_reduce(out=ring[0:TT, slot, :], in0=ring[0:TT, slot, :], in1=X[:, tile, :], scale=1.0, scalar=0.0,
                                       op0=ALU.mult, op1=ALU.add, accum_out=ACC[:, group, k:k + 1]).then_inc(half_used[half], 1)
            v.wait_ge(half_used[half], HALF * use + 2 * HALF)
            v.tensor_copy(ACTV[:, bass.ds(col, HALF)], ACC[:, group, :]).then_inc(dots_kept, 1)

        def unit_dots(layer, n):
            ring, use = RINGS[layer], layer * USES_PER_LAYER
            i, col = n // UNITS, (n % UNITS) * UCOLS
            with v.Fori(0, PER_UNIT // 2) as j:
                for s in range(2):
                    if n == 0:
                        dots(ring, i, s, s, j + use, j * RING + (col + s * HALF))
                    else:
                        dots(ring, i, 0, s, 2 * j + (use + LONE + (n - 1) * PER_UNIT + s), j * RING + (col + s * HALF))
            v.wait_ge(dots_kept, PER_UNIT * (layer * ALL + n + 1))

        def pick(layer, i, unit):
            moved(v, ("s", layer, i, unit))

            def top16(vals, val16, idx16, count):
                rows = range(count)
                at1 = [steps.add(v.max(val16(r, 0), vals(r))) for r in rows]
                at2 = []
                for r in rows:
                    steps.wait(at1[r])
                    at2.append(steps.add(v.max_index(idx16(r, 0), val16(r, 0), vals(r))))
                at3 = []
                for r in rows:
                    steps.wait(at2[r])
                    at3.append(steps.add(v.match_replace(vals(r), val16(r, 0), vals(r), GONE)))
                at4 = []
                for r in rows:
                    steps.wait(at3[r])
                    at4.append(steps.add(v.max(val16(r, 1), vals(r))))
                for r in rows:
                    steps.wait(at4[r])
                    steps.add(v.max_index(idx16(r, 1), val16(r, 1), vals(r)))

            top16(lambda r: S[:, i % 2, 4 * unit + r, :], lambda r, e: V16[:, r, 8 * e:8 * e + 8], lambda r, e: I16[:, r, 8 * e:8 * e + 8], 4)
            cand = CAND[:, :, :].rearrange("p h (a b) -> p h a b", a=TK)
            steps.wait()
            steps.add(v.tensor_tensor(cand, V16[:, 0:4:2, :].unsqueeze(3).to_broadcast([TT, 2, TK, TK]),
                                      V16[:, 1:4:2, :].unsqueeze(2).to_broadcast([TT, 2, TK, TK]), ALU.add))
            steps.add(v.tensor_copy(I16F[:, :, :], I16[:, :, :]))
            steps.wait()
            jj = J[:, :].rearrange("p (h k) -> p h k", h=2)
            top16(lambda r: CAND[:, r, :], lambda r, e: SC[:, r, 8 * e:8 * e + 8], lambda r, e: jj[:, r, 8 * e:8 * e + 8], 2)
            steps.wait()
            steps.add(v.tensor_scalar(JA[:, :], J[:, :], 4, None, ALU.logical_shift_right))
            steps.add(v.tensor_scalar(JB[:, :], J[:, :], 15, None, ALU.bitwise_and))
            ins = v.tensor_tensor(G[:, i, 2 * unit:2 * unit + 2, :], SC[:, :, :], SC[:, :, 0:1].to_broadcast([TT, 2, TK]), ALU.subtract)
            ins.then_inc(sc_ready, 1)
            steps.wait()
            steps.add(v.tensor_copy(JAF[:, :], JA[:, :]))
            steps.add(v.tensor_copy(JBF[:, :], JB[:, :]))
            steps.wait()
            iota = IOTA16[:, :].unsqueeze(1).to_broadcast([TT, 2 * TK, TK])
            eq4 = EQ[:, :, :].rearrange("p (h k) a -> p h k a", h=2)
            for half, jf, e in ((0, JAF, E1), (1, JBF, E2)):
                steps.add(v.tensor_tensor(EQ[:, :, :], jf[:, :].unsqueeze(2).to_broadcast([TT, 2 * TK, TK]), iota, ALU.is_equal))
                steps.wait()
                steps.add(v.tensor_tensor(eq4, eq4, I16F[:, half:4:2, :].unsqueeze(2).to_broadcast([TT, 2, TK, TK]), ALU.mult))
                steps.wait()
                steps.add(v.tensor_reduce(out=e[:, :], in_=EQ[:, :, :], axis=AXX, op=ALU.add))
                steps.wait()
            steps.add(v.tensor_scalar(E1[:, :], E1[:, :], float(NK), float(layer * NE), ALU.mult, ALU.add))
            steps.wait()
            cols = slice(2 * unit * TK, 2 * (unit + 1) * TK)
            v.tensor_tensor(IDXF[:, :], E1[:, :], E2[:, :], ALU.add).then_inc(idxf_ready, 1)
            v.wait_ge(idxf_ready, layer * ALL + i * UNITS + unit + 1)
            v.tensor_copy(IDX[:, i * SLOTS + cols.start:i * SLOTS + cols.stop], IDXF[:, :]).then_inc(idx_ready, 1)

        def weigh(layer, n):
            i, unit = n // UNITS, n % UNITS
            gs, g = GS[:, 2 * unit:2 * unit + 2], G[:, i, 2 * unit:2 * unit + 2, :]
            cols = slice(unit * UCOLS, (unit + 1) * UCOLS)
            v.wait_ge(exp_ready, layer * ALL + n + 1)
            steps.add(v.tensor_reduce(out=gs, in_=g, axis=AXX, op=ALU.add))
            steps.wait()
            steps.add(v.reciprocal(gs, gs))
            steps.wait()
            steps.add(v.tensor_tensor(g, g, gs.unsqueeze(2).to_broadcast([TT, 2, TK]), ALU.mult))
            steps.wait()
            v.wait_ge(act_ready, layer * ALL + n + 1)
            v.tensor_tensor(WN[:, cols], GELU[:, cols], g.rearrange("p h k -> p (h k)"), ALU.mult).then_inc(w_ready, 1)

        def last_rows(layer):
            x = X[:, NT - 1, :]
            steps.add(v.tensor_scalar(x, x, ALPHA, None, ALU.mult))
            steps.wait()
            v.wait_ge(w_ready, ALL * (layer + 1))
            for p in range(LONE):
                use = (layer + 1) * USES_PER_LAYER - LONE + p
                for k in range(HALF):
                    v.wait_ge(row_in[k], 16 * use + 16)
                    if p or k:
                        v.wait_ge(half_used[0], HALF * use + HALF + k)
                    col = SLOTS - UCOLS + p * RING + k
                    v.scalar_tensor_tensor(out=x, in0=RINGS[layer][:, k, :], scalar=WN[:, col:col + 1], in1=x,
                                           op0=ALU.mult, op1=ALU.add).then_inc(half_used[0], 1)
            v.wait_ge(half_used[0], HALF * (layer + 1) * USES_PER_LAYER + HALF)

        def expert_norm(layer, i):
            v.wait_ge(y_summed, layer * NT + i + 1)
            v.scalar_tensor_tensor(out=X[:, i, :], in0=X[:, i, :], scalar=ALPHA if i < NT - 1 else 1.0, in1=VB[i % 2][0:TT, :, :].rearrange("p a d -> p (a d)"),
                                   op0=ALU.mult, op1=ALU.add).then_inc(y_taken, 1)
            v.wait_ge(y_taken, layer * NT + i + 1)
            layer_norm(2 * layer + 1, i)

        def experts(layer):
            for j in range(4):
                half, h0 = j // 2, (j % 2) * 4
                out_of(("kt", layer, j), KT[:, half, h0:h0 + 4, :].rearrange("p h k -> p (h k)"), ps(("kt", layer, j), 128, 0, 512))
            pick(layer, 0, 0)
            pick(layer, 0, 1)
            mixer_residual(layer, [NT - 1])
            for n in range(ALL):
                unit_dots(layer, n)
                if n:
                    weigh(layer, n)
                if n in NORM_AT:
                    expert_norm(layer, NORM_AT.index(n))
                if n + 2 < ALL:
                    pick(layer, (n + 2) // UNITS, (n + 2) % UNITS)
                if n == 0:
                    weigh(layer, n)
            last_rows(layer)
            expert_norm(layer, NT - 1)

        experts(0)
        x_transposed(2, [NT - 1])
        for hf in range(2):
            for i in range(NT - 1):
                kn_out(i, hf)

        v.wait_ge(wff_loaded, 32)
        computed(v, ("f",))
        v.tensor_scalar(LF[4][:, :], ps(("f",), H, 0, T), BF[:, 0:1], None, ALU.add).then_inc(bank_free[at[("f",)][0]], 1)
        moved(v, ("f",))
        log_sigmoid(LF[4][:, :], [LF[n][:, :] for n in (0, 1, 2, 3, 5)], LF[6][:, :], f_in, f_exp, f_u, f_ln)
        v.sem_inc(f_ready, 1)
        for hf in range(2):
            kn_out(NT - 1, hf)
        for i in range(NT):
            for hf in range(2):
                out_of(("kf", i, hf), KF[:, 4 * hf:4 * hf + 4, i * TT:(i + 1) * TT],
                       ps(("kf", i, hf), 128, 0, 4 * TT).rearrange("p (c t) -> p c t", c=4))
        out_of(("lfT",), LFN[:, :, :].rearrange("p i h -> p (i h)"), ps(("lfT",), TT, 0, NT * H))
        for j in range(4):
            out_of(("lpT", j), LPX[:, 2 * j:2 * j + 2, 0:PAST], ps(("lpT", j), H, 0, 512).rearrange("p (b t) -> p b t", b=2))
        steps.add(v.tensor_copy(LPX[:, :, PAST:PAST + DS], LF[6][:, 0:NS].rearrange("p (b t) -> p b t", b=DB)))
        v.wait_ge(consts_ready, 1)
        for j in range(4):
            moved(v, ("lpT", j))
        steps.wait()
        for bb in range(DB):
            steps.add(v.tensor_tensor_scan(CS[:, bb, :], ONES[:, 0:PAST + DS], LPX[:, bb, :], 0.0, ALU.mult, ALU.add))
        steps.add(v.tensor_tensor_scan(CP[:, :], ONES[:, 0:TP], LF[6][:, NS:T], 0.0, ALU.mult, ALU.add))
        steps.wait()
        steps.add(v.tensor_copy(CSN[:, :].rearrange("p (b t) -> p b t", b=DB), CS[:, :, PAST:PAST + DS]))
        v.tensor_scalar(NCP[:, :], CP[:, :], -1.0, None, ALU.mult).then_inc(c_ready, 1)
        moved(v, ("lfT",))
        for i in range(NT):
            for hf in range(2):
                moved(v, ("kf", i, hf))
        for s in range(2):
            ins = v.tensor_copy(KC[:, s, :, PAST:NKEYS], KF[:, :, 0:NS])
            if s == 0:
                steps.add(ins)
        ins.then_inc(kc_new, 1)
        for n in range(-1, len(ITEMS) + OLAG):
            if n >= OLAG:
                m = n - OLAG
                kind, x, t = ITEMS[m]
                if kind == "p":
                    out_of(("O", m), Y[:, x, QCOL[t]:QCOL[t] + QROWS[t]], ps(("O", m), 128, 0, QROWS[t]))
                else:
                    out_of(("O", m), Y[:, :, x * DS:(x + 1) * DS], ps(("O", m), 128, 0, NS).rearrange("p (h s) -> p h s", h=H))
            if 0 <= n < len(ITEMS):
                kind, x, t = ITEMS[n]
                name = ("S", n)
                computed(v, name)
                if kind == "p":
                    nq, nk = QROWS[t], KEYS[t]
                    masked, mask, whole = ps(name, nq, nk - nq, nk), MASKC[0:nq, 0:nq], ps(name, nq, 0, nk)
                else:
                    nq = NS
                    masked, mask, whole = ps(name, NS, PAST, NKEYS), MASKS[:, x, :], ps(name, NS, 0, NKEYS)
                steps.add(v.tensor_tensor(masked, masked, mask, ALU.add))
                steps.wait()
                v.tensor_reduce(out=NMX[0:nq, n % NP:n % NP + 1], in_=whole, axis=AXX, op=ALU.max, negate=True).then_inc(nmax_ready, 1)
            if 0 <= n - 1 < len(ITEMS):
                m = n - 1
                kind, x, t = ITEMS[m]
                nq = QROWS[t] if kind == "p" else NS
                moved(v, ("S", m))
                steps.add(v.reciprocal(RSUM[0:nq, m % NP:m % NP + 1], SUMS[0:nq, m % NP:m % NP + 1]))
                steps.wait()
                p = PP[0:nq, m % NP, NS:NS + KEYS[t]] if kind == "p" else PS[:, m % NP, :]
                v.tensor_scalar(p, p, RSUM[0:nq, m % NP:m % NP + 1], None, ALU.mult).then_inc(probs_ready, 1)
            if n + 1 in SAMPLE:
                x = SAMPLE.index(n + 1)
                for j in (1, 3):
                    out_of(("kc", x, j), KC[:, x % 2, 4:8, (j // 2) * 128:(j // 2) * 128 + 128],
                           ps(("kc", x, j), 128, 0, 512).rearrange("p (h k) -> p h k", h=4))
        mixer_residual(1, range(NT - 1))
        experts(1)

    ctx.close()


INS = ["x_prompt", "x_sample", "cache_k", "cache_v", "cache_logf", "state_h", "state_conv", "page_table", "meta_tokens",
       "rg_w_in", "rg_conv_w", "rg_conv_b", "rg_w_a", "rg_b_a", "rg_w_x", "rg_b_x", "rg_lambda", "rg_w_out", "fox_w_in",
       "fox_b_f", "fox_w_o", "peer_w_q", "peer_keys1", "peer_keys2", "peer_u", "peer_v", "ln_mix_g", "ln_mix_b",
       "ln_ffn_g", "ln_ffn_b"]
OUTS = [("y_prompt", (1, SEQ, D)), ("y_sample", (DB, DS, D)), ("state_h_prompt", (1, 1, D)),
        ("state_conv_prompt", (1, 1, CW - 1, D)), ("k_prompt", (1, 1, TP, H, HD)), ("v_prompt", (1, 1, TP, H, HD)),
        ("logf_prompt", (1, 1, TP, H)), ("state_h_sample", (1, DB, D)), ("state_conv_sample", (1, DB, CW - 1, D)),
        ("k_sample", (1, DB, DS, H, HD)), ("v_sample", (1, DB, DS, H, HD)), ("logf_sample", (1, DB, DS, H))]


def kernel(**inputs):
    import concourse.bacc as bacc
    from concourse.bass_utils import run_bass_kernel_spmd

    nc = bacc.Bacc("TRN2", target_bir_lowering=False, num_devices=1)
    arrays = {name: np.ascontiguousarray(inputs[name]) for name in INS}
    a = {name: nc.dram_tensor(name, x.shape, mybir.dt.from_np(x.dtype), kind="ExternalInput").ap() for name, x in arrays.items()}
    o = {name: nc.dram_tensor("out_" + name, shape, F32, kind="ExternalOutput").ap() for name, shape in OUTS}
    trunk(nc, a, o)
    r = run_bass_kernel_spmd(nc, [arrays], core_ids=[0])
    return tuple(r.results[0]["out_" + name] for name, _ in OUTS)
```
